# Optimizing a Trainium2 kernel written in Bass

```python
import jax, jax.numpy as jnp
from jax import lax
import numpy as np
import math

D_MODEL = 1024
BATCH = 1
SEQ = 256
DEPTH = 2

CHUNK = 64
D_MIX = D_MODEL
GM_WIDTH = D_MIX // 2
GM_HEADS = 8
GM_HEAD_DIM = GM_WIDTH // GM_HEADS
GM_BLOCK = 128
SB_WIDTH = D_MIX - GM_WIDTH
SB_HEADS = 8
SB_HEAD_DIM = SB_WIDTH // SB_HEADS
SB_BLOCK = 128
IN_COLS = 2 * GM_WIDTH + 3 * SB_WIDTH
PEER_HEADS = 8
PEER_QUERY_DIM = 256
PEER_HALF = PEER_QUERY_DIM // 2
N_KEYS = 128
N_EXPERTS = N_KEYS * N_KEYS
PEER_TOPK = 16
PEER_BLOCK = 128
ADA_SCALE = 0.5
EPS = 1e-6


def rmsnorm(x, g):
    xf = x.astype(jnp.float32)
    y = xf * lax.rsqrt(jnp.mean(xf * xf, axis=-1, keepdims=True) + EPS)
    return (y * g.astype(jnp.float32)).astype(x.dtype)

def spatial_gating(u, v, ws, bs, v_gain):
    B, S, _ = v.shape
    pos_chunk = jnp.arange(GM_BLOCK) // CHUNK
    mask = pos_chunk[None, :] <= pos_chunk[:, None]
    w = jnp.where(mask[None], ws, jnp.zeros_like(ws))
    vh = v.reshape(B, S // GM_BLOCK, GM_BLOCK, GM_HEADS, GM_HEAD_DIM)
    vh = rmsnorm(vh, v_gain.reshape(GM_HEADS, GM_HEAD_DIM))
    z = jnp.einsum('hts,bnshc->bnthc', w, vh) + bs.T[None, None, :, :, None]
    return u * z.reshape(B, S, GM_WIDTH)

def stick_breaking(q, k, v):
    B, S, H, dh = q.shape
    scale = 1.0 / np.sqrt(dh)
    outs = []
    for i in range(S // SB_BLOCK):
        t0, t1 = i * SB_BLOCK, (i + 1) * SB_BLOCK
        qb, kb, vb = q[:, t0:t1], k[:, :t1], v[:, :t1]
        z = jnp.einsum('bthd,bshd->bhts', qb, kb).astype(jnp.float32) * scale
        t_idx = t0 + jnp.arange(SB_BLOCK)[:, None]
        s_idx = jnp.arange(t1)[None, :]
        causal = s_idx < t_idx
        log_beta = jax.nn.log_sigmoid(z)
        log_keep = jnp.where(causal, jax.nn.log_sigmoid(-z), 0.0)
        later = lax.cumsum(log_keep, axis=3, reverse=True) - log_keep
        a = jnp.where(causal, jnp.exp(log_beta + later), 0.0)
        outs.append(jnp.einsum('bhts,bshd->bthd', a.astype(vb.dtype), vb))
    return jnp.concatenate(outs, axis=1)

def mixer(h, w_in, gm_ws, gm_bs, gm_vnorm, out_norm_a, out_norm_b, w_out):
    B, S, _ = h.shape
    proj = h @ w_in
    a_u, a_v, sq, sk, sv = jnp.split(
        proj, [GM_WIDTH, 2 * GM_WIDTH, 2 * GM_WIDTH + SB_WIDTH, 2 * GM_WIDTH + 2 * SB_WIDTH], axis=-1)
    y_a = spatial_gating(jax.nn.gelu(a_u), jax.nn.gelu(a_v), gm_ws, gm_bs, gm_vnorm)
    hs = (B, S, SB_HEADS, SB_HEAD_DIM)
    y_b = stick_breaking(sq.reshape(hs), sk.reshape(hs), sv.reshape(hs)).reshape(B, S, SB_WIDTH)
    y = jnp.concatenate([rmsnorm(y_a, out_norm_a), rmsnorm(y_b, out_norm_b)], axis=-1)
    return y @ w_out

def peer_ffn(h, wq, k1, k2, u_tab, v_tab):
    B, S, D = h.shape
    hb = h.reshape((B * S) // PEER_BLOCK, PEER_BLOCK, D)

    def block(xb):
        q = (xb @ wq).reshape(PEER_BLOCK, PEER_HEADS, 2, PEER_HALF)
        s1 = jnp.einsum('phd,kd->phk', q[:, :, 0], k1).astype(jnp.float32)
        s2 = jnp.einsum('phd,kd->phk', q[:, :, 1], k2).astype(jnp.float32)
        v1, i1 = lax.top_k(s1, PEER_TOPK)
        v2, i2 = lax.top_k(s2, PEER_TOPK)
        cand = (v1[..., :, None] + v2[..., None, :]).reshape(PEER_BLOCK, PEER_HEADS, PEER_TOPK * PEER_TOPK)
        cand_id = (i1[..., :, None] * N_KEYS + i2[..., None, :]).reshape(PEER_BLOCK, PEER_HEADS, PEER_TOPK * PEER_TOPK)
        top_s, top_pos = lax.top_k(cand, PEER_TOPK)
        eid = jnp.take_along_axis(cand_id, top_pos, axis=-1)
        g = jax.nn.softmax(top_s, axis=-1)
        ue = u_tab[eid]
        ve = v_tab[eid]
        act = jax.nn.gelu(jnp.einsum('pd,phkd->phk', xb, ue))
        return jnp.einsum('phk,phkd->pd', g.astype(xb.dtype) * act, ve)

    return lax.map(block, hb).reshape(B, S, D)

def first_inputs(seed: int = 0) -> dict:
    key = jax.random.key(seed)
    ks = jax.random.split(key, 20)
    f32 = jnp.float32
    nrm = lambda k, shape, s: jax.random.normal(k, shape, f32) * s
    L, D = DEPTH, D_MODEL
    return {
        "x": nrm(ks[0], (BATCH, SEQ, D), 1.0),
        "c": nrm(ks[1], (BATCH, D), 1.0),
        "ada_w": nrm(ks[2], (L, D, 6 * D), ADA_SCALE * D ** -0.5),
        "ada_b": nrm(ks[3], (L, 6 * D), 0.02),
        "norm_mix": 1.0 + nrm(ks[4], (L, D), 0.05),
        "norm_ffn": 1.0 + nrm(ks[5], (L, D), 0.05),
        "w_in": nrm(ks[6], (L, D, IN_COLS), D ** -0.5),
        "gm_ws": nrm(ks[7], (L, GM_HEADS, GM_BLOCK, GM_BLOCK), GM_BLOCK ** -0.5),
        "gm_bs": 1.0 + nrm(ks[8], (L, GM_HEADS, GM_BLOCK), 0.1),
        "gm_vnorm": 1.0 + nrm(ks[9], (L, GM_WIDTH), 0.05),
        "out_norm_a": 1.0 + nrm(ks[10], (L, GM_WIDTH), 0.05),
        "out_norm_b": 1.0 + nrm(ks[11], (L, SB_WIDTH), 0.05),
        "w_out": nrm(ks[12], (L, D_MIX, D), D_MIX ** -0.5),
        "peer_wq": nrm(ks[13], (L, D, PEER_HEADS * PEER_QUERY_DIM), D ** -0.5),
        "peer_k1": nrm(ks[14], (L, N_KEYS, PEER_HALF), PEER_HALF ** -0.5),
        "peer_k2": nrm(ks[15], (L, N_KEYS, PEER_HALF), PEER_HALF ** -0.5),
        "peer_u": nrm(ks[16], (L, N_EXPERTS, D), D ** -0.5),
        "peer_v": nrm(ks[17], (L, N_EXPERTS, D), PEER_HEADS ** -0.5),
        "final_norm": 1.0 + nrm(ks[18], (D,), 0.05),
    }

def first_block(x, c, ada_w, ada_b, norm_mix, norm_ffn, w_in, gm_ws, gm_bs, gm_vnorm,
              out_norm_a, out_norm_b, w_out, peer_wq, peer_k1, peer_k2, peer_u, peer_v,
              final_norm):
    c_act = jax.nn.silu(c)
    for l in range(DEPTH):
        mod = c_act @ ada_w[l] + ada_b[l]
        sh1, sc1, g1, sh2, sc2, g2 = jnp.split(mod[:, None, :], 6, axis=-1)
        h = rmsnorm(x, norm_mix[l]) * (1.0 + sc1) + sh1
        x = x + g1 * mixer(h, w_in[l], gm_ws[l], gm_bs[l], gm_vnorm[l],
                           out_norm_a[l], out_norm_b[l], w_out[l])
        h = rmsnorm(x, norm_ffn[l]) * (1.0 + sc2) + sh2
        x = x + g2 * peer_ffn(h, peer_wq[l], peer_k1[l], peer_k2[l], peer_u[l], peer_v[l])
    return rmsnorm(x, final_norm)


N_EVEN = (DEPTH + 1) // 2
N_ODD = DEPTH // 2

D_FF = 2816
FFN_RES = 0.5
NORM_EPS = 1e-6

POOL_WINDOWS = (2, 4, 8, 16)
N_POOL_GROUPS = 4
POOL_WIDTH = D_MODEL // 2
POOL_GROUP = POOL_WIDTH // N_POOL_GROUPS

CONV_WIDTH = D_MODEL // 2
CONV_KERNEL = 31

AB_IN = POOL_WIDTH + 2 * CONV_WIDTH
AB_OUT = POOL_WIDTH + CONV_WIDTH

N_HEADS = 16
HEAD_DIM = 64
ATTN_WIDTH = N_HEADS * HEAD_DIM
N_IDX_HEADS = 8
IDX_DIM = 64
TOPK_MAX = 256
Q_BLOCK = 128
C_SPLITS = (ATTN_WIDTH, ATTN_WIDTH, ATTN_WIDTH, N_IDX_HEADS * IDX_DIM, IDX_DIM, N_IDX_HEADS)
C_IN = sum(C_SPLITS)

REL_BUCKETS = 32
REL_MAX_DIST = 128


def _offsets(sizes):
    out, acc = [], 0
    for s in sizes[:-1]:
        acc += s
        out.append(acc)
    return out

def rms_norm(x, g):
    xf = x.astype(jnp.float32)
    y = xf * lax.rsqrt(jnp.mean(xf * xf, axis=-1, keepdims=True) + NORM_EPS)
    return (y * g.astype(jnp.float32)).astype(x.dtype)

def swiglu(h, w_gate, w_up, w_down):
    return (jax.nn.silu(h @ w_gate) * (h @ w_up)) @ w_down

def pool_mixer(u, pool_w, pool_scale):
    B, S, _ = u.shape
    uf = u.astype(jnp.float32).reshape(B, S, N_POOL_GROUPS, POOL_GROUP)
    c0 = jnp.concatenate([jnp.zeros((B, 1, N_POOL_GROUPS, POOL_GROUP), jnp.float32),
                          jnp.cumsum(uf, axis=1)], axis=1)
    t = jnp.arange(S, dtype=jnp.int32)[:, None]
    win = jnp.array(POOL_WINDOWS, dtype=jnp.int32)[None, :]
    lo = jnp.maximum(t + 1 - win, 0)
    g_idx = jnp.arange(N_POOL_GROUPS, dtype=jnp.int32)[None, :]
    lo_sum = c0[:, lo, g_idx, :]
    count = (t + 1 - lo).astype(jnp.float32)
    mean = (c0[:, 1:] - lo_sum) / count[None, :, :, None]
    y = jnp.einsum('bsgc,gcd->bsgd', mean - uf, pool_w.astype(jnp.float32))
    y = y * pool_scale.astype(jnp.float32).reshape(N_POOL_GROUPS, POOL_GROUP)
    return y.reshape(B, S, POOL_WIDTH).astype(u.dtype)

def conv_module(a, gate, conv_w, conv_b, ln_g, ln_b):
    z = a * jax.nn.sigmoid(gate)
    z = lax.conv_general_dilated(
        z, conv_w[:, None, :].astype(z.dtype), window_strides=(1,),
        padding=[(CONV_KERNEL - 1, 0)], dimension_numbers=('NWC', 'WIO', 'NWC'),
        feature_group_count=CONV_WIDTH) + conv_b
    zf = z.astype(jnp.float32)
    mu = jnp.mean(zf, axis=-1, keepdims=True)
    var = jnp.mean(jnp.square(zf - mu), axis=-1, keepdims=True)
    zf = (zf - mu) * lax.rsqrt(var + NORM_EPS) * ln_g.astype(jnp.float32) + ln_b.astype(jnp.float32)
    return jax.nn.silu(zf).astype(a.dtype)

def t5_bucket(dist):
    max_exact = REL_BUCKETS // 2
    d = jnp.maximum(dist, max_exact).astype(jnp.float32)
    large = max_exact + (jnp.log(d / max_exact) / math.log(REL_MAX_DIST / max_exact)
                         * (REL_BUCKETS - max_exact)).astype(jnp.int32)
    large = jnp.minimum(large, REL_BUCKETS - 1)
    return jnp.where(dist < max_exact, dist, large)

def dsa_attention(q, k, v, qi, ki, wi, rel_bias):
    S = q.shape[1]
    top_k = min(TOPK_MAX, S // 4)
    nb = S // Q_BLOCK
    pos = jnp.arange(S, dtype=jnp.int32)
    idx_scale = (N_IDX_HEADS * IDX_DIM) ** -0.5
    attn_scale = HEAD_DIM ** -0.5

    def one_seq(args):
        qb, kb, vb, qib, kib, wib = args
        kib32 = kib.astype(jnp.float32)

        def one_block(bargs):
            q_t, qi_t, wi_t, t = bargs
            rel = jax.nn.relu(jnp.einsum('thd,sd->ths', qi_t.astype(jnp.float32), kib32))
            score = jnp.einsum('ths,th->ts', rel, wi_t.astype(jnp.float32)) * idx_scale
            score = jnp.where(pos[None, :] <= t[:, None], score, -jnp.inf)
            _, sel = lax.top_k(score, top_k)
            k_sel = kb[sel]
            v_sel = vb[sel]
            logits = jnp.einsum('thd,tkhd->thk', q_t, k_sel).astype(jnp.float32) * attn_scale
            bias = rel_bias[t5_bucket(t[:, None] - sel)]
            logits = logits + jnp.transpose(bias, (0, 2, 1)).astype(jnp.float32)
            logits = jnp.where((sel <= t[:, None])[:, None, :], logits, -jnp.inf)
            p = jax.nn.softmax(logits, axis=-1).astype(v_sel.dtype)
            return jnp.einsum('thk,tkhd->thd', p, v_sel)

        blocks = (qb.reshape(nb, Q_BLOCK, N_HEADS, HEAD_DIM),
                  qib.reshape(nb, Q_BLOCK, N_IDX_HEADS, IDX_DIM),
                  wib.reshape(nb, Q_BLOCK, N_IDX_HEADS),
                  pos.reshape(nb, Q_BLOCK))
        out = lax.map(one_block, blocks)
        return out.reshape(S, ATTN_WIDTH)

    return lax.map(one_seq, (q, k, v, qi, ki, wi))

def second_inputs(seed: int = 0) -> dict:
    key = jax.random.key(seed)
    ks = jax.random.split(key, 24)
    f32 = jnp.float32

    def w(k, shape, fan_in):
        return jax.random.normal(k, shape, f32) * (fan_in ** -0.5)

    def gain(k, shape):
        return 1.0 + 0.02 * jax.random.normal(k, shape, f32)

    def small(k, shape):
        return 0.01 * jax.random.normal(k, shape, f32)

    return {
        'x': jax.random.normal(ks[0], (BATCH, SEQ, D_MODEL), f32),
        'ffn1_norm': gain(ks[1], (DEPTH, D_MODEL)),
        'ffn1_w_gate': w(ks[2], (DEPTH, D_MODEL, D_FF), D_MODEL),
        'ffn1_w_up': w(ks[3], (DEPTH, D_MODEL, D_FF), D_MODEL),
        'ffn1_w_down': w(ks[4], (DEPTH, D_FF, D_MODEL), D_FF),
        'mix_norm': gain(ks[5], (DEPTH, D_MODEL)),
        'ffn2_norm': gain(ks[6], (DEPTH, D_MODEL)),
        'ffn2_w_gate': w(ks[7], (DEPTH, D_MODEL, D_FF), D_MODEL),
        'ffn2_w_up': w(ks[8], (DEPTH, D_MODEL, D_FF), D_MODEL),
        'ffn2_w_down': w(ks[9], (DEPTH, D_FF, D_MODEL), D_FF),
        'ab_w_in': w(ks[10], (N_EVEN, D_MODEL, AB_IN), D_MODEL),
        'pool_w': w(ks[11], (N_EVEN, N_POOL_GROUPS, POOL_GROUP, POOL_GROUP), POOL_GROUP),
        'pool_scale': gain(ks[12], (N_EVEN, POOL_WIDTH)),
        'conv_w': w(ks[13], (N_EVEN, CONV_KERNEL, CONV_WIDTH), CONV_KERNEL),
        'conv_b': small(ks[14], (N_EVEN, CONV_WIDTH)),
        'conv_ln_g': gain(ks[15], (N_EVEN, CONV_WIDTH)),
        'conv_ln_b': small(ks[16], (N_EVEN, CONV_WIDTH)),
        'ab_w_out': w(ks[17], (N_EVEN, AB_OUT, D_MODEL), AB_OUT),
        'c_w_in': w(ks[18], (N_ODD, D_MODEL, C_IN), D_MODEL),
        'c_w_out': w(ks[19], (N_ODD, ATTN_WIDTH, D_MODEL), ATTN_WIDTH),
        'rel_bias': 0.1 * jax.random.normal(ks[20], (REL_BUCKETS, N_HEADS), f32),
        'final_norm': gain(ks[21], (D_MODEL,)),
    }

def second_block(x, ffn1_norm, ffn1_w_gate, ffn1_w_up, ffn1_w_down, mix_norm, ffn2_norm,
              ffn2_w_gate, ffn2_w_up, ffn2_w_down, ab_w_in, pool_w, pool_scale, conv_w,
              conv_b, conv_ln_g, conv_ln_b, ab_w_out, c_w_in, c_w_out, rel_bias, final_norm):
    B, S, _ = x.shape
    ab_cuts = _offsets((POOL_WIDTH, CONV_WIDTH, CONV_WIDTH))
    c_cuts = _offsets(C_SPLITS)
    for layer in range(DEPTH):
        h = rms_norm(x, ffn1_norm[layer])
        x = x + FFN_RES * swiglu(h, ffn1_w_gate[layer], ffn1_w_up[layer], ffn1_w_down[layer])
        h = rms_norm(x, mix_norm[layer])
        i = layer // 2
        if layer % 2 == 0:
            proj = h @ ab_w_in[i]
            u_pool, u_val, u_gate = jnp.split(proj, ab_cuts, axis=-1)
            y_pool = pool_mixer(u_pool, pool_w[i], pool_scale[i])
            y_conv = conv_module(u_val, u_gate, conv_w[i], conv_b[i], conv_ln_g[i], conv_ln_b[i])
            y = jnp.concatenate([y_pool, y_conv], axis=-1) @ ab_w_out[i]
        else:
            proj = h @ c_w_in[i]
            q, k, v, qi, ki, wi = jnp.split(proj, c_cuts, axis=-1)
            attn = dsa_attention(q.reshape(B, S, N_HEADS, HEAD_DIM),
                                 k.reshape(B, S, N_HEADS, HEAD_DIM),
                                 v.reshape(B, S, N_HEADS, HEAD_DIM),
                                 qi.reshape(B, S, N_IDX_HEADS, IDX_DIM), ki, wi, rel_bias)
            y = attn @ c_w_out[i]
        x = x + y
        h = rms_norm(x, ffn2_norm[layer])
        x = x + FFN_RES * swiglu(h, ffn2_w_gate[layer], ffn2_w_up[layer], ffn2_w_down[layer])
    return rms_norm(x, final_norm)


_first_inputs = second_inputs


def second_inputs(seed=0):
    import zlib

    import numpy as np

    out = dict(_first_inputs(seed))
    spreads = {}
    factors = {'ffn1_norm': 2.961,
     'ffn2_norm': 11.707,
     'pool_scale': 38.357,
     'conv_b': 3.816,
     'conv_ln_g': 47.054,
     'conv_ln_b': 90.109,
     'rel_bias': 18.649,
     'final_norm': 20.714}
    for name, (base, spread) in spreads.items():
        noise = np.random.default_rng([zlib.crc32(name.encode()), seed]).standard_normal(out[name].shape)
        drawn = base * np.exp(spread * noise) if base else spread * noise
        out[name] = __import__('jax').numpy.asarray(drawn.astype(out[name].dtype))
    for name, factor in factors.items():
        out[name] = (out[name] * factor).astype(out[name].dtype)
    return out


DEPTH_3 = 1

SSM_EXPAND = 2
SSM_D_INNER = SSM_EXPAND * D_MODEL
SSM_HEAD_DIM = 64
SSM_HEADS = SSM_D_INNER // SSM_HEAD_DIM
SSM_GROUPS = 8
SSM_HEADS_PER_GROUP = SSM_HEADS // SSM_GROUPS
SSM_STATE = 128
SSM_CONV = 4
SSM_CHUNK = 128
SSM_CONV_DIM = SSM_D_INNER + 2 * SSM_GROUPS * SSM_STATE
ATT_HEADS = 8
ATT_HEAD_DIM = 128
ATT_WIDTH = ATT_HEADS * ATT_HEAD_DIM
MOBA_BLOCK = 256
MOBA_TOPK = 3
N_BRANCHES = 2
IN_COLS_3 = SSM_D_INNER + SSM_CONV_DIM + SSM_HEADS + 3 * ATT_WIDTH + N_BRANCHES * D_MODEL
DEEPNORM_ALPHA = (2 * DEPTH_3) ** 0.25
DEEPNORM_BETA = (8 * DEPTH_3) ** -0.25
LN_EPS = 1e-5
RMS_EPS = 1e-5


def layer_norm(x, g, b):
    xf = x.astype(jnp.float32)
    mu = xf.mean(-1, keepdims=True)
    var = jnp.square(xf - mu).mean(-1, keepdims=True)
    y = (xf - mu) * lax.rsqrt(var + LN_EPS) * g.astype(jnp.float32) + b.astype(jnp.float32)
    return y.astype(x.dtype)

def swiglu_3(x, w_gate, w_up, w_down):
    return (jax.nn.silu(x @ w_gate) * (x @ w_up)) @ w_down

def causal_depthwise_conv(u, w, b):
    out = lax.conv_general_dilated(
        u, w[:, None, :].astype(u.dtype), window_strides=(1,), padding=[(SSM_CONV - 1, 0)],
        dimension_numbers=("NWC", "WIO", "NWC"), feature_group_count=u.shape[-1])
    return out + b

def ssd_chunked_scan(xh, dt, a, bm, cm):
    bsz, s, g, r, p = xh.shape
    n = bm.shape[-1]
    nc = s // SSM_CHUNK

    def to_chunks(t):
        return jnp.moveaxis(t.reshape(bsz, nc, SSM_CHUNK, *t.shape[2:]), 1, 0)

    xs = (to_chunks(xh * dt[..., None]), to_chunks(dt * a), to_chunks(bm), to_chunks(cm))
    causal = jnp.tril(jnp.ones((SSM_CHUNK, SSM_CHUNK), dtype=bool))

    def step(state, inp):
        xdt, da, b, c = inp
        acum = jnp.moveaxis(jnp.cumsum(da, axis=1), 1, -1)
        seg = acum[..., :, None] - acum[..., None, :]
        decay_ls = jnp.exp(jnp.where(causal, seg, -jnp.inf))
        cb = jnp.einsum("blgn,bsgn->bgls", c, b)
        y = jnp.einsum("bgrls,bsgrp->blgrp", decay_ls * cb[:, :, None], xdt)
        y = y + jnp.einsum("blgn,bgrpn,bgrl->blgrp", c, state, jnp.exp(acum))
        last = acum[..., -1:]
        new_state = state * jnp.exp(last)[..., None] + jnp.einsum(
            "bsgn,bgrs,bsgrp->bgrpn", b, jnp.exp(last - acum), xdt)
        return new_state, y

    state0 = jnp.zeros((bsz, g, r, p, n), jnp.float32)
    _, ys = lax.scan(step, state0, xs)
    return jnp.moveaxis(ys, 0, 1).reshape(bsz, s, g, r, p)

def mamba2_branch(z, xbc, dt_raw, conv_w, conv_b, dt_bias, a_log, d_skip, norm_w):
    bsz, s, _ = z.shape
    g, r, p, n = SSM_GROUPS, SSM_HEADS_PER_GROUP, SSM_HEAD_DIM, SSM_STATE
    xbc = jax.nn.silu(causal_depthwise_conv(xbc, conv_w, conv_b))
    xs, bm, cm = jnp.split(xbc, [SSM_D_INNER, SSM_D_INNER + g * n], axis=-1)
    xh = xs.reshape(bsz, s, g, r, p).astype(jnp.float32)
    bm = bm.reshape(bsz, s, g, n).astype(jnp.float32)
    cm = cm.reshape(bsz, s, g, n).astype(jnp.float32)
    dt = jax.nn.softplus(dt_raw.astype(jnp.float32) + dt_bias.astype(jnp.float32)).reshape(bsz, s, g, r)
    a = -jnp.exp(a_log.astype(jnp.float32)).reshape(g, r)
    y = ssd_chunked_scan(xh, dt, a, bm, cm)
    y = y + d_skip.astype(jnp.float32).reshape(g, r)[:, :, None] * xh
    y = y.reshape(bsz, s, SSM_D_INNER) * jax.nn.silu(z.astype(jnp.float32))
    yg = y.reshape(bsz, s, SSM_GROUPS, -1)
    yg = yg * lax.rsqrt(jnp.mean(jnp.square(yg), -1, keepdims=True) + RMS_EPS)
    return (yg.reshape(bsz, s, SSM_D_INNER) * norm_w.astype(jnp.float32)).astype(z.dtype)

def moba_attention(q, k, v):
    bsz, s, h, dh = q.shape
    nb = -(-s // MOBA_BLOCK)
    s_pad = nb * MOBA_BLOCK
    nqb = s // Q_BLOCK
    topk = min(MOBA_TOPK, nb)
    scale = 1.0 / math.sqrt(dh)
    q = q.transpose(0, 2, 1, 3)
    k = k.transpose(0, 2, 1, 3)
    v = v.transpose(0, 2, 1, 3)
    pad = ((0, 0), (0, 0), (0, s_pad - s), (0, 0))
    k_blocks = jnp.pad(k, pad).reshape(bsz, h, nb, MOBA_BLOCK, dh)
    v_blocks = jnp.pad(v, pad).reshape(bsz, h, nb, MOBA_BLOCK, dh)
    k_mean = k_blocks.astype(jnp.float32).mean(axis=3)
    gate = jnp.einsum("bhsd,bhjd->bhsj", q.astype(jnp.float32), k_mean)
    q_blk = jnp.arange(s) // MOBA_BLOCK
    fully_past = jnp.arange(nb)[None, :] < q_blk[:, None]
    gate = jnp.where(fully_past, gate, -jnp.inf)
    _, sel = lax.top_k(gate, topk)
    valid = sel < q_blk[:, None]

    def to_qblocks(t):
        c = t.shape[-1]
        return t.reshape(bsz, h, nqb, Q_BLOCK, c).transpose(0, 2, 1, 3, 4).reshape(bsz * nqb, h, Q_BLOCK, c)

    b_idx = jnp.repeat(jnp.arange(bsz), nqb)
    qb_idx = jnp.tile(jnp.arange(nqb), bsz)
    head_idx = jnp.arange(h)[:, None, None]
    offs_q = jnp.arange(Q_BLOCK)
    offs_k = jnp.arange(MOBA_BLOCK)

    def one_block(inp):
        b, qi, qb, sb, ok = inp
        kb = k_blocks[b]
        vb = v_blocks[b]
        own = (qi * Q_BLOCK) // MOBA_BLOCK
        k_own = lax.dynamic_index_in_dim(kb, own, axis=1, keepdims=False)
        v_own = lax.dynamic_index_in_dim(vb, own, axis=1, keepdims=False)
        k_sel = kb[head_idx, sb]
        v_sel = vb[head_idx, sb]
        s_own = jnp.einsum("hqd,hkd->hqk", qb, k_own).astype(jnp.float32) * scale
        causal = (own * MOBA_BLOCK + offs_k)[None, :] <= (qi * Q_BLOCK + offs_q)[:, None]
        s_own = jnp.where(causal, s_own, -jnp.inf)
        s_sel = jnp.einsum("hqd,hqjkd->hqjk", qb, k_sel).astype(jnp.float32) * scale
        s_sel = jnp.where(ok[..., None], s_sel, -jnp.inf)
        scores = jnp.concatenate([s_own, s_sel.reshape(h, Q_BLOCK, topk * MOBA_BLOCK)], axis=-1)
        probs = jax.nn.softmax(scores, axis=-1).astype(v.dtype)
        p_own = probs[..., :MOBA_BLOCK]
        p_sel = probs[..., MOBA_BLOCK:].reshape(h, Q_BLOCK, topk, MOBA_BLOCK)
        return (jnp.einsum("hqk,hkd->hqd", p_own, v_own)
                + jnp.einsum("hqjk,hqjkd->hqd", p_sel, v_sel))

    out = lax.map(one_block, (b_idx, qb_idx, to_qblocks(q), to_qblocks(sel), to_qblocks(valid)))
    return out.reshape(bsz, nqb, h, Q_BLOCK, dh).transpose(0, 1, 3, 2, 4).reshape(bsz, s, h * dh)

def hybrid_mixer(h, w_in, conv_w, conv_b, dt_bias, a_log, d_skip, ssm_norm_w,
                 w_ssm_out, w_att_out, b_gate, w_o):
    bsz, s, _ = h.shape
    proj = h @ w_in
    splits = np.cumsum([SSM_D_INNER, SSM_CONV_DIM, SSM_HEADS, ATT_WIDTH, ATT_WIDTH, ATT_WIDTH]).tolist()
    z, xbc, dt_raw, q, k, v, g_raw = jnp.split(proj, splits, axis=-1)
    y_ssm = mamba2_branch(z, xbc, dt_raw, conv_w, conv_b, dt_bias, a_log, d_skip, ssm_norm_w) @ w_ssm_out
    shp = (bsz, s, ATT_HEADS, ATT_HEAD_DIM)
    y_att = moba_attention(q.reshape(shp), k.reshape(shp), v.reshape(shp)) @ w_att_out
    gates = jax.nn.sigmoid((g_raw + b_gate).astype(jnp.float32)).astype(h.dtype)
    g_ssm, g_att = jnp.split(gates, N_BRANCHES, axis=-1)
    return (g_ssm * y_ssm + g_att * y_att) @ w_o

def third_inputs(seed: int = 0) -> dict:
    key = jax.random.key(seed)
    ks = jax.random.split(key, 32)
    f32 = jnp.float32

    def nrm(k, shape, scale):
        return jax.random.normal(k, shape, f32) * scale

    def gain(k, n):
        return 1.0 + 0.01 * jax.random.normal(k, (n,), f32)

    dt0 = jnp.exp(jax.random.uniform(ks[10], (SSM_HEADS,), f32)
                  * (math.log(0.1) - math.log(0.001)) + math.log(0.001))
    dt0 = jnp.maximum(dt0, 1e-4)
    return {
        "x": jax.random.normal(ks[0], (BATCH, SEQ, D_MODEL), f32),
        "ffn1_w_gate": nrm(ks[1], (D_MODEL, D_FF), D_MODEL ** -0.5),
        "ffn1_w_up": nrm(ks[2], (D_MODEL, D_FF), D_MODEL ** -0.5),
        "ffn1_w_down": nrm(ks[3], (D_FF, D_MODEL), DEEPNORM_BETA * D_FF ** -0.5),
        "ln1_g": gain(ks[4], D_MODEL),
        "ln1_b": nrm(ks[5], (D_MODEL,), 0.01),
        "w_in": nrm(ks[6], (D_MODEL, IN_COLS_3), D_MODEL ** -0.5),
        "conv_w": nrm(ks[7], (SSM_CONV, SSM_CONV_DIM), SSM_CONV ** -0.5),
        "conv_b": nrm(ks[8], (SSM_CONV_DIM,), 0.01),
        "dt_bias": dt0 + jnp.log(-jnp.expm1(-dt0)),
        "a_log": jnp.log(jax.random.uniform(ks[11], (SSM_HEADS,), f32, 1.0, 16.0)),
        "d_skip": gain(ks[12], SSM_HEADS),
        "ssm_norm_w": gain(ks[13], SSM_D_INNER),
        "w_ssm_out": nrm(ks[14], (SSM_D_INNER, D_MODEL), SSM_D_INNER ** -0.5),
        "w_att_out": nrm(ks[15], (ATT_WIDTH, D_MODEL), ATT_WIDTH ** -0.5),
        "b_gate": nrm(ks[16], (N_BRANCHES * D_MODEL,), 0.01),
        "w_o": nrm(ks[17], (D_MODEL, D_MODEL), DEEPNORM_BETA * D_MODEL ** -0.5),
        "ln2_g": gain(ks[18], D_MODEL),
        "ln2_b": nrm(ks[19], (D_MODEL,), 0.01),
        "ffn2_w_gate": nrm(ks[20], (D_MODEL, D_FF), D_MODEL ** -0.5),
        "ffn2_w_up": nrm(ks[21], (D_MODEL, D_FF), D_MODEL ** -0.5),
        "ffn2_w_down": nrm(ks[22], (D_FF, D_MODEL), DEEPNORM_BETA * D_FF ** -0.5),
        "ln3_g": gain(ks[23], D_MODEL),
        "ln3_b": nrm(ks[24], (D_MODEL,), 0.01),
    }

def third_block(x, ffn1_w_gate, ffn1_w_up, ffn1_w_down, ln1_g, ln1_b, w_in, conv_w, conv_b,
              dt_bias, a_log, d_skip, ssm_norm_w, w_ssm_out, w_att_out, b_gate, w_o,
              ln2_g, ln2_b, ffn2_w_gate, ffn2_w_up, ffn2_w_down, ln3_g, ln3_b):
    h = x
    for _ in range(DEPTH_3):
        h = layer_norm(DEEPNORM_ALPHA * h + 0.5 * swiglu_3(h, ffn1_w_gate, ffn1_w_up, ffn1_w_down), ln1_g, ln1_b)
        h = layer_norm(DEEPNORM_ALPHA * h + hybrid_mixer(h, w_in, conv_w, conv_b, dt_bias, a_log, d_skip,
                                                         ssm_norm_w, w_ssm_out, w_att_out, b_gate, w_o),
                       ln2_g, ln2_b)
        h = layer_norm(DEEPNORM_ALPHA * h + 0.5 * swiglu_3(h, ffn2_w_gate, ffn2_w_up, ffn2_w_down), ln3_g, ln3_b)
    return h


_first_inputs_3 = third_inputs


def third_inputs(seed=0):
    import zlib

    import numpy as np

    out = dict(_first_inputs_3(seed))
    spreads = {}
    factors = {'ln1_g': 5.396,
     'ln1_b': 4.802,
     'conv_b': 50.423,
     'd_skip': 64.0,
     'ssm_norm_w': 64.0,
     'b_gate': 55.668,
     'ln2_g': 27.208,
     'ln2_b': 26.495,
     'ln3_g': 33.768,
     'ln3_b': 33.048}
    for name, (base, spread) in spreads.items():
        noise = np.random.default_rng([zlib.crc32(name.encode()), seed]).standard_normal(out[name].shape)
        drawn = base * np.exp(spread * noise) if base else spread * noise
        out[name] = __import__('jax').numpy.asarray(drawn.astype(out[name].dtype))
    for name, factor in factors.items():
        out[name] = (out[name] * factor).astype(out[name].dtype)
    return out


_narrow_inputs = third_inputs


def third_inputs(seed=0):

    out = dict(_narrow_inputs(seed))
    wider = {'d_skip': 12.0,
     'ssm_norm_w': 4.73,
     'ln2_g': 4.66,
     'ln2_b': 4.67,
     'ln3_g': 6.53,
     'ln3_b': 6.55}
    for name, times in wider.items():
        mean = out[name].mean()
        out[name] = (mean + times * (out[name] - mean)).astype(out[name].dtype)
    return out


def setup_inputs(seed=0):
    out = dict(first_inputs(seed))
    for name, value in second_inputs(seed + 1).items():
        if name != "x":
            out[name + "_2"] = value
    for name, value in third_inputs(seed + 2).items():
        if name != "x":
            out[name + "_3"] = value
    return out


def reference(
    x, c, ada_w, ada_b, norm_mix, norm_ffn, w_in, gm_ws, gm_bs, gm_vnorm, out_norm_a,
    out_norm_b, w_out, peer_wq, peer_k1, peer_k2, peer_u, peer_v, final_norm, ffn1_norm_2,
    ffn1_w_gate_2, ffn1_w_up_2, ffn1_w_down_2, mix_norm_2, ffn2_norm_2, ffn2_w_gate_2,
    ffn2_w_up_2, ffn2_w_down_2, ab_w_in_2, pool_w_2, pool_scale_2, conv_w_2, conv_b_2,
    conv_ln_g_2, conv_ln_b_2, ab_w_out_2, c_w_in_2, c_w_out_2, rel_bias_2, final_norm_2,
    ffn1_w_gate_3, ffn1_w_up_3, ffn1_w_down_3, ln1_g_3, ln1_b_3, w_in_3, conv_w_3, conv_b_3,
    dt_bias_3, a_log_3, d_skip_3, ssm_norm_w_3, w_ssm_out_3, w_att_out_3, b_gate_3, w_o_3,
    ln2_g_3, ln2_b_3, ffn2_w_gate_3, ffn2_w_up_3, ffn2_w_down_3, ln3_g_3, ln3_b_3,
):
    x = first_block(
        x, c, ada_w, ada_b, norm_mix, norm_ffn, w_in, gm_ws, gm_bs, gm_vnorm, out_norm_a,
        out_norm_b, w_out, peer_wq, peer_k1, peer_k2, peer_u, peer_v, final_norm,
    )
    x = second_block(
        x, ffn1_norm_2, ffn1_w_gate_2, ffn1_w_up_2, ffn1_w_down_2, mix_norm_2, ffn2_norm_2,
        ffn2_w_gate_2, ffn2_w_up_2, ffn2_w_down_2, ab_w_in_2, pool_w_2, pool_scale_2, conv_w_2,
        conv_b_2, conv_ln_g_2, conv_ln_b_2, ab_w_out_2, c_w_in_2, c_w_out_2, rel_bias_2,
        final_norm_2,
    )
    return third_block(
        x, ffn1_w_gate_3, ffn1_w_up_3, ffn1_w_down_3, ln1_g_3, ln1_b_3, w_in_3, conv_w_3,
        conv_b_3, dt_bias_3, a_log_3, d_skip_3, ssm_norm_w_3, w_ssm_out_3, w_att_out_3,
        b_gate_3, w_o_3, ln2_g_3, ln2_b_3, ffn2_w_gate_3, ffn2_w_up_3, ffn2_w_down_3, ln3_g_3,
        ln3_b_3,
    )


_drawn_inputs = setup_inputs


def setup_inputs(seed=0):
    import zlib

    import numpy as np

    out = dict(_drawn_inputs(seed))
    spreads = {}
    factors = {'d_skip_3': 2.758}
    for name, (base, spread) in spreads.items():
        noise = np.random.default_rng([zlib.crc32(name.encode()), seed]).standard_normal(out[name].shape)
        drawn = base * np.exp(spread * noise) if base else spread * noise
        out[name] = __import__('jax').numpy.asarray(drawn.astype(out[name].dtype))
    for name, factor in factors.items():
        out[name] = (out[name] * factor).astype(out[name].dtype)
    return out
```

```python
from collections import namedtuple
from contextlib import ExitStack, contextmanager
import math

import numpy as np
import concourse.bass as bass
from concourse import mybir

ALU = mybir.AluOpType
ACT = mybir.ActivationFunctionType
AX = mybir.AxisListType
F32 = mybir.dt.float32
I32 = mybir.dt.int32
U32 = mybir.dt.uint32

P = 128
D = 1024
KT = D // P
SEQ = 256
NB = SEQ // P
HALF = D // 2
RING = 6
SLOT = 2048
BANK = 512
DFF = 2816
FF_STEPS = DFF // 256
EPS = 1e-6
LN_EPS = 1e-5
NEG = -1e30
TAKEN = -3e38
HEADS = 8
TOPK = 16
GRING = 16
GHALF = GRING // 2
DSA_TOPK = 64
KERN = 31
ALPHA = 2 ** 0.25
SSM_D = 2048
SSM_G = 8
SSM_R = 4
SSM_H = SSM_G * SSM_R
SSM_P = 64


def shape_constants():
    i = np.arange(P)
    eye = np.eye(P)
    before = i[:, None] < i[None, :]
    upto = i[:, None] <= i[None, :]
    strict3 = np.concatenate([before, np.ones((P, P)), before], 1)
    count = np.minimum(np.arange(SEQ)[None] + 1, np.array([2, 4, 8, 16])[:, None])
    dist = 255 - np.arange(384)
    d = np.maximum(dist, 16).astype(np.float32)
    big = 16 + (np.log(d / np.float32(16)) / np.float32(math.log(8)) * np.float32(16)).astype(np.int32)
    bucket = np.where(dist < 16, dist, np.minimum(big, 31))
    onehot = np.zeros((P, 384))
    for c in range(256):
        onehot[bucket[c], c] = 1.0
    causal = np.where(i[None, :] > i[:, None], NEG, 0.0)
    parts = {
        "ident": eye,
        "anti": eye[::-1],
        "upto": upto,
        "after": i[:, None] > i[None, :],
        "from_": i[:, None] >= i[None, :],
        "ones": np.ones((P, P)),
        "strict3": strict3,
        "strict3_add": np.where(strict3 > 0, 0.0, NEG),
        "causal3_add": np.concatenate([causal, np.zeros((P, P)), causal], 1),
        "iota16": np.tile(np.arange(16), (P, 1)),
        "neghalf": np.full((P, 32), -0.5),
        "invcount": np.tile((1.0 / count[:, :16]).reshape(1, -1), (P, 1)),
        "onehot": onehot,
    }
    at, where = 0, {}
    for name, a in parts.items():
        where[name] = (at, at + a.shape[1])
        at += a.shape[1]
    return np.concatenate([np.asarray(a, np.float32) for a in parts.values()], 1), where


PARAM_GROUPS = [
    [("norm_mix", 16), ("norm_ffn", 16)],
    [("conv_w_3", 128)],
    [("conv_w_2", KERN * 4)],
    [("gm_bs", 16), ("out_norm_a", 8), ("out_norm_b", 8), ("ffn1_norm_2", 16), ("mix_norm_2", 16),
     ("ffn2_norm_2", 16), ("conv_b_2", 4), ("conv_ln_g_2", 4), ("conv_ln_b_2", 4), ("pool_scale_2", 4)],
    [("ssm_norm_w_3", 16), ("conv_b_3", 32), ("c", 8)],
]


class Program:
    def __init__(self, nc, a):
        self.nc, self.a = nc, a
        self.ctx = ExitStack()
        self.n_stage = 0

    def sb(self, name, shape, dt=F32, ctx=None):
        if ctx is not None:
            name = f"{name}_{self.n_stage}"
        return (ctx or self.ctx).enter_context(self.nc.sbuf_tensor(name, shape, dt))

    def place(self):
        nc = self.nc
        consts, where = shape_constants()
        self.X = self.sb("X", [P, NB, D])
        self.hT = self.sb("hT", [P, KT, SEQ])
        self.ring = self.sb("ring", [P, RING, SLOT])
        self.cst = self.sb("cst", [P, consts.shape[1]])

        def table(name):
            lo, hi = where[name]
            return self.cst[:, lo:hi]
        self.ident = table("ident")
        self.anti = table("anti")
        self.upto = table("upto")
        self.after = table("after")
        self.from_ = table("from_")
        self.ones = table("ones")
        self.strict3 = table("strict3")
        self.strict3_add = table("strict3_add")
        self.causal3_add = table("causal3_add")
        self.iota16 = table("iota16")
        self.neghalf = table("neghalf")
        self.invcount = table("invcount")
        self.onehot = table("onehot")
        self.prm = self.sb("prm", [P, len(PARAM_GROUPS), P])
        self.ms = self.sb("ms", [P, NB])
        self.rstd = self.sb("rstd", [P, NB])
        self.mu = self.sb("mu", [P, NB])
        self.negmu = self.sb("negmu", [P, NB])
        self.xn = self.sb("xn", [P, NB, D])
        self.mod = self.sb("mod", [P, 48])
        self.modA = self.sb("modA", [P, 2, KT])
        self.gate = self.sb("gate", [P, 2, D])
        self.PS = self.ctx.enter_context(nc.psum_tensor("PS", [P, 8, BANK], F32))
        self.banks = [[nc.alloc_semaphore(f"stage{b}_{i}") for i in range(20)] for b in range(2)]
        self.w_landed = [nc.alloc_semaphore(f"w_landed{i}") for i in range(RING)]
        self.w_used = nc.alloc_semaphore("w_used")
        self.g_landed = [nc.alloc_semaphore(f"g_landed{i}") for i in range(GRING)]
        self.g_used = nc.alloc_semaphore("g_used")
        self.g_index = nc.alloc_semaphore("g_index")
        self.g_turn = nc.alloc_semaphore("g_turn")

    def col(self, name, j=0):
        for g, rows in enumerate(PARAM_GROUPS):
            at = 0
            for n, count in rows:
                if n == name:
                    return self.prm[:, g, at + j:at + count]
                at += count
        raise KeyError(name)

    def plan(self):
        a = self.a

        def lin(w, jobs):
            out = []
            for cols in jobs:
                cols = [cols] if isinstance(cols, tuple) else cols
                width = sum(n for _, n in cols)
                for g in range(w.shape[0] // 512):
                    rows = w[g * 512:(g + 1) * 512, :].rearrange("(k p) n -> p k n", p=P)
                    at, pieces = 0, []
                    for c0, n in cols:
                        pieces.append((at, n, width, rows[:, :, c0:c0 + n]))
                        at += n
                    out.append(("lin", pieces))
            return out

        def full(n):
            return [(c, 512) for c in range(0, n, 512)]

        def ffn(wg, wu, wd):
            def up(i):
                return [("up", w[:, i * 256:(i + 1) * 256].rearrange("(k p) n -> p k n", p=P)) for w in (wg, wu)]

            def down(i):
                return [("down", wd[i * 256:(i + 1) * 256, :].rearrange("(k p) n -> p k n", p=P))]
            out = up(0)
            for i in range(FF_STEPS):
                out += (up(i + 1) if i + 1 < FF_STEPS else []) + down(i)
            return out

        stages = []
        for l in range(2):
            stages += [(f"ada{l}", lin(a["ada_w"][l], full(6 * D))),
                       (f"mix_in{l}", lin(a["w_in"][l], full(2560))),
                       (f"mix_out{l}", lin(a["w_out"][l], full(D))),
                       (f"peer_q{l}", lin(a["peer_wq"][l], full(2048)))]
        for l in range(2):
            stages.append((f"ffn1_{l}", ffn(a["ffn1_w_gate_2"][l], a["ffn1_w_up_2"][l], a["ffn1_w_down_2"][l])))
            if l == 0:
                stages += [("ab_in", lin(a["ab_w_in_2"][0], full(1536))),
                           ("ab_out", lin(a["ab_w_out_2"][0], full(D)))]
            else:
                stages += [("c_in", lin(a["c_w_in_2"][0], full(3584) + [[(3584, 64), (3584, 64), (3648, 8)]])),
                           ("c_out", lin(a["c_w_out_2"][0], full(D)))]
            stages.append((f"ffn2_{l}", ffn(a["ffn2_w_gate_2"][l], a["ffn2_w_up_2"][l], a["ffn2_w_down_2"][l])))
        w3 = a["w_in_3"]
        stages += [("ffn1_3", ffn(a["ffn1_w_gate_3"], a["ffn1_w_up_3"], a["ffn1_w_down_3"])),
                   ("ssm_in", lin(w3, [(2048 + c, 512) for c in range(0, 4096, 512)] + [(6144, 32)])),
                   ("ssm_z", lin(w3, full(2048))),
                   ("ssm_out", lin(a["w_ssm_out_3"], full(D))),
                   ("att_in", lin(w3, [(6176 + c, 512) for c in range(0, 3072, 512)])),
                   ("att_out", lin(a["w_att_out_3"], full(D)) + lin(w3, [(9248 + c, 512) for c in range(0, 2048, 512)])),
                   ("mix3_out", lin(a["w_o_3"], full(D))),
                   ("ffn2_3", ffn(a["ffn2_w_gate_3"], a["ffn2_w_up_3"], a["ffn2_w_down_3"]))]
        self.chunks, self.chunk_end = [], {}
        for name, chunks in stages:
            self.chunks += chunks
            self.chunk_end[name] = len(self.chunks)
        self.landed_at, total = [], [0] * RING
        for n, chunk in enumerate(self.chunks):
            total[n % RING] += 16 * (len(chunk[1]) if chunk[0] == "lin" else 1)
            self.landed_at.append(total[n % RING])
        self.issued = self.taken = 0

    def load_weights(self, sp, name):
        end = self.chunk_end.get(name, self.taken)
        for n in range(self.issued, min(len(self.chunks), end + RING)):
            if n >= RING:
                sp.wait_ge(self.w_used, n - RING + 1)
            slot = self.ring[:, n % RING, :]
            kind, what = self.chunks[n]
            if kind == "lin":
                for at, w, width, src in what:
                    dst = slot[:, 0:4 * width].rearrange("p (k n) -> p k n", k=4)[:, :, at:at + w]
                    sp.dma_start(dst, src).then_inc(self.w_landed[n % RING], 16)
            else:
                dst = slot.rearrange("p (k n) -> p k n", k=8 if kind == "up" else 2)
                sp.dma_start(dst, what).then_inc(self.w_landed[n % RING], 16)
        self.issued = max(self.issued, min(len(self.chunks), end + RING))

    def take(self, pe):
        n = self.taken
        self.taken += 1
        pe.wait_ge(self.w_landed[n % RING], self.landed_at[n])
        return self.ring[:, n % RING, :]

    @contextmanager
    def stage(self, names, weights=None):
        nc = self.nc
        mine, other = self.banks[self.n_stage % 2], self.banks[(self.n_stage + 1) % 2]
        self.n_stage += 1
        self.base = self.taken
        names = names.split()
        assert len(names) <= len(mine)
        with nc.Block(no_gpsimd_drain=True) as block:
            @block.gpsimd
            def _(pool):
                nc.gpsimd.sem_clear(range(other[0].num, other[-1].num + 1))

            @block.sync
            def _(sp):
                if weights:
                    self.load_weights(sp, weights)

            yield block, namedtuple("StageSemaphores", names)(*mine[:len(names)])

    def norm_vector(self, ve, S, scale, shift, tap=None):
        nc = self.nc
        for b in range(NB):
            nc.vector.tensor_tensor_reduce(self.xn[:, b, :], self.X[:, b, :], self.X[:, b, :], 1.0 / D, EPS,
                                           ALU.mult, ALU.add, self.ms[:, b:b + 1])
        nc.vector.drain().then_inc(S.n_ms, 1)
        ve.wait_ge(S.n_rstd, 1)
        for b in range(NB):
            nc.vector.tensor_scalar(self.xn[:, b, :], self.X[:, b, :], self.rstd[:, b:b + 1], None,
                                    ALU.mult).then_inc(S.n_xn, 1)
        self.evacuate_tiles(ve, nc.vector, S, 1, scale, shift)

    def norm_gpsimd(self, pool, S):
        pool.wait_ge(S.n_ms, 1)
        self.nc.gpsimd.tensor_tensor(self.rstd[:], self.ms[:], self.neghalf[:, 0:NB], ALU.pow).then_inc(S.n_rstd, 1)

    def norm_tensor(self, pe, S, src=None):
        nc = self.nc
        for b in range(NB):
            pe.wait_ge(S.n_xn, b + 1)
            for g in range(2):
                for j in range(4):
                    k = 4 * g + j
                    ins = nc.tensor.transpose(self.PS[:, 4 + 2 * b + g, j * P:(j + 1) * P],
                                              (src or self.xn)[:, b, k * P:(k + 1) * P], self.ident)
                ins.then_inc(S.n_tr, 1)

    def evacuate_tiles(self, eng, ops, S, odd, scale, shift):
        for b in range(NB):
            for g in (odd,):
                eng.wait_ge(S.n_tr, 2 * b + g + 1)
                for j in range(4):
                    k = 4 * g + j
                    out = self.hT[:, k, b * P:(b + 1) * P]
                    src = self.PS[:, 4 + 2 * b + g, j * P:(j + 1) * P]
                    bias = shift[:, k:k + 1] if shift is not None else 0.0
                    if odd:
                        if shift is None:
                            ins = ops.tensor_scalar(out, src, scale[:, k:k + 1], None, ALU.mult)
                        else:
                            ins = ops.tensor_scalar(out, src, scale[:, k:k + 1], bias, ALU.mult, ALU.add)
                    elif shift is None:
                        ins = ops.activation(out, src, ACT.Copy, scale=scale[:, k:k + 1])
                    else:
                        ins = ops.activation(out, src, ACT.Identity, bias=bias, scale=scale[:, k:k + 1])
                ins.then_inc(S.n_hT, 1)

    def norm_scalar(self, act, S, scale, shift):
        self.evacuate_tiles(act, self.nc.scalar, S, 0, scale, shift)

    N_HT = 4

    def project(self, pe, S, jobs, actT, kts, first=0):
        nc = self.nc
        for j, (kind, w) in enumerate(jobs, first):
            pair = 2 * (j % 2)
            if j >= 2:
                pe.wait_ge((S.p_free0, S.p_free1)[j % 2], 2 * (j // 2))
            for g in range(kts // 4):
                slot = self.take(pe)[:, 0:4 * w].rearrange("p (k n) -> p k n", k=4)
                for kk in range(4):
                    k = 4 * g + kk
                    if kind == "T":
                        for b in range(NB):
                            ins = nc.tensor.matmul(self.PS[:, pair + b, 0:w], actT[:, k, b * P:(b + 1) * P],
                                                   slot[:, kk, :], start=(k == 0), stop=(k == kts - 1),
                                                   skip_group_check=True)
                    else:
                        for t in range(w // P):
                            ins = nc.tensor.matmul(
                                self.PS[:, pair + t // 2, (t % 2) * SEQ:(t % 2 + 1) * SEQ],
                                slot[:, kk, t * P:(t + 1) * P], actT[:, k, :],
                                start=(k == 0 and t % 2 == 0), stop=(k == kts - 1), skip_group_check=True)
                ins.then_inc(self.w_used, 1)

    def leave(self, eng, j, per=2):
        eng.wait_ge(self.w_used, self.base + (j + 1) * per)

    def bank(self, j, e):
        return self.PS[:, 2 * (j % 2) + e, :]

    def freed(self, S, j):
        return (S.p_free0, S.p_free1)[j % 2]

    def load_constants(self):
        nc, a = self.nc, self.a
        with ExitStack() as ctx, self.stage("rows turned turned_out") as (block, S):
            rows = self.sb("param_rows", [P, len(PARAM_GROUPS), P], ctx=ctx)
            loads = nc.alloc_semaphore("const_landed")
            dmas = [(self.cst[:], a["shape_consts"])] + [
                (self.X[:], a["x"][0].rearrange("(b p) d -> p b d", p=P))]
            for g, group in enumerate(PARAM_GROUPS):
                at = 0
                for name, count in group:
                    src = a[name]
                    flat = src.rearrange(" ".join("abc"[:len(src.shape)]) + " -> (" + " ".join("abc"[:len(src.shape)]) + ")")
                    dmas.append((rows[at:at + count, g, :], flat.rearrange("(r p) -> r p", p=P)))
                    at += count

            @block.vector
            def _(ve):
                nc.vector.memset(rows[:], 0.0).then_inc(S.rows, 1)
                ve.wait_ge(S.turned, 1)
                for g in range(len(PARAM_GROUPS)):
                    ins = nc.vector.tensor_copy(self.prm[:, g, :], self.PS[:, g, 0:P])
                ins.then_inc(S.turned_out, 1)

            @block.scalar
            def _(act):
                act.wait_ge(S.rows, 1)
                for dst, src in dmas:
                    act.dma_start(dst, src).then_inc(loads, 16)
                act.wait_ge(loads, 16 * len(dmas))

            @block.tensor
            def _(pe):
                pe.wait_ge(loads, 16 * len(dmas))
                for g in range(len(PARAM_GROUPS)):
                    ins = nc.tensor.transpose(self.PS[:, g, 0:P], rows[:, g, :], self.ident)
                ins.then_inc(S.turned, 1)

    def ada(self, l):
        nc, a = self.nc, self.a
        with ExitStack() as ctx, self.stage("silu row spread", f"ada{l}") as (block, S):
            cact = self.sb("cact", [P, KT], ctx=ctx)
            row = self.sb("mod_row", [1, 6 * D], ctx=ctx)
            brow = self.sb("ada_b_row", [1, 6 * D], ctx=ctx)
            landed = nc.alloc_semaphore(f"ada_b_landed{l}")
            n_jobs = 6 * D // BANK

            @block.scalar
            def _(act):
                act.dma_start(brow[:], a["ada_b"][l:l + 1, :]).then_inc(landed, 16)
                nc.scalar.activation(cact[:], self.col("c"), ACT.Silu).then_inc(S.silu, 1)

            @block.tensor
            def _(pe):
                pe.wait_ge(S.silu, 1)
                for j in range(n_jobs):
                    if j >= 3:
                        pe.wait_ge(S.row, j - 2)
                    for g in range(2):
                        slot = self.take(pe).rearrange("p (k n) -> p k n", k=4)
                        for kk in range(4):
                            k = 4 * g + kk
                            ins = nc.tensor.matmul(self.PS[0:1, j % 3, :], cact[:, k:k + 1], slot[:, kk, :],
                                                   start=(k == 0), stop=(k == KT - 1))
                        ins.then_inc(self.w_used, 1)
                pe.wait_ge(S.row, n_jobs)
                for n in range(6 * KT):
                    nc.tensor.matmul(self.PS[:, 3, n:n + 1], row[:, n * P:(n + 1) * P], self.ones[0:1, 0:1],
                                     start=(n == 0), stop=True, skip_group_check=True)
                for i in range(4):
                    c = (2 if i < 2 else 5) * D + (i % 2) * BANK
                    ins = nc.tensor.matmul(self.PS[:, 4 + i, :], self.ones[0:1, :], row[:, c:c + BANK],
                                           start=True, stop=True)
                ins.then_inc(S.spread, 1)

            @block.vector
            def _(ve):
                ve.wait_ge(landed, 16)
                for j in range(n_jobs):
                    c = slice(j * BANK, (j + 1) * BANK)
                    self.leave(ve, j)
                    nc.vector.tensor_tensor(row[:, c], self.PS[0:1, j % 3, :], brow[:, c], ALU.add)
                    nc.vector.drain().then_inc(S.row, 1)
                ve.wait_ge(S.spread, 1)
                nc.vector.tensor_copy(self.mod[:], self.PS[:, 3, 0:48])
                nc.vector.tensor_copy(self.gate[:].rearrange("p i (h n) -> p (i h) n", n=BANK), self.PS[:, 4:8, :])
                nc.vector.drain()
                for i, name in enumerate(("norm_mix", "norm_ffn")):
                    gain = self.col(name)[:, KT * l:KT * (l + 1)]
                    scale = self.mod[:, (3 * i + 1) * KT:(3 * i + 2) * KT]
                    nc.vector.scalar_tensor_tensor(self.modA[:, i, :], scale, 1.0, gain, ALU.add, ALU.mult)

    def ffn(self, name, gain=None, layer_norm=None):
        nc = self.nc
        with ExitStack() as ctx, self.stage(
                "n_ms n_rstd n_xn n_tr n_hT up_done silu_done hid_ready down_done l_ms l_rstd x_done", name) as (block, S):
            sg = self.sb("silu_gate", [P, 2, 2, SEQ], ctx=ctx)
            hid = self.sb("hidden", [P, 2, 2, SEQ], ctx=ctx)
            if layer_norm:
                lnp = self.sb("ln_params", [P, 2, D], ctx=ctx)
                ln_landed = nc.alloc_semaphore("ln_landed_" + name)
            base = self.taken

            def landed(n, i):
                return self.landed_at[n] + 16 * i

            def up(pe, c, i, it, parity):
                for m in range(2):
                    n = base + c + m
                    pe.wait_ge(self.w_landed[n % RING], landed(n, i))
                    slot = self.ring[:, n % RING, :].rearrange("p (k n) -> p k n", k=KT)
                    if m == 0 and it is not None:
                        pe.wait_ge(S.hid_ready, it)
                    for t in range(2):
                        for k in range(KT):
                            ins = nc.tensor.matmul(self.PS[:, 2 * parity + m, t * SEQ:(t + 1) * SEQ],
                                                   slot[:, k, t * P:(t + 1) * P], self.hT[:, k, :],
                                                   start=(k == 0), stop=(k == KT - 1))
                    ins.then_inc(self.w_used, 1)

            def down(pe, c, i, it, parity, first=False, last=False):
                n = base + c
                pe.wait_ge(self.w_landed[n % RING], landed(n, i))
                pe.wait_ge(S.hid_ready, it + 1)
                slot = self.ring[:, n % RING, :].rearrange("p (k n) -> p k n", k=2)
                for t in range(2):
                    for b in range(NB):
                        for h in range(2):
                            ins = nc.tensor.matmul(self.PS[:, 4 + 2 * b + h, :], hid[:, parity, t, b * P:(b + 1) * P],
                                                   slot[:, t, h * BANK:(h + 1) * BANK],
                                                   start=(first and t == 0), stop=(last and t == 1),
                                                   skip_group_check=True)
                ins.then_inc(self.w_used, 1)

            @block.tensor
            def _(pe):
                if layer_norm:
                    for b in range(NB):
                        for g in range(2):
                            for j in range(4):
                                k = 4 * g + j
                                ins = nc.tensor.transpose(self.PS[:, 4 + 2 * b + g, j * P:(j + 1) * P],
                                                          self.X[:, b, k * P:(k + 1) * P], self.ident)
                            ins.then_inc(S.n_tr, 1)
                else:
                    self.norm_tensor(pe, S)
                pe.wait_ge(S.n_hT, self.N_HT)
                up(pe, 0, 0, None, 0)
                up(pe, 2, 0, None, 1)
                down(pe, 4, 0, 0, 0, first=True)
                with pe.Fori(0, (FF_STEPS - 3) // 2) as i:
                    for u in range(2):
                        up(pe, 5 + 3 * u, i, i * 2 + (1 + u), u)
                        down(pe, 7 + 3 * u, i, i * 2 + (1 + u), 1 - u)
                s = FF_STEPS - 2
                c = 5 + 3 * (s - 1)
                up(pe, c, 0, s, (s + 1) % 2)
                down(pe, c + 2, 0, s, s % 2)
                down(pe, c + 3, 0, s + 1, (s + 1) % 2, last=True)
                self.taken += 3 * FF_STEPS

            def silu_step(act, it, used, parity):
                act.wait_ge(self.w_used, used)
                nc.scalar.activation(sg[:, parity].rearrange("p t n -> p (t n)"), self.PS[:, 2 * parity, :],
                                     ACT.Silu).then_inc(S.silu_done, 1)

            def used_at(s):
                return base + (2 if s == 0 else 3 * s + 1)

            @block.scalar
            def _(act):
                if layer_norm:
                    for i, v in enumerate(layer_norm):
                        act.dma_start(lnp[:, i, :], v.partition_broadcast(P)).then_inc(ln_landed, 16)
                    self.copy_tiles(act, nc.scalar.copy, S, 0)
                else:
                    self.norm_scalar(act, S, gain, None)
                silu_step(act, 0, used_at(0), 0)
                with act.Fori(0, (FF_STEPS - 1) // 2) as i:
                    for u in range(2):
                        silu_step(act, None, i * 6 + used_at(1 + u), 1 - u)

            def hid_step(ve, parity, silu, downs):
                ve.wait_ge(S.silu_done, silu)
                if downs is not None:
                    ve.wait_ge(self.w_used, downs)
                nc.vector.tensor_tensor(hid[:, parity].rearrange("p t n -> p (t n)"),
                                        sg[:, parity].rearrange("p t n -> p (t n)"),
                                        self.PS[:, 2 * parity + 1, :], ALU.mult).then_inc(S.hid_ready, 1)

            @block.vector
            def _(ve):
                if layer_norm:
                    self.copy_tiles(ve, nc.vector.tensor_copy, S, 1)
                else:
                    self.norm_vector(ve, S, gain, None)
                hid_step(ve, 0, 1, None)
                hid_step(ve, 1, 2, None)
                with ve.Fori(0, (FF_STEPS - 3) // 2) as i:
                    for u in range(2):
                        hid_step(ve, u, i * 2 + (3 + u), i * 6 + (base + 3 * (u + 2) - 1))
                s = FF_STEPS - 1
                hid_step(ve, s % 2, s + 1, base + 3 * s - 1)
                ve.wait_ge(self.w_used, base + 3 * FF_STEPS)
                out = self.PS[:, 4:8, :].rearrange("p (b h) n -> p b (h n)", b=NB)
                if not layer_norm:
                    for b in range(NB):
                        nc.vector.scalar_tensor_tensor(self.X[:, b, :], out[:, b, :], 0.5, self.X[:, b, :],
                                                       ALU.mult, ALU.add)
                else:
                    for b in range(NB):
                        nc.vector.tensor_scalar(self.X[:, b, :], self.X[:, b, :], ALPHA, None, ALU.mult)
                    nc.vector.drain()
                    for b in range(NB):
                        nc.vector.scalar_tensor_tensor(self.X[:, b, :], out[:, b, :], 0.5, self.X[:, b, :],
                                                       ALU.mult, ALU.add)
                    nc.vector.drain()
                    ve.wait_ge(ln_landed, 32)
                    self.layer_norm_vector(ve, S, lnp)

            @block.gpsimd
            def _(pool):
                if layer_norm:
                    self.layer_norm_gpsimd(pool, S)
                else:
                    self.norm_gpsimd(pool, S)

    def copy_tiles(self, eng, copy, S, odd):
        for b in range(NB):
            eng.wait_ge(S.n_tr, 2 * b + odd + 1)
            copy(self.hT[:, 4 * odd:4 * odd + 4, b * P:(b + 1) * P],
                 self.PS[:, 4 + 2 * b + odd, :].rearrange("p (k n) -> p k n", k=4)).then_inc(S.n_hT, 1)

    def layer_norm_vector(self, ve, S, lnp):
        nc = self.nc
        nc.vector.reduce_sum(self.mu[:], self.X[:], AX.X)
        nc.vector.drain()
        nc.vector.tensor_scalar(self.negmu[:], self.mu[:], -1.0 / D, None, ALU.mult)
        nc.vector.drain()
        for b in range(NB):
            nc.vector.tensor_scalar(self.X[:, b, :], self.X[:, b, :], self.negmu[:, b:b + 1], None, ALU.add)
        nc.vector.drain()
        for b in range(NB):
            nc.vector.tensor_tensor_reduce(self.xn[:, b, :], self.X[:, b, :], self.X[:, b, :], 1.0 / D, LN_EPS,
                                           ALU.mult, ALU.add, self.ms[:, b:b + 1])
        nc.vector.drain().then_inc(S.l_ms, 1)
        ve.wait_ge(S.l_rstd, 1)
        for b in range(NB):
            nc.vector.scalar_tensor_tensor(self.X[:, b, :], self.X[:, b, :], self.rstd[:, b:b + 1], lnp[:, 0, :],
                                           ALU.mult, ALU.mult)
        nc.vector.drain()
        for b in range(NB):
            nc.vector.tensor_tensor(self.X[:, b, :], self.X[:, b, :], lnp[:, 1, :], ALU.add)

    def layer_norm_gpsimd(self, pool, S):
        pool.wait_ge(S.l_ms, 1)
        self.nc.gpsimd.tensor_tensor(self.rstd[:], self.ms[:], self.neghalf[:, 0:NB], ALU.pow).then_inc(S.l_rstd, 1)

    def final_norm(self, gain):
        nc = self.nc
        with ExitStack() as ctx, self.stage("ms rstd done") as (block, S):
            g = self.sb("final_gain", [P, D], ctx=ctx)
            landed = nc.alloc_semaphore("gain_landed_" + str(self.n_stage))

            @block.scalar
            def _(act):
                act.dma_start(g[:], gain.partition_broadcast(P)).then_inc(landed, 16)

            @block.vector
            def _(ve):
                for b in range(NB):
                    nc.vector.tensor_tensor_reduce(self.xn[:, b, :], self.X[:, b, :], self.X[:, b, :], 1.0 / D, EPS,
                                                   ALU.mult, ALU.add, self.ms[:, b:b + 1])
                nc.vector.drain().then_inc(S.ms, 1)
                ve.wait_ge(S.rstd, 1)
                ve.wait_ge(landed, 16)
                for b in range(NB):
                    nc.vector.scalar_tensor_tensor(self.X[:, b, :], self.X[:, b, :], self.rstd[:, b:b + 1], g[:],
                                                   ALU.mult, ALU.mult)

            @block.gpsimd
            def _(pool):
                pool.wait_ge(S.ms, 1)
                nc.gpsimd.tensor_tensor(self.rstd[:], self.ms[:], self.neghalf[:, 0:NB], ALU.pow).then_inc(S.rstd, 1)

    def store(self, out):
        nc = self.nc
        stored = nc.alloc_semaphore("stored")
        with self.stage("") as (block, S):
            @block.scalar
            def _(act):
                act.dma_start(out[0].rearrange("(b p) d -> p b d", p=P), self.X[:]).then_inc(stored, 16)
                act.wait_ge(stored, 16)

    def mixer(self, l):
        nc, a = self.nc, self.a
        with ExitStack() as ctx:
            U = self.sb("gelu_u", [P, NB, HALF], ctx=ctx)
            V = self.sb("gelu_v", [P, NB, HALF], ctx=ctx)
            QT = self.sb("stick_qT", [P, 4, SEQ], ctx=ctx)
            KT_ = self.sb("stick_kT", [P, 4, SEQ], ctx=ctx)
            SV = self.sb("stick_v", [P, NB, HALF], ctx=ctx)
            Y = self.sb("mixed", [P, NB, D], ctx=ctx)
            vgain = self.sb("v_gain", [P, HALF], ctx=ctx)
            ws = self.sb("gm_w", [P, HEADS, P], ctx=ctx)
            side = nc.alloc_semaphore(f"mixer_side{l}")

            with self.stage("n_ms n_rstd n_xn n_tr n_hT p_free0 p_free1", f"mix_in{l}") as (block, S):
                jobs = [("T", 512), ("T", 512), ("F", 512), ("F", 512), ("T", 512)]

                @block.tensor
                def _(pe):
                    self.norm_tensor(pe, S)
                    pe.wait_ge(S.n_hT, self.N_HT)
                    self.project(pe, S, jobs, self.hT, KT)

                @block.scalar
                def _(act):
                    act.dma_start(vgain[:], a["gm_vnorm"][l].partition_broadcast(P)).then_inc(side, 16)
                    act.dma_start(ws[:], a["gm_ws"][l].rearrange("h t s -> t h s")).then_inc(side, 16)
                    self.norm_scalar(act, S, self.modA[:, 0, :], self.mod[:, 0:KT])
                    for j, dst in enumerate((U, V)):
                        self.leave(act, j)
                        for e in range(2):
                            nc.scalar.activation(dst[:, e, :], self.bank(j, e), ACT.Gelu_apprx_tanh).then_inc(self.freed(S, j), 1)
                    self.leave(act, 4)
                    for e in range(2):
                        nc.scalar.copy(SV[:, e, :], self.bank(4, e)).then_inc(self.freed(S, 4), 1)

                @block.vector
                def _(ve):
                    self.norm_vector(ve, S, self.modA[:, 0, :], self.mod[:, 0:KT])
                    for j, dst, scale in ((2, QT, 0.125), (3, KT_, 1.0)):
                        self.leave(ve, j)
                        for e in range(2):
                            nc.vector.tensor_scalar(dst[:, 2 * e:2 * e + 2, :].rearrange("p t n -> p (t n)"),
                                                    self.bank(j, e), scale, None, ALU.mult).then_inc(self.freed(S, j), 1)

                @block.gpsimd
                def _(pool):
                    self.norm_gpsimd(pool, S)

            with self.stage("scores sp keep summed expo att pv y_b wT wT_out v_ms v_rstd v_hat gated") as (block, S):
                wT = self.sb("gm_wT", [P, HEADS, P], ctx=ctx)
                sq = self.sb("v_squares", [P, NB, HALF], ctx=ctx)
                vms = self.sb("v_ms", [P, NB * HEADS], ctx=ctx)
                vrs = self.sb("v_rstd", [P, NB * HEADS], ctx=ctx)
                W3 = 3 * P
                ab = self.sb("stick_abs", [P, 2, W3], ctx=ctx)
                sp = self.sb("stick_softplus", [P, 2, W3], ctx=ctx)
                keep = self.sb("stick_keep", [P, 2, W3], ctx=ctx)
                lg = self.sb("stick_log", [P, 2, W3], ctx=ctx)
                at = self.sb("stick_att", [P, 2, W3], ctx=ctx)
                v3 = lambda t: t.rearrange("p b (h c) -> p (b h) c", h=HEADS)

                @block.tensor
                def _(pe):
                    pe.wait_ge(side, 32)
                    for h in range(HEADS):
                        ins = nc.tensor.transpose(self.PS[:, 4 + h // 4, (h % 4) * P:(h % 4 + 1) * P], ws[:, h, :], self.ident)
                    ins.then_inc(S.wT, 1)

                    def scores(h):
                        r, t, Z = 64 * (h % 2), h // 2, self.PS[:, h % 2, :]
                        if h >= 2:
                            pe.wait_ge(S.expo, h - 1)
                        nc.tensor.matmul(Z[:, 0:SEQ], KT_[r:r + 64, t, 0:P], QT[r:r + 64, t, :], start=True, stop=False,
                                         skip_group_check=True)
                        nc.tensor.matmul(Z[:, SEQ:W3], KT_[r:r + 64, t, P:SEQ], QT[r:r + 64, t, P:SEQ], start=False,
                                         stop=False, skip_group_check=True).then_inc(S.scores, 1)

                    def sums(h):
                        Z, lk = self.PS[:, h % 2, :], keep[:, h % 2, :]
                        pe.wait_ge(S.keep, h + 1)
                        nc.tensor.matmul(Z[:, 0:SEQ], self.from_, lk[:, 0:SEQ], start=False, stop=True, skip_group_check=True)
                        nc.tensor.matmul(Z[:, P:SEQ], self.ones, lk[:, SEQ:W3], start=False, stop=True, skip_group_check=True)
                        nc.tensor.matmul(Z[:, SEQ:W3], self.from_, lk[:, SEQ:W3], start=False, stop=True,
                                         skip_group_check=True).then_inc(S.summed, 1)

                    def values(h):
                        c = slice(64 * h, 64 * h + 64)
                        pe.wait_ge(S.att, h + 1)
                        A = at[:, h % 2, :]
                        nc.tensor.matmul(self.PS[:, 2, c], A[:, 0:P], SV[:, 0, c], start=True, stop=True)
                        nc.tensor.matmul(self.PS[:, 3, c], A[:, P:SEQ], SV[:, 0, c], start=True, stop=False)
                        nc.tensor.matmul(self.PS[:, 3, c], A[:, SEQ:W3], SV[:, 1, c], start=False, stop=True).then_inc(S.pv, 1)

                    scores(0)
                    for h in range(HEADS):
                        if h + 1 < HEADS:
                            scores(h + 1)
                        sums(h)
                        if h >= 1:
                            values(h - 1)
                        if h == 3:
                            pe.wait_ge(S.wT_out, 1)
                            pe.wait_ge(S.v_hat, 1)
                            for b in range(NB):
                                for g in range(HEADS):
                                    c = slice(64 * g, 64 * g + 64)
                                    ins = nc.tensor.matmul(self.PS[:, 6 + b, c], wT[:, g, :], V[:, b, c], start=True, stop=True)
                            ins.then_inc(S.gated, 1)
                    values(HEADS - 1)

                @block.scalar
                def _(act):
                    def log_keep(h):
                        i = h % 2
                        act.wait_ge(S.scores, h + 1)
                        nc.scalar.activation(ab[:, i, :], self.PS[:, i, 0:W3], ACT.Abs)
                        nc.scalar.drain()
                        nc.scalar.activation(sp[:, i, :], ab[:, i, :], ACT.Exp, scale=-1.0)
                        nc.scalar.drain()
                        nc.scalar.activation(sp[:, i, :], sp[:, i, :], ACT.Ln, bias=1.0).then_inc(S.sp, 1)

                    def weights(h):
                        act.wait_ge(S.expo, h + 1)
                        if h >= 2:
                            act.wait_ge(S.pv, h - 1)
                        nc.scalar.activation(at[:, h % 2, :], lg[:, h % 2, :], ACT.Exp).then_inc(S.att, 1)

                    log_keep(0)
                    for h in range(HEADS):
                        if h + 1 < HEADS:
                            log_keep(h + 1)
                        weights(h)

                @block.vector
                def _(ve):
                    def keeps(h):
                        i = h % 2
                        ve.wait_ge(S.sp, h + 1)
                        nc.vector.scalar_tensor_tensor(sp[:, i, :], self.PS[:, i, 0:W3], 0.0, sp[:, i, :], ALU.max, ALU.add)
                        nc.vector.drain()
                        nc.vector.scalar_tensor_tensor(keep[:, i, :], sp[:, i, :], -1.0, self.strict3, ALU.mult,
                                                       ALU.mult).then_inc(S.keep, 1)

                    def exponents(h):
                        ve.wait_ge(S.summed, h + 1)
                        if h >= 2:
                            ve.wait_ge(S.att, h - 1)
                        nc.vector.tensor_tensor(lg[:, h % 2, :], self.PS[:, h % 2, 0:W3], self.strict3_add,
                                                ALU.add).then_inc(S.expo, 1)

                    def gate_inputs():
                        nc.vector.tensor_tensor(sq[:], V[:], V[:], ALU.mult)
                        nc.vector.drain()
                        nc.vector.tensor_reduce(vms[:], v3(sq[:]), AX.X, ALU.add)
                        nc.vector.drain()
                        nc.vector.tensor_scalar(vms[:], vms[:], 1.0 / 64, EPS, ALU.mult, ALU.add).then_inc(S.v_ms, 1)
                        ve.wait_ge(S.wT, 1)
                        nc.vector.tensor_copy(wT[:].rearrange("p (g h) n -> p g (h n)", g=2), self.PS[:, 4:6, :])
                        nc.vector.drain()
                        nc.vector.memset(wT[64:128, :, 0:64], 0.0).then_inc(S.wT_out, 1)

                    def gate_scale():
                        ve.wait_ge(S.v_rstd, 1)
                        nc.vector.tensor_tensor(v3(V[:]), v3(V[:]), vrs[:].unsqueeze(2).to_broadcast([P, NB * HEADS, 64]), ALU.mult)
                        nc.vector.drain()
                        nc.vector.tensor_tensor(V[:], V[:], vgain[:].unsqueeze(1).to_broadcast([P, NB, HALF]),
                                                ALU.mult).then_inc(S.v_hat, 1)

                    def gate_outputs():
                        ve.wait_ge(S.gated, 1)
                        bias = self.col("gm_bs")[:, HEADS * l:HEADS * (l + 1)].unsqueeze(2).to_broadcast([P, HEADS, 64])
                        for b in range(NB):
                            nc.vector.tensor_tensor(sq[:, b, :].rearrange("p (h c) -> p h c", h=HEADS),
                                                    self.PS[:, 6 + b, :].rearrange("p (h c) -> p h c", h=HEADS), bias, ALU.add)
                        nc.vector.drain()
                        nc.vector.tensor_tensor(Y[:, :, 0:HALF], sq[:], U[:], ALU.mult)

                    ve.wait_ge(side, 32)
                    gate_inputs()
                    keeps(0)
                    for h in range(HEADS):
                        if h == 1:
                            gate_scale()
                        if h + 1 < HEADS:
                            keeps(h + 1)
                        exponents(h)
                        if h == 5:
                            gate_outputs()
                    ve.wait_ge(S.pv, HEADS)
                    nc.vector.tensor_copy(Y[:, :, HALF:D], self.PS[:, 2:4, :])

                @block.gpsimd
                def _(pool):
                    pool.wait_ge(S.v_ms, 1)
                    nc.gpsimd.tensor_tensor(vrs[:], vms[:], self.neghalf[:, 0:NB * HEADS], ALU.pow).then_inc(S.v_rstd, 1)

            with self.stage("n_ms n_rstd n_xn n_tr n_hT p_free0 p_free1", f"mix_out{l}") as (block, S):
                ms4 = self.sb("group_ms", [P, 4], ctx=ctx)
                rs4 = self.sb("group_rstd", [P, 4], ctx=ctx)
                junk = self.sb("junk", [P, HALF], ctx=ctx)
                halves = Y[:].rearrange("p b (g n) -> p (b g) n", g=2)
                gains = self.sb("group_gains", [P, KT], ctx=ctx)

                @block.tensor
                def _(pe):
                    self.norm_tensor(pe, S, src=Y)
                    pe.wait_ge(S.n_hT, self.N_HT)
                    self.project(pe, S, [("T", 512)] * 2, self.hT, KT)

                @block.scalar
                def _(act):
                    act.wait_ge(S.n_xn, 1)
                    self.norm_scalar(act, S, gains[:], None)

                @block.vector
                def _(ve):
                    for i, name in enumerate(("out_norm_a", "out_norm_b")):
                        nc.vector.tensor_copy(gains[:, 4 * i:4 * i + 4], self.col(name)[:, 4 * l:4 * l + 4])
                    for i in range(4):
                        nc.vector.tensor_tensor_reduce(self.xn[:, i // 2, (i % 2) * HALF:(i % 2 + 1) * HALF], halves[:, i, :], halves[:, i, :], 1.0 / HALF, EPS,
                                                       ALU.mult, ALU.add, ms4[:, i:i + 1])
                    nc.vector.drain().then_inc(S.n_ms, 1)
                    ve.wait_ge(S.n_rstd, 1)
                    for i in range(4):
                        ins = nc.vector.tensor_scalar(halves[:, i, :], halves[:, i, :], rs4[:, i:i + 1], None, ALU.mult)
                        if i % 2:
                            ins.then_inc(S.n_xn, 1)
                    self.evacuate_tiles(ve, nc.vector, S, 1, gains[:], None)
                    self.gated_residual(ve, S, 0, ctx)

                @block.gpsimd
                def _(pool):
                    pool.wait_ge(S.n_ms, 1)
                    nc.gpsimd.tensor_tensor(rs4[:], ms4[:], self.neghalf[:, 0:4], ALU.pow).then_inc(S.n_rstd, 1)

    def gated_residual(self, ve, S, which, ctx):
        nc = self.nc
        for j in range(2):
            c = slice(j * BANK, (j + 1) * BANK)
            self.leave(ve, j)
            for b in range(NB):
                nc.vector.tensor_tensor(self.xn[:, b, c], self.bank(j, b), self.gate[:, which, c],
                                        ALU.mult).then_inc(self.freed(S, j), 1)
            nc.vector.drain()
            nc.vector.tensor_tensor(self.X[:, :, c], self.X[:, :, c], self.xn[:, :, c], ALU.add)

    def plain_residual(self, ve, S):
        for j in range(2):
            c = slice(j * BANK, (j + 1) * BANK)
            self.leave(ve, j)
            for b in range(NB):
                self.nc.vector.tensor_tensor(self.X[:, b, c], self.bank(j, b), self.X[:, b, c],
                                             ALU.add).then_inc(self.freed(S, j), 1)

    def peer(self, l):
        nc, a = self.nc, self.a
        with ExitStack() as ctx:
            N2 = 2 * HEADS
            H = self.sb("peer_h", [P, NB, D], ctx=ctx)
            keys = self.sb("peer_keys", [P, 2, P], ctx=ctx)
            keysT = self.sb("peer_keysT", [P, 2, P], ctx=ctx)
            SC = self.sb("peer_scores", [P, NB, 2 * HEADS, P], ctx=ctx)
            E = self.sb("peer_ids", [P, NB, P], I32, ctx=ctx)
            G = self.sb("peer_gates", [P, NB, P], ctx=ctx)
            side = nc.alloc_semaphore(f"peer_side{l}")

            with ExitStack() as inner, self.stage(
                    "n_ms n_rstd n_xn n_tr n_hT p_free0 p_free1 back back_out keysT keysT_out scores", f"peer_q{l}") as (block, S):
                QT = self.sb("peer_qT", [P, N2, SEQ], ctx=inner)
                shift = self.mod[:, 3 * KT:4 * KT]

                @block.tensor
                def _(pe):
                    self.norm_tensor(pe, S)
                    pe.wait_ge(S.n_hT, self.N_HT)
                    for b in range(NB):
                        for g in range(2):
                            for j in range(4):
                                k = 4 * g + j
                                ins = nc.tensor.transpose(self.PS[:, 4 + 2 * b + g, j * P:(j + 1) * P],
                                                          self.hT[:, k, b * P:(b + 1) * P], self.ident)
                    ins.then_inc(S.back, 1)
                    self.project(pe, S, [("F", 512)] * 4, self.hT, KT)
                    pe.wait_ge(side, 32)
                    pe.wait_ge(S.back_out, 1)
                    for i in range(2):
                        ins = nc.tensor.transpose(self.PS[:, 4, i * P:(i + 1) * P], keys[:, i, :], self.ident)
                    ins.then_inc(S.keysT, 1)
                    pe.wait_ge(S.p_free0, 4)
                    pe.wait_ge(S.p_free1, 4)
                    pe.wait_ge(S.keysT_out, 1)
                    for b in range(NB):
                        for i in range(N2):
                            ins = nc.tensor.matmul(self.PS[:, 4 * b + i // 4, (i % 4) * P:(i % 4 + 1) * P],
                                                   QT[:, i, b * P:(b + 1) * P], keysT[:, i % 2, :], start=True, stop=True)
                        ins.then_inc(S.scores, 1)

                @block.scalar
                def _(act):
                    for i, name in enumerate(("peer_k1", "peer_k2")):
                        act.dma_start(keys[:, i, :], a[name][l]).then_inc(side, 16)
                    self.norm_scalar(act, S, self.modA[:, 1, :], shift)
                    act.wait_ge(S.back, 1)
                    nc.scalar.copy(H[:].rearrange("p b (g n) -> p (b g) n", n=BANK), self.PS[:, 4:8, :]).then_inc(S.back_out, 1)
                    for j in (1, 3):
                        self.leave(act, j)
                        for e in range(2):
                            nc.scalar.copy(QT[:, 4 * j + 2 * e:4 * j + 2 * e + 2, :].rearrange("p t n -> p (t n)"),
                                           self.bank(j, e)).then_inc(self.freed(S, j), 1)
                    for b in range(NB):
                        act.wait_ge(S.scores, b + 1)
                        nc.scalar.copy(SC[:, b].rearrange("p (g i) n -> p g (i n)", g=4), self.PS[:, 4 * b:4 * b + 4, :])

                @block.vector
                def _(ve):
                    self.norm_vector(ve, S, self.modA[:, 1, :], shift)
                    for j in (0, 2):
                        self.leave(ve, j)
                        for e in range(2):
                            nc.vector.tensor_copy(QT[:, 4 * j + 2 * e:4 * j + 2 * e + 2, :].rearrange("p t n -> p (t n)"),
                                                  self.bank(j, e)).then_inc(self.freed(S, j), 1)
                    ve.wait_ge(S.keysT, 1)
                    nc.vector.tensor_copy(keysT[:].rearrange("p i n -> p (i n)"), self.PS[:, 4, 0:2 * P]).then_inc(S.keysT_out, 1)

                @block.gpsimd
                def _(pool):
                    self.norm_gpsimd(pool, S)

            with self.stage("ids shifted expd dots gelu") as (block, S):
                v16 = self.sb("top_values", [P, N2, TOPK], ctx=ctx)
                i16 = self.sb("top_indices", [P, N2, TOPK], U32, ctx=ctx)
                i16f = self.sb("top_indices_f", [P, N2, TOPK], ctx=ctx)
                cand = self.hT[:].rearrange("p k n -> p (k n)").rearrange("p (h n) -> p h n", h=HEADS)
                ts = self.sb("pair_scores", [P, HEADS, TOPK], ctx=ctx)
                tp = self.sb("pair_positions", [P, HEADS, TOPK], U32, ctx=ctx)
                part = self.sb("pair_part", [P, 2, HEADS, TOPK], U32, ctx=ctx)
                partf = self.sb("pair_part_f", [P, 2, HEADS, TOPK], ctx=ctx)
                pick = self.xn[:].rearrange("p b n -> p (b n)").rearrange("p (h x y) -> p h x y", h=HEADS, x=TOPK)
                found = self.sb("pair_found", [P, 2, HEADS, TOPK], ctx=ctx)
                idf = self.sb("expert_f", [P, HEADS * TOPK], ctx=ctx)
                sums = self.sb("gate_sums", [P, HEADS], ctx=ctx)
                rsum = self.sb("gate_rsums", [P, HEADS], ctx=ctx)
                shifted = self.sb("gate_shifted", [P, HEADS, TOPK], ctx=ctx)
                rows = self.sb("expert_rows", [P, GRING, D], ctx=ctx)
                turn = self.sb("gather_index", [P, 2, GHALF], I32, ctx=ctx)
                part16 = self.sb("dots16", [P, GRING], ctx=ctx)
                dots = self.sb("dots", [P, P], ctx=ctx)
                wts = self.sb("expert_weights", [P, P], ctx=ctx)
                acc = self.sb("peer_out", [P, D], ctx=ctx)
                base = l * 4 * P

                @block.scalar
                def _(act):
                    for b in range(NB):
                        act.wait_ge(S.shifted, b + 1)
                        nc.scalar.activation(G[:, b, :], shifted[:].rearrange("p h k -> p (h k)"), ACT.Exp).then_inc(S.expd, 1)
                    for b in range(NB):
                        act.wait_ge(S.dots, b + 1)
                        nc.scalar.activation(wts[:], dots[:], ACT.Gelu_apprx_tanh).then_inc(S.gelu, 1)

                def top16(values, indices, src, n):
                    for i in range(n):
                        nc.vector.max(values[:, i, 0:8], src[:, i, :])
                    nc.vector.drain()
                    for i in range(n):
                        nc.vector.max_index(indices[:, i, 0:8], values[:, i, 0:8], src[:, i, :])
                    nc.vector.drain()
                    for i in range(n):
                        nc.vector.match_replace(src[:, i, :], values[:, i, 0:8], src[:, i, :], TAKEN)
                    nc.vector.drain()
                    for i in range(n):
                        nc.vector.max(values[:, i, 8:16], src[:, i, :])
                    nc.vector.drain()
                    for i in range(n):
                        nc.vector.max_index(indices[:, i, 8:16], values[:, i, 8:16], src[:, i, :])
                    nc.vector.drain()

                def retrieve(ve, b):
                    top16(v16, i16, SC[:, b], N2)
                    nc.vector.tensor_copy(i16f[:], i16[:])
                    v = v16[:].rearrange("p (h s) k -> p s h k", s=2)
                    full = [P, HEADS, TOPK, TOPK]
                    nc.vector.tensor_tensor(cand.rearrange("p h (x y) -> p h x y", x=TOPK),
                                            v[:, 0].unsqueeze(3).to_broadcast(full), v[:, 1].unsqueeze(2).to_broadcast(full), ALU.add)
                    nc.vector.drain()
                    top16(ts, tp, cand, HEADS)
                    nc.vector.tensor_scalar(part[:, 0], tp[:], 4, None, ALU.logical_shift_right)
                    nc.vector.tensor_scalar(part[:, 1], tp[:], 15, None, ALU.bitwise_and)
                    nc.vector.tensor_tensor(shifted[:], ts[:], ts[:, :, 0:1].to_broadcast([P, HEADS, TOPK]), ALU.subtract)
                    nc.vector.drain().then_inc(S.shifted, 1)
                    nc.vector.tensor_copy(partf[:], part[:])
                    nc.vector.drain()
                    idx = i16f[:].rearrange("p (h s) k -> p s h k", s=2)
                    for s in range(2):
                        nc.vector.tensor_tensor(pick, partf[:, s].unsqueeze(3).to_broadcast(full),
                                                self.iota16.unsqueeze(1).unsqueeze(1).to_broadcast(full), ALU.is_equal)
                        nc.vector.drain()
                        nc.vector.tensor_tensor(pick, pick, idx[:, s].unsqueeze(2).to_broadcast(full), ALU.mult)
                        nc.vector.drain()
                        nc.vector.tensor_reduce(found[:, s], pick, AX.X, ALU.add)
                        nc.vector.drain()
                    nc.vector.scalar_tensor_tensor(idf[:], found[:, 0].rearrange("p h k -> p (h k)"), float(P),
                                                   found[:, 1].rearrange("p h k -> p (h k)"), ALU.mult, ALU.add)
                    nc.vector.drain()
                    nc.vector.tensor_scalar(E[:, b, :], idf[:], float(l * P * P), None, ALU.add).then_inc(S.ids, 1)
                    ve.wait_ge(S.expd, b + 1)
                    g = G[:, b, :].rearrange("p (h k) -> p h k", h=HEADS)
                    nc.vector.tensor_reduce(sums[:], g, AX.X, ALU.add)
                    nc.vector.drain()
                    nc.vector.reciprocal(rsum[:], sums[:])
                    nc.vector.drain()
                    nc.vector.tensor_tensor(g, g, rsum[:].unsqueeze(2).to_broadcast([P, HEADS, TOPK]), ALU.mult)
                    nc.vector.drain()

                steps = P // GRING

                def turns(phase):
                    return (base + phase * P) // GRING

                @block.vector
                def _(ve):
                    if l == 0:
                        ve.sem_inc(self.g_used, GHALF + 1)
                    for b in range(NB):
                        retrieve(ve, b)
                    for b in range(NB):
                        with ve.Fori(0, steps) as i:
                            for u in range(GRING):
                                ve.wait_ge(self.g_landed[u], i * 16 + 16 * (turns(2 * b) + 1))
                                nc.vector.tensor_tensor_reduce(rows[:, u, :], rows[:, u, :], H[:, b, :], 1.0, 0.0, ALU.mult,
                                                               ALU.add, part16[:, u:u + 1]).then_inc(self.g_used, 1)
                            nc.vector.drain()
                            nc.vector.tensor_copy(dots[:, bass.ds(i * GRING, GRING)], part16[:])
                            nc.vector.drain()
                        nc.vector.memset(acc[:], 0.0)
                        nc.vector.drain().then_inc(S.dots, 1)
                        ve.wait_ge(S.gelu, b + 1)
                        nc.vector.tensor_tensor(wts[:], wts[:], G[:, b, :], ALU.mult)
                        nc.vector.drain()
                        with ve.Fori(0, steps) as i:
                            for u in range(GRING):
                                ve.wait_ge(self.g_landed[u], i * 16 + 16 * (turns(2 * b + 1) + 1))
                                nc.vector.scalar_tensor_tensor(acc[:], rows[:, u, :], wts[:, bass.ds(i * GRING + u, 1)], acc[:],
                                                               ALU.mult, ALU.add).then_inc(self.g_used, 1)
                                nc.vector.drain()
                        nc.vector.tensor_tensor(acc[:], acc[:], self.gate[:, 1, :], ALU.mult)
                        nc.vector.drain()
                        nc.vector.tensor_tensor(self.X[:, b, :], self.X[:, b, :], acc[:], ALU.add)
                        nc.vector.drain()

                @block.gpsimd
                def _(pool):
                    for phase in range(2 * NB):
                        b = phase // 2
                        table = a[("peer_u", "peer_v")[phase % 2]].rearrange("l n d -> (l n) d")
                        if phase % 2 == 0:
                            pool.wait_ge(S.ids, b + 1)
                        with pool.Fori(0, steps) as i:
                            for half in range(2):
                                n = i * GRING + (base + phase * P + half * GHALF + 1)
                                pool.wait_ge(self.g_used, n)
                                nc.gpsimd.sem_inc(self.g_turn, 1)
                                nc.gpsimd.tensor_copy(turn[:, half, :], E[:, b, bass.ds(i * GRING + half * GHALF, GHALF)]
                                                      ).then_inc(self.g_index, 1)
                                pool.wait_ge(self.g_index, i * 2 + (2 * turns(phase) + half + 1))
                                nc.gpsimd.sem_inc(self.g_turn, 1)
                                for u in range(GHALF):
                                    s = half * GHALF + u
                                    pool.indirect_dma_start(rows[:, s, :], None, table,
                                                            bass.IndirectOffsetOnAxis(ap=turn[:, half, u:u + 1], axis=0)
                                                            ).then_inc(self.g_landed[s], 16)

    def pool_conv(self):
        nc, a = self.nc, self.a
        PAD = KERN - 1
        with ExitStack() as ctx:
            u = self.sb("pool_u", [P, 4, 16 + SEQ], ctx=ctx)
            val = self.sb("conv_value", [P, 4, SEQ], ctx=ctx)
            z = self.sb("conv_z", [P, 4, PAD + SEQ], ctx=ctx)
            YT = self.sb("pool_conv_yT", [P, KT, SEQ], ctx=ctx)
            sig = self.sb("conv_sigmoid", [P, 4, SEQ], ctx=ctx)
            pw = self.sb("pool_w", [P, 4, P], ctx=ctx)
            side = nc.alloc_semaphore("pool_w_landed")
            gain = self.col("mix_norm_2")[:, 0:KT]

            with self.stage("n_ms n_rstd n_xn n_tr n_hT p_free0 p_free1 sig", "ab_in") as (block, S):
                @block.tensor
                def _(pe):
                    self.norm_tensor(pe, S)
                    pe.wait_ge(S.n_hT, self.N_HT)
                    self.project(pe, S, [("F", 512)] * 3, self.hT, KT)

                @block.scalar
                def _(act):
                    act.dma_start(pw[:], a["pool_w_2"][0].rearrange("g c d -> c g d")).then_inc(side, 16)
                    self.norm_scalar(act, S, gain, None)
                    self.leave(act, 2)
                    for e in range(2):
                        nc.scalar.activation(sig[:, 2 * e:2 * e + 2, :].rearrange("p t n -> p (t n)"), self.bank(2, e),
                                             ACT.Sigmoid).then_inc(S.sig, 1)

                @block.vector
                def _(ve):
                    nc.vector.memset(u[:, :, 0:16], 0.0)
                    nc.vector.memset(z[:, :, 0:PAD], 0.0)
                    self.norm_vector(ve, S, gain, None)
                    for j, dst in ((0, u[:, :, 16:]), (1, val[:])):
                        self.leave(ve, j)
                        for e in range(2):
                            nc.vector.tensor_copy(dst[:, 2 * e:2 * e + 2, :],
                                                  self.bank(j, e).rearrange("p (t n) -> p t n", t=2)).then_inc(self.freed(S, j), 1)
                    nc.vector.drain()
                    ve.wait_ge(S.sig, 2)
                    nc.vector.tensor_tensor(z[:, :, PAD:], val[:], sig[:], ALU.mult)

                @block.gpsimd
                def _(pool):
                    self.norm_gpsimd(pool, S)

            with self.stage("diag conv_pe pool_in pool_mm pool_out mean_mm centred var_mm c_var c_rstd c_diag c_spread zn conv_out sq") as (block, S):
                W = 16 + SEQ
                s2 = self.sb("sum2", [P, 4, W], ctx=ctx)
                s4 = self.sb("sum4", [P, 4, W], ctx=ctx)
                diff = self.sb("pool_diff", [P, 4, SEQ], ctx=ctx)
                conv = self.sb("conv_out", [P, 4, SEQ], ctx=ctx)
                NDIAG = 8
                diag = self.sb("tap_diag", [P, NDIAG, P], ctx=ctx)
                row = self.sb("chan_rows", [P, SEQ], ctx=ctx)
                sq = sig
                taps = self.col("conv_w_2").rearrange("p (j c) -> p j c", c=4)
                bias = self.col("conv_b_2")

                @block.scalar
                def _(act):
                    n = 0
                    for c in (2, 3):
                        for j in range(KERN):
                            if n >= NDIAG:
                                act.wait_ge(S.conv_pe, n - NDIAG + 1)
                            nc.scalar.activation(diag[:, n % NDIAG, :], self.ident, ACT.Copy, scale=taps[:, j, c:c + 1]).then_inc(S.diag, 1)
                            n += 1
                        act.wait_ge(S.conv_pe, n)
                        nc.scalar.activation(conv[:, c, :], self.PS[:, c - 2, 0:SEQ], ACT.Identity, bias=bias[:, c:c + 1]).then_inc(S.conv_out, 1)
                    g, b = self.col("conv_ln_g_2"), self.col("conv_ln_b_2")
                    act.wait_ge(S.zn, 1)
                    for c in range(4):
                        nc.scalar.activation(YT[:, 4 + c, :], conv[:, c, :], ACT.Silu, bias=b[:, c:c + 1], scale=g[:, c:c + 1])

                @block.tensor
                def _(pe):
                    pe.wait_ge(side, 16)
                    pe.wait_ge(S.pool_in, 1)
                    for g in range(4):
                        ins = nc.tensor.matmul(self.PS[:, 2 + g // 2, (g % 2) * SEQ:(g % 2 + 1) * SEQ], pw[:, g, :], diff[:, g, :],
                                               start=True, stop=True)
                    ins.then_inc(S.pool_mm, 1)
                    n = 0
                    for c in (2, 3):
                        for j in range(KERN):
                            pe.wait_ge(S.diag, n + 1)
                            nc.tensor.matmul(self.PS[:, c - 2, 0:SEQ], diag[:, n % NDIAG, :], z[:, c, j:j + SEQ],
                                             start=(j == 0), stop=(j == KERN - 1)).then_inc(S.conv_pe, 1)
                            n += 1
                    pe.wait_ge(S.conv_out, 4)
                    for c in range(4):
                        ins = nc.tensor.matmul(self.PS[:, 4, 0:SEQ], self.ones, conv[:, c, :], start=(c == 0), stop=(c == 3))
                    ins.then_inc(S.mean_mm, 1)
                    pe.wait_ge(S.sq, 1)
                    for b in range(NB):
                        for c in range(4):
                            ins = nc.tensor.matmul(self.PS[:, 5, b:b + 1], sq[:, c, b * P:(b + 1) * P], self.ones[:, 0:1],
                                                   start=(c == 0), stop=(c == 3))
                    ins.then_inc(S.var_mm, 1)
                    pe.wait_ge(S.c_diag, 1)
                    for b in range(NB):
                        ins = nc.tensor.matmul(self.PS[:, 6, b * P:(b + 1) * P], self.ones, diag[:, b, :], start=True, stop=True)
                    ins.then_inc(S.c_spread, 1)

                @block.vector
                def _(ve):
                    nc.vector.tensor_tensor(s2[:, :, 1:W], u[:, :, 1:W], u[:, :, 0:W - 1], ALU.add)
                    nc.vector.drain()
                    nc.vector.tensor_tensor(s4[:, 1:4, 4:W], s2[:, 1:4, 4:W], s2[:, 1:4, 2:W - 2], ALU.add)
                    nc.vector.drain()
                    nc.vector.tensor_tensor(s2[:, 2:4, 8:W], s4[:, 2:4, 8:W], s4[:, 2:4, 4:W - 4], ALU.add)
                    nc.vector.drain()
                    nc.vector.tensor_tensor(s4[:, 3, 16:W], s2[:, 3, 16:W], s2[:, 3, 8:W - 8], ALU.add)
                    nc.vector.drain()
                    inv = self.invcount.rearrange("p (g n) -> p g n", g=4)
                    for g, s in enumerate((s2, s4, s2, s4)):
                        nc.vector.tensor_tensor(s[:, g, 16:32], s[:, g, 16:32], inv[:, g, :], ALU.mult)
                        nc.vector.tensor_scalar(s[:, g, 32:W], s[:, g, 32:W], 1.0 / 2 ** (g + 1), None, ALU.mult)
                    nc.vector.drain()
                    for g, s in enumerate((s2, s4, s2, s4)):
                        ins = nc.vector.tensor_tensor(diff[:, g, :], s[:, g, 16:W], u[:, g, 16:W], ALU.subtract)
                    ins.then_inc(S.pool_in, 1)
                    for j in range(KERN):
                        for c in range(2):
                            if j == 0:
                                nc.vector.tensor_scalar(conv[:, c, :], z[:, c, 0:SEQ], taps[:, 0, c:c + 1], bias[:, c:c + 1], ALU.mult, ALU.add)
                            else:
                                nc.vector.scalar_tensor_tensor(conv[:, c, :], z[:, c, j:j + SEQ], taps[:, j, c:c + 1], conv[:, c, :],
                                                               ALU.mult, ALU.add)
                        nc.vector.drain()
                    nc.vector.drain().then_inc(S.conv_out, 2)
                    ve.wait_ge(S.pool_mm, 1)
                    scale = self.col("pool_scale_2")
                    for g in range(4):
                        nc.vector.tensor_scalar(YT[:, g, :], self.PS[:, 2 + g // 2, (g % 2) * SEQ:(g % 2 + 1) * SEQ],
                                                scale[:, g:g + 1], None, ALU.mult)
                    ve.wait_ge(S.mean_mm, 1)
                    nc.vector.tensor_scalar(row[:], self.PS[:, 4, 0:SEQ], 1.0 / HALF, None, ALU.mult)
                    nc.vector.drain()
                    nc.vector.tensor_tensor(conv[:], conv[:], row[:].unsqueeze(1).to_broadcast([P, 4, SEQ]), ALU.subtract)
                    nc.vector.drain()
                    nc.vector.tensor_tensor(sq[:], conv[:], conv[:], ALU.mult).then_inc(S.sq, 1)
                    ve.wait_ge(S.var_mm, 1)
                    nc.vector.tensor_scalar(self.ms[:], self.PS[:, 5, 0:NB], 1.0 / HALF, EPS, ALU.mult, ALU.add).then_inc(S.c_var, 1)
                    ve.wait_ge(S.c_rstd, 1)
                    for b in range(NB):
                        ins = nc.vector.tensor_scalar(diag[:, b, :], self.ident, self.rstd[:, b:b + 1], None, ALU.mult)
                    ins.then_inc(S.c_diag, 1)
                    ve.wait_ge(S.c_spread, 1)
                    nc.vector.tensor_tensor(conv[:], conv[:], self.PS[:, 6, 0:SEQ].unsqueeze(1).to_broadcast([P, 4, SEQ]), ALU.mult).then_inc(S.zn, 1)

                @block.gpsimd
                def _(pool):
                    pool.wait_ge(S.c_var, 1)
                    nc.gpsimd.tensor_tensor(self.rstd[:], self.ms[:], self.neghalf[:, 0:NB], ALU.pow).then_inc(S.c_rstd, 1)

            self.output_projection("ab_out", YT)

    def output_projection(self, name, YT):
        with self.stage("p_free0 p_free1", name) as (block, S):
            @block.tensor
            def _(pe):
                self.project(pe, S, [("T", 512)] * 2, YT, KT)

            @block.vector
            def _(ve):
                self.plain_residual(ve, S)

    def attention(self, block, S, ctx, heads, dh, QT, KT_, V, mask, bias, YT):
        nc = self.nc
        W3 = 3 * P
        lg = self.sb("att_logits", [P, 2, W3], ctx=ctx)
        nmax = self.sb("att_negmax", [P, 2, NB], ctx=ctx)
        sums = self.sb("att_sums", [P, 2, NB], ctx=ctx)
        rsum = self.sb("att_rsums", [P, 2, NB], ctx=ctx)
        pT = self.sb("att_probsT", [P, 2, W3], ctx=ctx)
        per = P // dh

        def rows(h):
            return slice(dh * (h % per), dh * (h % per) + dh)

        @block.tensor
        def _(pe):
            def scores(h):
                L, r, t = self.PS[:, h % 2, :], rows(h), h // per
                if h >= 2:
                    pe.wait_ge(S.a_masked, h - 1)
                nc.tensor.matmul(L[:, 0:P], QT[r, t, 0:P], KT_[r, t, 0:P], start=True, stop=(bias is None), skip_group_check=True)
                ins = nc.tensor.matmul(L[:, P:W3], QT[r, t, P:SEQ], KT_[r, t, :], start=False, stop=(bias is None), skip_group_check=True)
                if bias is not None:
                    nc.tensor.matmul(L[:, 0:P], self.anti, bias[:, h, P:SEQ], start=False, stop=True, skip_group_check=True)
                    ins = nc.tensor.matmul(L[:, P:W3], self.anti, bias[:, h, :], start=False, stop=True, skip_group_check=True)
                ins.then_inc(S.a_scores, 1)

            def turn(h):
                pe.wait_ge(S.a_norm, h + 1)
                if h >= 2:
                    pe.wait_ge(S.a_turned, h - 1)
                T, p = self.PS[:, 2 + h % 2, :], lg[:, h % 2, :]
                nc.tensor.transpose(T[:, 0:P], p[:, 0:P], self.ident)
                nc.tensor.transpose(T[:, P:SEQ], p[:, P:SEQ], self.ident)
                nc.tensor.transpose(T[:, SEQ:W3], p[:, SEQ:W3], self.ident).then_inc(S.a_turn, 1)

            def values(h):
                pe.wait_ge(S.a_turned, h + 1)
                if h >= 2:
                    pe.wait_ge(S.a_out, h - 1)
                O, c = self.PS[rows(h), 4 + h % 2, 0:SEQ], slice(dh * h, dh * h + dh)
                nc.tensor.matmul(O, V[:, 0, c], pT[:, h % 2, 0:SEQ], start=True, stop=False, skip_group_check=True)
                nc.tensor.matmul(O[:, P:SEQ], V[:, 1, c], pT[:, h % 2, SEQ:W3], start=False, stop=True,
                                 skip_group_check=True).then_inc(S.a_val, 1)

            scores(0)
            for h in range(heads):
                if h + 1 < heads:
                    scores(h + 1)
                if h >= 1:
                    values(h - 1)
                turn(h)
            values(heads - 1)

        @block.vector
        def _(ve):
            def masked(h):
                i = h % 2
                ve.wait_ge(S.a_scores, h + 1)
                if h >= 2:
                    ve.wait_ge(S.a_turn, h - 1)
                nc.vector.tensor_tensor(lg[:, i, :], self.PS[:, i, 0:W3], mask, ALU.add).then_inc(S.a_masked, 1)
                nc.vector.drain()
                nc.vector.tensor_reduce(nmax[:, i, 0:1], lg[:, i, 0:P], AX.X, ALU.max, negate=True)
                nc.vector.tensor_reduce(nmax[:, i, 1:2], lg[:, i, P:W3], AX.X, ALU.max, negate=True)
                nc.vector.drain().then_inc(S.a_max, 1)

            def normalised(h):
                i = h % 2
                ve.wait_ge(S.a_exp, h + 1)
                nc.vector.reciprocal(rsum[:, i, :], sums[:, i, :])
                nc.vector.drain()
                nc.vector.tensor_scalar(lg[:, i, 0:P], lg[:, i, 0:P], rsum[:, i, 0:1], None, ALU.mult)
                nc.vector.tensor_scalar(lg[:, i, P:W3], lg[:, i, P:W3], rsum[:, i, 1:2], None, ALU.mult)
                nc.vector.drain().then_inc(S.a_norm, 1)

            masked(0)
            for h in range(heads):
                if h + 1 < heads:
                    masked(h + 1)
                normalised(h)
                if h >= 1:
                    self.attention_out(ve, S, nc.vector.tensor_copy, h - 1, rows, per, YT)
            self.attention_out(ve, S, nc.vector.tensor_copy, heads - 1, rows, per, YT)

        @block.scalar
        def _(act):
            def turned(h):
                act.wait_ge(S.a_turn, h + 1)
                if h >= 2:
                    act.wait_ge(S.a_val, h - 1)
                nc.scalar.copy(pT[:, h % 2, :], self.PS[:, 2 + h % 2, 0:W3]).then_inc(S.a_turned, 1)

            for h in range(heads):
                i = h % 2
                act.wait_ge(S.a_max, h + 1)
                nc.scalar.activation(lg[:, i, 0:P], lg[:, i, 0:P], ACT.Exp, bias=nmax[:, i, 0:1], accum_out=sums[:, i, 0:1])
                nc.scalar.activation(lg[:, i, P:W3], lg[:, i, P:W3], ACT.Exp, bias=nmax[:, i, 1:2], accum_out=sums[:, i, 1:2])
                nc.scalar.drain().then_inc(S.a_exp, 1)
                if h >= 1:
                    turned(h - 1)
            turned(heads - 1)

    ATT = "a_scores a_masked a_max a_exp a_norm a_turn a_turned a_val a_out"

    def attention_out(self, eng, S, copy, h, rows, per, YT):
        eng.wait_ge(S.a_val, h + 1)
        copy(YT[rows(h), h // per, :], self.PS[rows(h), 4 + h % 2, 0:SEQ]).then_inc(S.a_out, 1)

    def sparse_attention(self):
        nc, a = self.nc, self.a
        W3 = 3 * P
        AH = 16
        with ExitStack() as ctx:
            QT = self.sb("dsa_qT", [P, KT, SEQ], ctx=ctx)
            KT_ = self.sb("dsa_kT", [P, KT, SEQ], ctx=ctx)
            V = self.sb("dsa_v", [P, NB, D], ctx=ctx)
            QI = self.sb("dsa_qiT", [P, 4, SEQ], ctx=ctx)
            KI = self.sb("dsa_kiT", [P, SEQ], ctx=ctx)
            WI = self.sb("dsa_wi", [P, NB, 8], ctx=ctx)
            mask = self.sb("dsa_mask", [P, W3], ctx=ctx)
            B = self.sb("dsa_bias", [P, AH, SEQ], ctx=ctx)
            rb = self.sb("rel_bias", [32, AH], ctx=ctx)
            rbT = self.sb("rel_bias_by_distance", [AH, 384], ctx=ctx)
            scratch = nc.dram_tensor("rel_bias_scratch", [AH, 384], F32, kind="Internal").ap()
            side = nc.alloc_semaphore("dsa_side")
            gain = self.col("mix_norm_2")[:, KT:2 * KT]

            with self.stage("n_ms n_rstd n_xn n_tr n_hT p_free0 p_free1 rb rb_out", "c_in") as (block, S):
                jobs = [("F", 512)] * 4 + [("T", 512)] * 2 + [("F", 512)]

                @block.tensor
                def _(pe):
                    self.norm_tensor(pe, S)
                    pe.wait_ge(S.n_hT, self.N_HT)
                    pe.wait_ge(side, 16)
                    nc.tensor.matmul(self.PS[0:AH, 4, 0:384], rb[:], self.onehot[0:32, :], start=True, stop=True).then_inc(S.rb, 1)
                    self.project(pe, S, jobs, self.hT, KT)
                    for g in range(2):
                        slot = self.take(pe)[:, 0:4 * 136].rearrange("p (k n) -> p k n", k=4)
                        for kk in range(4):
                            k = 4 * g + kk
                            st, sp = k == 0, k == KT - 1
                            nc.tensor.matmul(self.PS[:, 5, 0:SEQ], slot[:, kk, 0:P], self.hT[:, k, :], start=st, stop=sp)
                            for b in range(NB):
                                ins = nc.tensor.matmul(self.PS[:, 6 + b, 0:8], self.hT[:, k, b * P:(b + 1) * P],
                                                       slot[:, kk, P:P + 8], start=st, stop=sp)
                        ins.then_inc(self.w_used, 1)

                @block.scalar
                def _(act):
                    act.dma_start(rb[:], a["rel_bias_2"]).then_inc(side, 16)
                    self.norm_scalar(act, S, gain, None)
                    act.wait_ge(S.rb, 1)
                    nc.scalar.copy(rbT[:], self.PS[0:AH, 4, 0:384]).then_inc(S.rb_out, 1)
                    act.wait_ge(S.rb_out, 1)
                    act.dma_start(scratch, rbT[:]).then_inc(side, 16)
                    act.wait_ge(side, 32)
                    act.dma_start(B[:], bass.AP(scratch.tensor, 0, [[1, P], [384, AH], [1, SEQ]])).then_inc(side, 16)
                    for j in (1, 3, 5):
                        dst = {1: QT[:, 4:8], 3: KT_[:, 4:8], 5: V[:, :, BANK:]}[j]
                        self.leave(act, j)
                        for e in range(2):
                            if j == 5:
                                ins = nc.scalar.copy(dst[:, e, :], self.bank(j, e))
                            else:
                                ins = nc.scalar.mul(dst[:, 2 * e:2 * e + 2, :].rearrange("p t n -> p (t n)"), self.bank(j, e),
                                                    0.125 if j == 1 else 1.0)
                            ins.then_inc(self.freed(S, j), 1)

                @block.vector
                def _(ve):
                    self.norm_vector(ve, S, gain, None)
                    for j in (0, 2, 4, 6):
                        dst = {0: QT[:, 0:4], 2: KT_[:, 0:4], 4: V[:, :, 0:BANK], 6: QI[:]}[j]
                        self.leave(ve, j)
                        for e in range(2):
                            if j == 4:
                                ins = nc.vector.tensor_copy(dst[:, e, :], self.bank(j, e))
                            else:
                                ins = nc.vector.tensor_scalar(dst[:, 2 * e:2 * e + 2, :].rearrange("p t n -> p (t n)"), self.bank(j, e),
                                                              0.125 if j == 0 else 1.0, None, ALU.mult)
                            ins.then_inc(self.freed(S, j), 1)
                    self.leave(ve, 7)
                    nc.vector.tensor_copy(KI[:], self.PS[:, 5, 0:SEQ])
                    nc.vector.tensor_copy(WI[:], self.PS[:, 6:8, 0:8])

                @block.gpsimd
                def _(pool):
                    self.norm_gpsimd(pool, S)

            with self.stage("index relu used") as (block, S):
                rel = self.sb("dsa_rel", [P, 2, W3], ctx=ctx)
                sc = self.sb("dsa_scores", [P, W3], ctx=ctx)
                top = self.sb("dsa_top", [P, NB, 8], ctx=ctx)

                @block.tensor
                def _(pe):
                    for h in range(8):
                        r, t, L = slice(64 * (h % 2), 64 * (h % 2) + 64), h // 2, self.PS[:, h % 4, :]
                        if h >= 4:
                            pe.wait_ge(S.relu, h - 3)
                        nc.tensor.matmul(L[:, 0:P], QI[r, t, 0:P], KI[r, 0:P], start=True, stop=True)
                        nc.tensor.matmul(L[:, P:W3], QI[r, t, P:SEQ], KI[r, :], start=True, stop=True).then_inc(S.index, 1)

                @block.scalar
                def _(act):
                    for h in range(8):
                        act.wait_ge(S.index, h + 1)
                        if h >= 2:
                            act.wait_ge(S.used, h - 1)
                        nc.scalar.activation(rel[:, h % 2, :], self.PS[:, h % 4, 0:W3], ACT.Relu).then_inc(S.relu, 1)

                @block.vector
                def _(ve):
                    parts = ((0, slice(0, P)), (1, slice(P, W3)))
                    for h in range(8):
                        ve.wait_ge(S.relu, h + 1)
                        for b, c in parts:
                            if h == 0:
                                nc.vector.tensor_scalar(sc[:, c], rel[:, 0, c], WI[:, b, 0:1], None, ALU.mult)
                            else:
                                nc.vector.scalar_tensor_tensor(sc[:, c], rel[:, h % 2, c], WI[:, b, h:h + 1], sc[:, c], ALU.mult, ALU.add)
                        nc.vector.drain().then_inc(S.used, 1)
                    nc.vector.scalar_tensor_tensor(sc[:], sc[:], float(512 ** -0.5), self.causal3_add, ALU.mult, ALU.add)
                    nc.vector.drain()
                    for _ in range(DSA_TOPK // 8):
                        for b, c in parts:
                            nc.vector.max(top[:, b, :], sc[:, c])
                        nc.vector.drain()
                        for b, c in parts:
                            nc.vector.match_replace(sc[:, c], top[:, b, :], sc[:, c], TAKEN)
                        nc.vector.drain()
                    nc.vector.tensor_scalar(mask[:], sc[:], 0.5 * TAKEN, None, ALU.is_le)
                    nc.vector.drain()
                    nc.vector.tensor_scalar(mask[:], mask[:], 1.0, -NEG, ALU.subtract, ALU.mult)
                    nc.vector.drain()
                    nc.vector.tensor_tensor(mask[:], mask[:], self.causal3_add, ALU.add)

            YT = self.sb("dsa_yT", [P, KT, SEQ], ctx=ctx)
            with self.stage(self.ATT) as (block, S):
                @block.tensor
                def _(pe):
                    pe.wait_ge(side, 48)

                self.attention(block, S, ctx, AH, 64, QT, KT_, V, mask[:], B, YT)
            self.output_projection("c_out", YT)

    def turn_plain(self, pe, S, src):
        for b in range(NB):
            for g in range(2):
                for j in range(4):
                    k = 4 * g + j
                    ins = self.nc.tensor.transpose(self.PS[:, 4 + 2 * b + g, j * P:(j + 1) * P],
                                                   src[:, b, k * P:(k + 1) * P], self.ident)
                ins.then_inc(S.n_tr, 1)

    def hybrid(self):
        nc = self.nc
        with ExitStack() as ctx:
            YS = self.sb("ssm_branch", [P, NB, D], ctx=ctx)
            with ExitStack() as inner:
                self.mamba(inner, YS)
            with ExitStack() as inner:
                self.moba(inner, YS)

    def mamba(self, ctx, YS):
        nc, a = self.nc, self.a
        XS = self.sb("ssm_x", [P, NB, SSM_D], ctx=ctx)
        with ExitStack() as scan:
            CO = self.sb("ssm_conv", [P, 32, SEQ], ctx=scan)
            DT = self.sb("ssm_dt", [P, NB, SSM_H], ctx=scan)
            DA = self.sb("ssm_da", [P, NB, SSM_H], ctx=scan)
            rows = self.sb("ssm_rows", [P, 3, SSM_H], ctx=scan)
            side = nc.alloc_semaphore("ssm_rows_landed")

            with ExitStack() as inner, self.stage("n_tr n_hT p_free0 p_free1 raw conv dt1 dt2 dt3 aexp", "ssm_in") as (block, S):
                XB = self.sb("ssm_raw", [P, 2, 4, 3 + SEQ], ctx=inner)
                dta = self.sb("ssm_dt_abs", [P, NB, SSM_H], ctx=inner)
                ea = self.sb("ssm_ea", [P, SSM_H], ctx=inner)
                taps = self.col("conv_w_3").rearrange("p (j c) -> p j c", c=32)
                bias = self.col("conv_b_3")

                @block.tensor
                def _(pe):
                    self.turn_plain(pe, S, self.X)
                    pe.wait_ge(S.n_hT, self.N_HT)
                    self.project(pe, S, [("F", 512)] * 8 + [("T", SSM_H)], self.hT, KT)

                @block.scalar
                def _(act):
                    for i, name in enumerate(("dt_bias_3", "a_log_3", "d_skip_3")):
                        act.dma_start(rows[:, i, :], a[name].partition_broadcast(P)).then_inc(side, 16)
                    self.copy_tiles(act, nc.scalar.copy, S, 0)

                    def silu(j):
                        act.wait_ge(S.conv, j + 1)
                        c = CO[:, 4 * j:4 * j + 4, :]
                        nc.scalar.activation(c, c, ACT.Silu)

                    for j in range(8):
                        self.leave(act, j)
                        if j >= 2:
                            act.wait_ge(S.conv, j - 1)
                        for e in range(2):
                            nc.scalar.copy(XB[:, j % 2, 2 * e:2 * e + 2, 3:], self.bank(j, e).rearrange("p (t n) -> p t n", t=2)
                                           ).then_inc(self.freed(S, j), 1)
                        nc.scalar.drain().then_inc(S.raw, 1)
                        if j >= 1:
                            silu(j - 1)
                    silu(7)
                    act.wait_ge(S.dt1, 1)
                    nc.scalar.activation(dta[:], DT[:], ACT.Abs)
                    nc.scalar.drain()
                    nc.scalar.activation(dta[:], dta[:], ACT.Exp, scale=-1.0)
                    nc.scalar.drain()
                    nc.scalar.activation(dta[:], dta[:], ACT.Ln, bias=1.0).then_inc(S.dt2, 1)
                    act.wait_ge(side, 48)
                    nc.scalar.activation(ea[:], rows[:, 1, :], ACT.Exp).then_inc(S.aexp, 1)

                @block.vector
                def _(ve):
                    nc.vector.memset(XB[:, :, :, 0:3], 0.0)
                    self.copy_tiles(ve, nc.vector.tensor_copy, S, 1)
                    nc.vector.drain()
                    for j in range(8):
                        ve.wait_ge(S.raw, j + 1)
                        for tap in range(4):
                            for t in range(4):
                                c = 4 * j + t
                                src = XB[:, j % 2, t, tap:tap + SEQ]
                                if tap == 0:
                                    nc.vector.tensor_scalar(CO[:, c, :], src, taps[:, 0, c:c + 1], bias[:, c:c + 1], ALU.mult, ALU.add)
                                else:
                                    nc.vector.scalar_tensor_tensor(CO[:, c, :], src, taps[:, tap, c:c + 1], CO[:, c, :], ALU.mult, ALU.add)
                            ins = nc.vector.drain()
                        ins.then_inc(S.conv, 1)
                    self.leave(ve, 8)
                    ve.wait_ge(side, 48)
                    for b in range(NB):
                        nc.vector.tensor_tensor(DT[:, b, :], self.PS[:, b, 0:SSM_H], rows[:, 0, :], ALU.add)
                    nc.vector.drain().then_inc(S.dt1, 1)
                    ve.wait_ge(S.dt2, 1)
                    nc.vector.scalar_tensor_tensor(DT[:], DT[:], 0.0, dta[:], ALU.max, ALU.add)
                    nc.vector.drain()
                    ve.wait_ge(S.aexp, 1)
                    for b in range(NB):
                        nc.vector.scalar_tensor_tensor(DA[:, b, :], DT[:, b, :], -1.0, ea[:], ALU.mult, ALU.mult)

            XD = self.sb("ssm_xdt", [P, NB, SSM_D], ctx=scan)
            heads = lambda t: t.rearrange("p (h c) -> p h c", c=SSM_P)
            wide = [P, SSM_H, SSM_P]
            BTK = self.sb("ssm_B_tok", [P, SSM_G, P], ctx=scan)
            with self.stage("x_turned x_out b_turned done") as (block, S):
                @block.tensor
                def _(pe):
                    for b in range(NB):
                        for g in range(4):
                            for j in range(4):
                                ins = nc.tensor.transpose(self.PS[:, 4 * b + g, j * P:(j + 1) * P],
                                                          CO[:, 4 * g + j, b * P:(b + 1) * P], self.ident)
                        ins.then_inc(S.x_turned, 1)
                    pe.wait_ge(S.x_out, 1)
                    for g in range(SSM_G):
                        ins = nc.tensor.transpose(self.PS[:, g // 4, (g % 4) * P:(g % 4 + 1) * P], CO[:, 16 + g, 0:P], self.ident)
                    ins.then_inc(S.b_turned, 1)

                @block.scalar
                def _(act):
                    act.wait_ge(S.x_turned, 1)
                    nc.scalar.copy(XS[:, 0, :].rearrange("p (g n) -> p g n", g=4), self.PS[:, 0:4, :]).then_inc(S.x_out, 1)
                    act.wait_ge(S.b_turned, 1)
                    nc.scalar.copy(BTK[:].rearrange("p (g i) n -> p g (i n)", g=2), self.PS[:, 0:2, :])

                @block.vector
                def _(ve):
                    ve.wait_ge(S.x_turned, 2)
                    nc.vector.tensor_copy(XS[:, 1, :].rearrange("p (g n) -> p g n", g=4), self.PS[:, 4:8, :])
                    nc.vector.drain()
                    ve.wait_ge(S.x_out, 1)
                    for b in range(NB):
                        nc.vector.tensor_tensor(heads(XD[:, b, :]), heads(XS[:, b, :]), DT[:, b, :].unsqueeze(2).to_broadcast(wide), ALU.mult)
                    nc.vector.drain()
                    for b in range(NB):
                        nc.vector.tensor_tensor(heads(XS[:, b, :]), heads(XS[:, b, :]), rows[:, 2, :].unsqueeze(2).to_broadcast(wide), ALU.mult)

            with ExitStack() as inner, self.stage(
                    "cums cum_exp decayed states states_out0 states_out cb cbm lhs seg segx m y y_out") as (block, S):
                ecum = self.sb("ssm_exp_cum", [P, 2, SSM_H], ctx=inner)
                XDD = self.sb("ssm_xdt_decayed", [P, SSM_D], ctx=inner)
                ST = self.sb("ssm_state", [P, SSM_G, SSM_R * SSM_P], ctx=inner)
                cbm = self.sb("ssm_cb", [P, 2, P], ctx=inner)
                lhs = self.sb("ssm_seg_lhs", [P, 2, SSM_R, P], ctx=inner)
                ex = self.sb("ssm_seg_exp", [P, 2, SSM_R, P], ctx=inner)
                inter = self.sb("ssm_inter", [P, SSM_R * SSM_P], ctx=inner)
                W = SSM_R * SSM_P
                work = [(c, g) for c in range(NB) for g in range(SSM_G)]

                @block.gpsimd
                def _(pool):
                    for n, (c, g) in enumerate(work):
                        if n >= 2:
                            pool.wait_ge(S.seg, n - 1)
                        for r in range(SSM_R):
                            h = SSM_R * g + r
                            ins = nc.gpsimd.tensor_scalar(lhs[:, n % 2, r, :], self.after, DA[:, c, h:h + 1], None, ALU.mult)
                        ins.then_inc(S.lhs, 1)

                @block.tensor
                def _(pe):
                    nc.tensor.matmul(self.PS[:, 6, 0:SSM_H], self.after, DA[:, 0, :], start=True, stop=True)
                    nc.tensor.matmul(self.PS[:, 6, SSM_H:2 * SSM_H], self.upto, DA[:, 1, :], start=True, stop=True).then_inc(S.cums, 1)

                    def first(n):
                        c, g = work[n]
                        t = slice(c * P, (c + 1) * P)
                        if n >= 2:
                            pe.wait_ge(S.cbm, n - 1)
                            pe.wait_ge(S.segx, n - 1)
                        nc.tensor.matmul(self.PS[:, n % 2, 0:P], CO[:, 16 + g, t], CO[:, 24 + g, t], start=True, stop=True).then_inc(S.cb, 1)
                        pe.wait_ge(S.lhs, n + 1)
                        for r in range(SSM_R):
                            ins = nc.tensor.matmul(self.PS[:, 2 + n % 2, r * P:(r + 1) * P], lhs[:, n % 2, r, :], self.upto,
                                                   start=True, stop=True)
                        ins.then_inc(S.seg, 1)

                    def second(n):
                        c, g = work[n]
                        pe.wait_ge(S.m, n + 1)
                        if n >= 2:
                            pe.wait_ge(S.y_out, n - 1)
                        if n == SSM_G:
                            pe.wait_ge(S.states_out, 1)
                        Yb = self.PS[:, 4 + n % 2, :]
                        for r in range(SSM_R):
                            q = (SSM_R * g + r) * SSM_P
                            ins = nc.tensor.matmul(Yb[:, r * SSM_P:(r + 1) * SSM_P], ex[:, n % 2, r, :], XD[:, c, q:q + SSM_P],
                                                   start=True, stop=True)
                        if c == 1:
                            ins = nc.tensor.matmul(Yb[:, W:2 * W], CO[:, 24 + g, P:SEQ], ST[:, g, :], start=True, stop=True)
                        ins.then_inc(S.y, 1)

                    first(0)
                    for n in range(len(work)):
                        if n + 1 < len(work):
                            first(n + 1)
                        second(n)
                        if n < SSM_G:
                            if n == 0:
                                pe.wait_ge(S.decayed, 1)
                            if n >= 2:
                                pe.wait_ge(S.states_out0, n - 1)
                            nc.tensor.matmul(self.PS[:, 6 + n % 2, 0:W], BTK[:, n, :], XDD[:, n * W:(n + 1) * W], start=True,
                                             stop=True).then_inc(S.states, 1)

                @block.scalar
                def _(act):
                    act.wait_ge(S.cums, 1)
                    nc.scalar.activation(ecum[:].rearrange("p i h -> p (i h)"), self.PS[:, 6, 0:2 * SSM_H], ACT.Exp).then_inc(S.cum_exp, 1)
                    for n in range(len(work)):
                        act.wait_ge(S.seg, n + 1)
                        if n >= 2:
                            act.wait_ge(S.y, n - 1)
                        nc.scalar.activation(ex[:, n % 2].rearrange("p r n -> p (r n)"), self.PS[:, 2 + n % 2, :], ACT.Exp).then_inc(S.segx, 1)
                        if n < SSM_G:
                            act.wait_ge(S.states, n + 1)
                            ins = nc.scalar.copy(ST[:, n, :], self.PS[:, 6 + n % 2, 0:W]).then_inc(S.states_out0, 1)
                            if n == SSM_G - 1:
                                nc.scalar.drain().then_inc(S.states_out, 1)

                @block.vector
                def _(ve):
                    ve.wait_ge(S.cum_exp, 1)
                    nc.vector.tensor_tensor(heads(XDD[:]), heads(XD[:, 0, :]), ecum[:, 0, :].unsqueeze(2).to_broadcast(wide), ALU.mult
                                            ).then_inc(S.decayed, 1)

                    def weights(n):
                        ve.wait_ge(S.cb, n + 1)
                        nc.vector.tensor_tensor(cbm[:, n % 2, :], self.PS[:, n % 2, 0:P], self.upto, ALU.mult).then_inc(S.cbm, 1)
                        nc.vector.drain()
                        ve.wait_ge(S.segx, n + 1)
                        nc.vector.tensor_tensor(ex[:, n % 2], ex[:, n % 2], cbm[:, n % 2, :].unsqueeze(1).to_broadcast([P, SSM_R, P]),
                                                ALU.mult).then_inc(S.m, 1)

                    def collect(n):
                        c, g = work[n]
                        ve.wait_ge(S.y, n + 1)
                        out = XS[:, c, g * W:(g + 1) * W]
                        Yb = self.PS[:, 4 + n % 2, :]
                        if c == 1:
                            h4 = ecum[:, 1, SSM_R * g:SSM_R * (g + 1)].unsqueeze(2).to_broadcast([P, SSM_R, SSM_P])
                            nc.vector.tensor_tensor(heads(inter[:]), heads(Yb[:, W:2 * W]), h4, ALU.mult)
                        nc.vector.tensor_tensor(out, out, Yb[:, 0:W], ALU.add).then_inc(S.y_out, 1)
                        if c == 1:
                            nc.vector.drain()
                            nc.vector.tensor_tensor(out, out, inter[:], ALU.add)
                            nc.vector.drain()

                    weights(0)
                    for n in range(len(work)):
                        if n + 1 < len(work):
                            weights(n + 1)
                        collect(n)

        YT = self.sb("ssm_yT", [P, 16, SEQ], ctx=ctx)
        with ExitStack() as inner, self.stage("p_free0 p_free1 z z_used g_ms g_rstd g_y turned0 turned1 out0 out1", "ssm_z") as (block, S):
            Z = self.sb("ssm_silu_z", [P, 2, NB, BANK], ctx=inner)
            gms = self.sb("ssm_group_ms", [P, NB * SSM_G], ctx=inner)
            grs = self.sb("ssm_group_rstd", [P, NB * SSM_G], ctx=inner)
            junk = self.sb("junk", [P, 256], ctx=inner)
            w = self.col("ssm_norm_w_3")
            groups = XS[:].rearrange("p b (g n) -> p (b g) n", g=SSM_G)

            @block.tensor
            def _(pe):
                self.project(pe, S, [("T", 512)] * 4, self.hT, KT)
                pe.wait_ge(S.g_y, 1)
                for i in range(8):
                    b, g = i // 4, i % 4
                    for j in range(4):
                        k = 4 * g + j
                        ins = nc.tensor.transpose(self.PS[:, 4 + i % 4, j * P:(j + 1) * P], XS[:, b, k * P:(k + 1) * P], self.ident)
                    ins.then_inc((S.turned0, S.turned1)[i % 2], 1)
                    if i == 3:
                        pe.wait_ge(S.out0, 2)
                        pe.wait_ge(S.out1, 2)

            def turned(eng, ops, odd):
                for i in range(odd, 8, 2):
                    b, g = i // 4, i % 4
                    eng.wait_ge((S.turned0, S.turned1)[odd], i // 2 + 1)
                    for j in range(4):
                        k = 4 * g + j
                        out, src = YT[:, k, b * P:(b + 1) * P], self.PS[:, 4 + i % 4, j * P:(j + 1) * P]
                        if odd:
                            ins = ops.tensor_scalar(out, src, w[:, k:k + 1], None, ALU.mult)
                        else:
                            ins = ops.activation(out, src, ACT.Copy, scale=w[:, k:k + 1])
                    ins.then_inc((S.out0, S.out1)[odd], 1)

            @block.scalar
            def _(act):
                for j in range(4):
                    self.leave(act, j)
                    if j >= 2:
                        act.wait_ge(S.z_used, j - 1)
                    for e in range(2):
                        nc.scalar.activation(Z[:, j % 2, e, :], self.bank(j, e), ACT.Silu).then_inc(self.freed(S, j), 1)
                    nc.scalar.drain().then_inc(S.z, 1)
                turned(act, nc.scalar, 0)

            @block.vector
            def _(ve):
                for j in range(4):
                    ve.wait_ge(S.z, j + 1)
                    c = slice(j * BANK, (j + 1) * BANK)
                    nc.vector.tensor_tensor(XS[:, :, c], XS[:, :, c], Z[:, j % 2], ALU.mult).then_inc(S.z_used, 1)
                nc.vector.drain()
                for i in range(NB * SSM_G):
                    nc.vector.tensor_tensor_reduce(self.xn[:].rearrange("p b (g n) -> p (b g) n", n=256)[:, i % 8, :] if i < 8 else
                                                   YT[:, i - 8, :], groups[:, i, :], groups[:, i, :], 1.0 / 256,
                                                   LN_EPS, ALU.mult, ALU.add, gms[:, i:i + 1])
                nc.vector.drain().then_inc(S.g_ms, 1)
                ve.wait_ge(S.g_rstd, 1)
                nc.vector.tensor_tensor(groups, groups, grs[:].unsqueeze(2).to_broadcast([P, NB * SSM_G, 256]), ALU.mult).then_inc(S.g_y, 1)
                turned(ve, nc.vector, 1)

            @block.gpsimd
            def _(pool):
                pool.wait_ge(S.g_ms, 1)
                nc.gpsimd.tensor_tensor(grs[:], gms[:], self.neghalf[:, 0:NB * SSM_G], ALU.pow).then_inc(S.g_rstd, 1)

        with self.stage("p_free0 p_free1", "ssm_out") as (block, S):
            @block.tensor
            def _(pe):
                self.project(pe, S, [("T", 512)] * 2, YT, 16)

            @block.scalar
            def _(act):
                for j in range(2):
                    self.leave(act, j, per=4)
                    for e in range(2):
                        nc.scalar.copy(YS[:, e, j * BANK:(j + 1) * BANK], self.bank(j, e)).then_inc(self.freed(S, j), 1)

    def moba(self, ctx, YS):
        nc, a = self.nc, self.a
        AH = 8
        QT = self.sb("moba_qT", [P, KT, SEQ], ctx=ctx)
        KT_ = self.sb("moba_kT", [P, KT, SEQ], ctx=ctx)
        V = self.sb("moba_v", [P, NB, D], ctx=ctx)
        YT = self.sb("moba_yT", [P, KT, SEQ], ctx=ctx)
        YA = self.sb("moba_branch", [P, NB, D], ctx=ctx)
        bg = self.sb("b_gate", [P, 2 * D], ctx=ctx)
        lnp = self.sb("ln2_params", [P, 2, D], ctx=ctx)
        side = nc.alloc_semaphore("moba_side")
        scale = 1.0 / math.sqrt(P)

        with self.stage("p_free0 p_free1", "att_in") as (block, S):
            @block.tensor
            def _(pe):
                self.project(pe, S, [("F", 512)] * 4 + [("T", 512)] * 2, self.hT, KT)

            @block.scalar
            def _(act):
                act.dma_start(bg[:], a["b_gate_3"].partition_broadcast(P)).then_inc(side, 16)
                act.dma_start(lnp[:, 0, :], a["ln2_g_3"].partition_broadcast(P)).then_inc(side, 16)
                act.dma_start(lnp[:, 1, :], a["ln2_b_3"].partition_broadcast(P)).then_inc(side, 16)
                for j in (1, 3, 5):
                    self.leave(act, j)
                    for e in range(2):
                        if j == 5:
                            ins = nc.scalar.copy(V[:, e, BANK:], self.bank(j, e))
                        else:
                            dst = (QT if j == 1 else KT_)[:, 4 + 2 * e:6 + 2 * e, :].rearrange("p t n -> p (t n)")
                            ins = nc.scalar.mul(dst, self.bank(j, e), scale if j == 1 else 1.0)
                        ins.then_inc(self.freed(S, j), 1)

            @block.vector
            def _(ve):
                for j in (0, 2, 4):
                    self.leave(ve, j)
                    for e in range(2):
                        if j == 4:
                            ins = nc.vector.tensor_copy(V[:, e, 0:BANK], self.bank(j, e))
                        else:
                            dst = (QT if j == 0 else KT_)[:, 2 * e:2 * e + 2, :].rearrange("p t n -> p (t n)")
                            ins = nc.vector.tensor_scalar(dst, self.bank(j, e), scale if j == 0 else 1.0, None, ALU.mult)
                        ins.then_inc(self.freed(S, j), 1)

        with self.stage(self.ATT) as (block, S):
            self.attention(block, S, ctx, AH, P, QT, KT_, V, self.causal3_add, None, YT)

        with self.stage("p_free0 p_free1 pre sig mixed", "att_out") as (block, S):
            pre = self.sb("gate_pre", [P, 2, NB, BANK], ctx=ctx)

            @block.tensor
            def _(pe):
                self.project(pe, S, [("T", 512)] * 2, YT, KT)
                self.project(pe, S, [("T", 512)] * 4, self.hT, KT, first=2)

            @block.scalar
            def _(act):
                for j in range(2):
                    self.leave(act, j)
                    for e in range(2):
                        nc.scalar.copy(YA[:, e, j * BANK:(j + 1) * BANK], self.bank(j, e)).then_inc(self.freed(S, j), 1)
                nc.scalar.drain()
                for i in range(4):
                    act.wait_ge(S.pre, i + 1)
                    nc.scalar.activation(pre[:, i % 2], pre[:, i % 2], ACT.Sigmoid).then_inc(S.sig, 1)

            @block.vector
            def _(ve):
                ve.wait_ge(side, 48)
                for i in range(4):
                    j = i + 2
                    self.leave(ve, j)
                    for e in range(2):
                        nc.vector.tensor_tensor(pre[:, i % 2, e, :], self.bank(j, e), bg[:, i * BANK:(i + 1) * BANK],
                                                ALU.add).then_inc(self.freed(S, j), 1)
                    nc.vector.drain().then_inc(S.pre, 1)
                    ve.wait_ge(S.sig, i + 1)
                    branch = (YS if i < 2 else YA)[:, :, (i % 2) * BANK:(i % 2 + 1) * BANK]
                    nc.vector.tensor_tensor(branch, branch, pre[:, i % 2], ALU.mult)
                    nc.vector.drain()
                nc.vector.tensor_tensor(YA[:], YA[:], YS[:], ALU.add)

        with self.stage("n_tr n_hT p_free0 p_free1 l_ms l_rstd", "mix3_out") as (block, S):
            @block.tensor
            def _(pe):
                self.turn_plain(pe, S, YA)
                pe.wait_ge(S.n_hT, self.N_HT)
                self.project(pe, S, [("T", 512)] * 2, self.hT, KT)

            @block.scalar
            def _(act):
                self.copy_tiles(act, nc.scalar.copy, S, 0)

            @block.vector
            def _(ve):
                for b in range(NB):
                    nc.vector.tensor_scalar(self.X[:, b, :], self.X[:, b, :], ALPHA, None, ALU.mult)
                self.copy_tiles(ve, nc.vector.tensor_copy, S, 1)
                nc.vector.drain()
                self.plain_residual(ve, S)
                nc.vector.drain()
                self.layer_norm_vector(ve, S, lnp)

            @block.gpsimd
            def _(pool):
                self.layer_norm_gpsimd(pool, S)

    def build(self, out):
        a = self.a
        with self.ctx:
            self.place()
            self.plan()
            self.load_constants()
            for l in range(2):
                self.ada(l)
                self.mixer(l)
                self.peer(l)
            self.final_norm(a["final_norm"])
            for l in range(2):
                cols = slice(KT * l, KT * (l + 1))
                self.ffn(f"ffn1_{l}", self.col("ffn1_norm_2")[:, cols])
                if l == 0:
                    self.pool_conv()
                else:
                    self.sparse_attention()
                self.ffn(f"ffn2_{l}", self.col("ffn2_norm_2")[:, cols])
            self.final_norm(a["final_norm_2"])
            self.ffn("ffn1_3", layer_norm=(a["ln1_g_3"], a["ln1_b_3"]))
            self.hybrid()
            self.ffn("ffn2_3", layer_norm=(a["ln3_g_3"], a["ln3_b_3"]))
            self.store(out)


def kernel(**inputs):
    import concourse.bacc as bacc
    from concourse.bass_utils import run_bass_kernel_spmd

    nc = bacc.Bacc("TRN2", target_bir_lowering=False, num_devices=1)
    arrays, args = {}, {}
    inputs = {**inputs, "shape_consts": shape_constants()[0]}
    for name, value in inputs.items():
        value = np.ascontiguousarray(value)
        arrays[f"in_{name}_dram"] = value
        args[name] = nc.dram_tensor(f"in_{name}_dram", value.shape, mybir.dt.from_np(value.dtype), kind="ExternalInput").ap()
    out = nc.dram_tensor("out_dram", (1, SEQ, D), F32, kind="ExternalOutput").ap()
    Program(nc, args).build(out)
    return run_bass_kernel_spmd(nc, [arrays], core_ids=[0]).results[0]["out_dram"]
```

```python
from collections import namedtuple
from contextlib import ExitStack, contextmanager
import math

import numpy as np
import concourse.bass as bass
from concourse import mybir

ALU = mybir.AluOpType
ACT = mybir.ActivationFunctionType
AX = mybir.AxisListType
F32 = mybir.dt.float32
F32R = mybir.dt.float32r
I32 = mybir.dt.int32
U32 = mybir.dt.uint32

P = 128
D = 1024
KT = D // P
SEQ = 256
NB = SEQ // P
HALF = D // 2
RING = 6
SLOT = 2048
BANK = 512
DFF = 2816
FF_COLS = 256
FF_STEPS = DFF // FF_COLS
EPS = 1e-6
LN_EPS = 1e-5
NEG = -1e30
TAKEN = -3e38
HEADS = 8
TOPK = 16
SIDE_RING = 6
SIDE_COLS = 1024
SIDE_GROUP = 2
SPLIT = 4
PAIR = 2
GRING = 16
GHALF = GRING // 2
PE_ROWS = 3
VE_ROWS = GHALF - PE_ROWS
PE_CREDIT = 2 * PE_ROWS + 2
VE_CREDIT = GHALF + 1
DSA_TOPK = 64
KERN = 31
ALPHA = 2 ** 0.25
SSM_D = 2048
SSM_G = 8
SSM_R = 4
SSM_H = SSM_G * SSM_R
SSM_P = 64


def shape_constants():
    i = np.arange(P)
    eye = np.eye(P)
    before = i[:, None] < i[None, :]
    upto = i[:, None] <= i[None, :]
    strict3 = np.concatenate([before, np.ones((P, P)), before], 1)
    count = np.minimum(np.arange(SEQ)[None] + 1, np.array([2, 4, 8, 16])[:, None])
    dist = 255 - np.arange(384)
    d = np.maximum(dist, 16).astype(np.float32)
    big = 16 + (np.log(d / np.float32(16)) / np.float32(math.log(8)) * np.float32(16)).astype(np.int32)
    bucket = np.where(dist < 16, dist, np.minimum(big, 31))
    onehot = np.zeros((P, 384))
    for c in range(256):
        onehot[bucket[c], c] = 1.0
    causal = np.where(i[None, :] > i[:, None], NEG, 0.0)
    parts = {
        "ident": eye,
        "anti": eye[::-1],
        "upto": upto,
        "after": i[:, None] > i[None, :],
        "from_": i[:, None] >= i[None, :],
        "ones": np.ones((P, P)),
        "strict3": strict3,
        "strict3_add": np.where(strict3 > 0, 0.0, NEG),
        "causal3_add": np.concatenate([causal, np.zeros((P, P)), causal], 1),
        "iota16": np.tile(np.arange(16), (P, 1)),
        "neghalf": np.full((P, 32), -0.5),
        "invcount": np.tile((1.0 / count[:, :16]).reshape(1, -1), (P, 1)),
        "onehot": onehot,
    }
    at, where = 0, {}
    for name, a in parts.items():
        where[name] = (at, at + a.shape[1])
        at += a.shape[1]
    return np.concatenate([np.asarray(a, np.float32) for a in parts.values()], 1), where


PARAM_GROUPS = [
    [("norm_mix", 16), ("norm_ffn", 16)],
    [("conv_w_3", 128)],
    [("conv_w_2", KERN * 4)],
    [("gm_bs", 16), ("out_norm_a", 8), ("out_norm_b", 8), ("ffn1_norm_2", 16), ("mix_norm_2", 16),
     ("ffn2_norm_2", 16), ("conv_b_2", 4), ("conv_ln_g_2", 4), ("conv_ln_b_2", 4), ("pool_scale_2", 4)],
    [("ssm_norm_w_3", 16), ("conv_b_3", 32), ("c", 8)],
    [("ada_b", 96)],
]


class Program:
    def __init__(self, nc, a):
        self.nc, self.a = nc, a
        self.ctx = ExitStack()
        self.n_stage = 0

    def sb(self, name, shape, dt=F32, ctx=None):
        if ctx is not None:
            name = f"{name}_{self.n_stage}"
        return (ctx or self.ctx).enter_context(self.nc.sbuf_tensor(name, shape, dt))

    def place(self):
        nc = self.nc
        consts, where = shape_constants()
        self.X = self.sb("X", [P, NB, D])
        self.hT = self.sb("hT", [P, KT, SEQ])
        self.ring = self.sb("ring", [P, RING, SLOT])
        self.cst = self.sb("cst", [P, consts.shape[1]])

        def table(name):
            lo, hi = where[name]
            return self.cst[:, lo:hi]
        self.ident = table("ident")
        self.anti = table("anti")
        self.upto = table("upto")
        self.after = table("after")
        self.from_ = table("from_")
        self.ones = table("ones")
        self.strict3 = table("strict3")
        self.strict3_add = table("strict3_add")
        self.causal3_add = table("causal3_add")
        self.iota16 = table("iota16")
        self.neghalf = table("neghalf")
        self.invcount = table("invcount")
        self.onehot = table("onehot")
        self.prm = self.sb("prm", [P, len(PARAM_GROUPS), P])
        self.ms = self.sb("ms", [P, NB])
        self.rstd = self.sb("rstd", [P, NB])
        self.mu = self.sb("mu", [P, NB])
        self.negmu = self.sb("negmu", [P, NB])
        self.xn = self.sb("xn", [P, NB, D])
        self.cact = self.sb("cact", [P, KT])
        self.first_mod = self.sb("first_mod", [P, 2 * KT])
        self.mod = self.sb("mod", [P, 48])
        self.modA = self.sb("modA", [P, 2, KT])
        self.gate = self.sb("gate", [P, 2, D])
        self.PS = self.ctx.enter_context(nc.psum_tensor("PS", [P, 8, BANK], F32))
        self.banks = [[nc.alloc_semaphore(f"stage{b}_{i}") for i in range(24)] for b in range(2)]
        self.w_landed = [nc.alloc_semaphore(f"w_landed{i}") for i in range(RING)]
        self.w_used = nc.alloc_semaphore("w_used")
        self.side_landed = [nc.alloc_semaphore(f"ada_landed{i}") for i in range(SIDE_RING)]
        self.side_used = nc.alloc_semaphore("ada_used")
        self.g_landed = [nc.alloc_semaphore(f"g_landed{i}") for i in range(GRING)]
        self.g_used = nc.alloc_semaphore("g_used_ve")
        self.g_used_pe = nc.alloc_semaphore("g_used_pe")
        self.g_index = nc.alloc_semaphore("g_index")
        self.g_turn = nc.alloc_semaphore("g_turn")

    def col(self, name, j=0):
        for g, rows in enumerate(PARAM_GROUPS):
            at = 0
            for n, count in rows:
                if n == name:
                    return self.prm[:, g, at + j:at + count]
                at += count
        raise KeyError(name)

    def plan(self):
        a = self.a

        def lin(w, jobs):
            out = []
            for cols in jobs:
                cols = [cols] if isinstance(cols, tuple) else cols
                width = sum(n for _, n in cols)
                for g in range(w.shape[0] // 512):
                    rows = w[g * 512:(g + 1) * 512, :].rearrange("(k p) n -> p k n", p=P)
                    at, pieces = 0, []
                    for c0, n in cols:
                        pieces.append((at, n, width, rows[:, :, c0:c0 + n]))
                        at += n
                    out.append(("lin", pieces))
            return out

        def full(n):
            return [(c, 512) for c in range(0, n, 512)]

        def ffn(wg, wu, wd):
            def up(i):
                return [("lin", [(256 * m, 256, 512, w[512 * g:512 * (g + 1), i * 256:(i + 1) * 256]
                                  .rearrange("(k p) n -> p k n", p=P)) for m, w in enumerate((wg, wu))]) for g in range(2)]

            def down(i):
                return [("down", wd[i * 256:(i + 1) * 256, :].rearrange("(k p) n -> p k n", p=P))]
            out = up(0)
            for i in range(FF_STEPS):
                out += (up(i + 1) if i + 1 < FF_STEPS else []) + down(i)
            return out

        stages = []
        for l in range(2):
            stages += [(f"mix_in{l}", lin(a["w_in"][l], full(2560))),
                       (f"mix_out{l}", lin(a["w_out"][l], full(D))),
                       (f"peer_q{l}", lin(a["peer_wq"][l], full(2048)))]
        for l in range(2):
            stages.append((f"ffn1_{l}", ffn(a["ffn1_w_gate_2"][l], a["ffn1_w_up_2"][l], a["ffn1_w_down_2"][l])))
            if l == 0:
                stages += [("ab_in", lin(a["ab_w_in_2"][0], full(1536))),
                           ("ab_out", lin(a["ab_w_out_2"][0], full(D)))]
            else:
                stages += [("c_in", lin(a["c_w_in_2"][0], full(3584) + [[(3584, 64), (3584, 64), (3648, 8)]])),
                           ("c_out", lin(a["c_w_out_2"][0], full(D)))]
            stages.append((f"ffn2_{l}", ffn(a["ffn2_w_gate_2"][l], a["ffn2_w_up_2"][l], a["ffn2_w_down_2"][l])))
        w3 = a["w_in_3"]
        stages += [("ffn1_3", ffn(a["ffn1_w_gate_3"], a["ffn1_w_up_3"], a["ffn1_w_down_3"])),
                   ("ssm_in", lin(w3, [(2048 + c, 512) for c in range(0, 4096, 512)] + [(6144, 32)])),
                   ("ssm_z", lin(w3, full(2048))),
                   ("ssm_out", lin(a["w_ssm_out_3"], full(D))),
                   ("att_in", lin(w3, [(6176 + c, 512) for c in range(0, 3072, 512)])),
                   ("att_out", lin(a["w_att_out_3"], full(D)) + lin(w3, [(9248 + c, 512) for c in range(0, 2048, 512)])),
                   ("mix3_out", lin(a["w_o_3"], full(D))),
                   ("ffn2_3", ffn(a["ffn2_w_gate_3"], a["ffn2_w_up_3"], a["ffn2_w_down_3"]))]
        self.chunks, self.chunk_end = [], {}
        for name, chunks in stages:
            self.chunks += chunks
            self.chunk_end[name] = len(self.chunks)
        self.landed_at, total = [], [0] * RING
        for n, chunk in enumerate(self.chunks):
            total[n % RING] += 16 * (len(chunk[1]) if chunk[0] == "lin" else 1)
            self.landed_at.append(total[n % RING])
        self.issued = self.taken = 0

    def load_weights(self, sp, name, side=None):
        end = self.chunk_end.get(name, self.taken)
        last = min(len(self.chunks), end + RING)
        side_last = min(self.side_end, self.side_taken + side + SIDE_RING) if side is not None else self.side_issued
        side_first, first = self.side_issued, self.issued
        for n in range(first, last):
            due = side_last if name == "ahead" else side_first + -(-(side_last - side_first) * (n - first + 1) // (last - first))
            self.load_side(sp, due)
            if n >= RING:
                sp.wait_ge(self.w_used, n - RING + 1)
            slot = self.ring[:, n % RING, :]
            kind, what = self.chunks[n]
            if kind == "lin":
                for at, w, width, src in what:
                    dst = slot[:, 0:4 * width].rearrange("p (k n) -> p k n", k=4)[:, :, at:at + w]
                    sp.dma_start(dst, src).then_inc(self.w_landed[n % RING], 16)
            else:
                dst = slot.rearrange("p (k n) -> p k n", k=2)
                sp.dma_start(dst, what).then_inc(self.w_landed[n % RING], 16)
        self.load_side(sp, side_last)
        self.issued = max(first, last)

    def plan_side(self):
        order = [(0, 0), (0, 1), (0, 2), (1, 0), (1, 1), (1, 2)]
        self.side_chunks = [(l, g, k, h) for l, g in order for k in range(KT) for h in range(SIDE_GROUP)]
        self.side_issued = self.side_taken = self.side_end = 0

    def load_side(self, sp, upto):
        for n in range(self.side_issued, upto):
            if n >= SIDE_RING:
                sp.wait_ge(self.side_used, n - SIDE_RING + 1)
            l, g, k, h = self.side_chunks[n]
            c = (SIDE_GROUP * g + h) * SIDE_COLS
            sp.dma_start(self.side_ring[:, n % SIDE_RING, :],
                         self.a["ada_w"][l, k * P:(k + 1) * P, c:c + SIDE_COLS]).then_inc(self.side_landed[n % SIDE_RING], 16)
        self.side_issued = max(self.side_issued, upto)

    def sum_side(self, ve, count):
        for n in range(self.side_taken, self.side_taken + count):
            l, g, k, h = self.side_chunks[n]
            ve.wait_ge(self.side_landed[n % SIDE_RING], 16 * (n // SIDE_RING + 1))
            slot, acc, c = self.side_ring[:, n % SIDE_RING, :], self.side_acc[:, SIDE_GROUP * g + h, :], self.cact[:, k:k + 1]
            if k == 0:
                self.nc.vector.tensor_scalar(acc, slot, c, None, ALU.mult).then_inc(self.side_used, 1)
            else:
                self.nc.vector.scalar_tensor_tensor(acc, slot, c, acc, ALU.mult, ALU.add).then_inc(self.side_used, 1)
            if h == SIDE_GROUP - 1:
                self.nc.vector.drain()
        self.side_taken += count

    def sum_columns(self, out, v):
        for k in range(KT):
            ins = self.nc.tensor.matmul(out[:, k:k + 1], self.side_acc[:, v, k * P:(k + 1) * P], self.ones[:, 0:1],
                                        start=True, stop=True, skip_group_check=True)
        return ins

    def sum_spread(self, bank, v):
        for h in range(2):
            ins = self.nc.tensor.matmul(self.PS[:, bank + h, :], self.ones, self.side_acc[:, v, h * BANK:(h + 1) * BANK],
                                        start=True, stop=True)
        return ins

    def place_side(self, ctx, count):
        self.side_ring = self.sb("ada_ring", [P, SIDE_RING, SIDE_COLS], ctx=ctx)
        self.side_acc = self.sb("ada_sums", [P, 6, D], ctx=ctx)
        self.side_end += count

    def take(self, pe):
        n = self.taken
        self.taken += 1
        pe.wait_ge(self.w_landed[n % RING], self.landed_at[n])
        return self.ring[:, n % RING, :]

    @contextmanager
    def stage(self, names, weights=None, side=None):
        nc = self.nc
        mine, other = self.banks[self.n_stage % 2], self.banks[(self.n_stage + 1) % 2]
        self.n_stage += 1
        self.base = self.taken
        names = names.split()
        assert len(names) <= len(mine)
        with nc.Block(no_gpsimd_drain=True) as block:
            @block.gpsimd
            def _(pool):
                nc.gpsimd.sem_clear(range(other[0].num, other[-1].num + 1))

            if weights or side is not None:
                @block.sync
                def _(sp):
                    self.load_weights(sp, weights, side)

            yield block, namedtuple("StageSemaphores", names)(*mine[:len(names)])

    def norm_vector(self, ve, S, scale, shift, tap=None):
        nc = self.nc
        for b in range(NB):
            nc.vector.tensor_tensor_reduce(self.xn[:, b, :], self.X[:, b, :], self.X[:, b, :], 1.0 / D, EPS,
                                           ALU.mult, ALU.add, self.ms[:, b:b + 1])
        nc.vector.drain().then_inc(S.n_ms, 1)
        ve.wait_ge(S.n_rstd, 1)
        for b in range(NB):
            nc.vector.tensor_scalar(self.xn[:, b, :], self.X[:, b, :], self.rstd[:, b:b + 1], None,
                                    ALU.mult).then_inc(S.n_xn, 1)
        self.evacuate_tiles(ve, nc.vector, S, 1, scale, shift)

    def norm_gpsimd(self, pool, S):
        pool.wait_ge(S.n_ms, 1)
        self.nc.gpsimd.tensor_tensor(self.rstd[:], self.ms[:], self.neghalf[:, 0:NB], ALU.pow).then_inc(S.n_rstd, 1)

    def norm_tensor(self, pe, S, src=None):
        nc = self.nc
        for b in range(NB):
            pe.wait_ge(S.n_xn, b + 1)
            for g in range(2):
                for j in range(4):
                    k = 4 * g + j
                    ins = nc.tensor.transpose(self.PS[:, 4 + 2 * b + g, j * P:(j + 1) * P],
                                              (src or self.xn)[:, b, k * P:(k + 1) * P], self.ident)
                ins.then_inc(S.n_tr, 1)

    def evacuate_tiles(self, eng, ops, S, odd, scale, shift):
        for b in range(NB):
            for g in (odd,):
                eng.wait_ge(S.n_tr, 2 * b + g + 1)
                for j in range(4):
                    k = 4 * g + j
                    out = self.hT[:, k, b * P:(b + 1) * P]
                    src = self.PS[:, 4 + 2 * b + g, j * P:(j + 1) * P]
                    bias = shift[:, k:k + 1] if shift is not None else 0.0
                    if odd:
                        if shift is None:
                            ins = ops.tensor_scalar(out, src, scale[:, k:k + 1], None, ALU.mult)
                        else:
                            ins = ops.tensor_scalar(out, src, scale[:, k:k + 1], bias, ALU.mult, ALU.add)
                    elif shift is None:
                        ins = ops.activation(out, src, ACT.Copy, scale=scale[:, k:k + 1])
                    else:
                        ins = ops.activation(out, src, ACT.Identity, bias=bias, scale=scale[:, k:k + 1])
                ins.then_inc(S.n_hT, 1)

    def norm_scalar(self, act, S, scale, shift):
        self.evacuate_tiles(act, self.nc.scalar, S, 0, scale, shift)

    N_HT = 4

    def project(self, pe, S, jobs, actT, kts, first=0):
        nc = self.nc
        for j, (kind, w) in enumerate(jobs, first):
            pair = 2 * (j % 2)
            if j >= 2:
                pe.wait_ge((S.p_free0, S.p_free1)[j % 2], 2 * (j // 2))
            for g in range(kts // 4):
                slot = self.take(pe)[:, 0:4 * w].rearrange("p (k n) -> p k n", k=4)
                for kk in range(4):
                    k = 4 * g + kk
                    if kind == "T":
                        for b in range(NB):
                            ins = nc.tensor.matmul(self.PS[:, pair + b, 0:w], actT[:, k, b * P:(b + 1) * P],
                                                   slot[:, kk, :], start=(k == 0), stop=(k == kts - 1),
                                                   skip_group_check=True)
                    else:
                        for t in range(w // P):
                            ins = nc.tensor.matmul(
                                self.PS[:, pair + t // 2, (t % 2) * SEQ:(t % 2 + 1) * SEQ],
                                slot[:, kk, t * P:(t + 1) * P], actT[:, k, :],
                                start=(k == 0 and t % 2 == 0), stop=(k == kts - 1), skip_group_check=True)
                ins.then_inc(self.w_used, 1)

    def leave(self, eng, j, per=2):
        eng.wait_ge(self.w_used, self.base + (j + 1) * per)

    def bank(self, j, e):
        return self.PS[:, 2 * (j % 2) + e, :]

    def freed(self, S, j):
        return (S.p_free0, S.p_free1)[j % 2]

    def load_constants(self):
        nc, a = self.nc, self.a
        with ExitStack() as ctx, self.stage("rows turned turned_out") as (block, S):
            rows = self.sb("param_rows", [P, len(PARAM_GROUPS), P], ctx=ctx)
            loads = nc.alloc_semaphore("const_landed")
            dmas = [(self.cst[:], a["shape_consts"])] + [
                (self.X[:], a["x"][0].rearrange("(b p) d -> p b d", p=P))]
            for g, group in enumerate(PARAM_GROUPS):
                at = 0
                for name, count in group:
                    src = a[name]
                    flat = src.rearrange(" ".join("abc"[:len(src.shape)]) + " -> (" + " ".join("abc"[:len(src.shape)]) + ")")
                    dmas.append((rows[at:at + count, g, :], flat.rearrange("(r p) -> r p", p=P)))
                    at += count

            @block.sync
            def _(sp):
                sp.wait_ge(loads, 16 * len(dmas))
                self.load_side(sp, SIDE_RING)

            @block.vector
            def _(ve):
                nc.vector.memset(rows[:], 0.0).then_inc(S.rows, 1)
                ve.wait_ge(S.turned, 1)
                for g in range(len(PARAM_GROUPS)):
                    ins = nc.vector.tensor_copy(self.prm[:, g, :], self.PS[:, g, 0:P])
                ins.then_inc(S.turned_out, 1)

            @block.scalar
            def _(act):
                act.wait_ge(S.rows, 1)
                for dst, src in dmas:
                    act.dma_start(dst, src).then_inc(loads, 16)
                act.wait_ge(loads, 16 * len(dmas))

            @block.tensor
            def _(pe):
                pe.wait_ge(loads, 16 * len(dmas))
                for g in range(len(PARAM_GROUPS)):
                    ins = nc.tensor.transpose(self.PS[:, g, 0:P], rows[:, g, :], self.ident)
                ins.then_inc(S.turned, 1)

    def ada_start(self):
        nc = self.nc
        group = KT * SIDE_GROUP
        with self.stage("silu summed columns", "ahead", side=group) as (block, S):
            @block.scalar
            def _(act):
                nc.scalar.activation(self.cact[:], self.col("c"), ACT.Silu).then_inc(S.silu, 1)
                act.wait_ge(S.columns, 1)
                nc.scalar.copy(self.first_mod[:], self.PS[:, 0, 0:2 * KT])

            @block.vector
            def _(ve):
                ve.wait_ge(S.silu, 1)
                self.sum_side(ve, group)
                nc.vector.drain().then_inc(S.summed, 1)

            @block.tensor
            def _(pe):
                pe.wait_ge(S.summed, 1)
                self.sum_columns(self.PS[:, 0, 0:KT], 0)
                self.sum_columns(self.PS[:, 0, KT:2 * KT], 1).then_inc(S.columns, 1)

    def ffn(self, name, gain=None, layer_norm=None):
        nc = self.nc
        with ExitStack() as ctx, self.stage(
                "n_ms n_rstd n_xn n_tr n_hT hT_hi hT_split w_hi w_lo silu_done hid_ready hid_turned hid_hi hid_lo l_ms l_rstd", name) as (block, S):
            silu = self.sb("silu_gate", [P, NB, FF_COLS], ctx=ctx)
            hid = self.sb("hidden", [P, NB, FF_COLS], ctx=ctx)
            hidT_hi = self.sb("hiddenT_hi", [P, 2, SEQ], F32R, ctx=ctx)
            hidT_lo = self.sb("hiddenT_lo", [P, 2, SEQ], F32R, ctx=ctx)
            hT_hi = self.sb("hT_hi", [P, KT, SEQ], F32R, ctx=ctx)
            hT_lo = self.sb("hT_lo", [P, KT, SEQ], F32R, ctx=ctx)
            ring_hi = self.sb("ring_hi", [P, SPLIT, SLOT], F32R, ctx=ctx)
            ring_lo = self.sb("ring_lo", [P, SPLIT, SLOT], F32R, ctx=ctx)
            WINDOWS = 4
            if layer_norm:
                lnp = self.sb("ln_params", [P, 2, D], ctx=ctx)
                ln_landed = nc.alloc_semaphore("ln_landed_" + name)
            base = self.taken
            last = 3 * FF_STEPS - 1

            def landed(c, i):
                per = self.landed_at[base + c + 3 * WINDOWS] - self.landed_at[base + c] if i is not None else 0
                return self.landed_at[base + c] if i is None else i * per + self.landed_at[base + c]

            def count(n, i, per):
                return n if i is None else i * per + n

            def product(out, left, right, start, stop):
                for a_, b_ in ((0, 0), (0, 1), (1, 0)):
                    ins = nc.tensor.matmul(out, left[a_], right[b_], start=start and a_ + b_ == 0, stop=stop and a_ == 1,
                                           skip_group_check=True)
                return ins

            def halves(c):
                return ring_hi[:, c % SPLIT, :], ring_lo[:, c % SPLIT, :]

            def up(pe, c, i, parity, half):
                pe.wait_ge(S.w_lo, count(c + 1, i, 3 * WINDOWS))
                parts = [x.rearrange("p (k n) -> p k n", k=4) for x in halves(c)]
                for kk in range(4):
                    k = 4 * half + kk
                    for b in range(NB):
                        tok = slice(b * P, (b + 1) * P)
                        ins = product(self.PS[:, 2 * parity + b, :], [hT_hi[:, k, tok], hT_lo[:, k, tok]],
                                      [x[:, kk, :] for x in parts], k == 0, k == KT - 1)
                ins.then_inc(self.w_used, 1)

            def turn(pe, s, i, parity):
                pe.wait_ge(S.hid_ready, count(s + 1, i, WINDOWS))
                for t in range(2):
                    for b in range(NB):
                        ins = nc.tensor.transpose(self.PS[:, 2 * parity, t * SEQ + b * P:t * SEQ + (b + 1) * P],
                                                  hid[:, b, t * P:(t + 1) * P], self.ident)
                ins.then_inc(S.hid_turned, 1)

            def down(pe, s, c, i, first=False):
                pe.wait_ge(S.w_lo, count(c + 1, i, 3 * WINDOWS))
                pe.wait_ge(S.hid_lo, count(s + 1, i, WINDOWS))
                parts = [x.rearrange("p (t n) -> p t n", t=2) for x in halves(c)]
                for t in range(2):
                    for b in range(NB):
                        tok = slice(b * P, (b + 1) * P)
                        for h in range(2):
                            ins = product(self.PS[:, 4 + 2 * b + h, :], [hidT_hi[:, t, tok], hidT_lo[:, t, tok]],
                                          [x[:, t, h * BANK:(h + 1) * BANK] for x in parts],
                                          first and t == 0, c == last and t == 1)
                ins.then_inc(self.w_used, 1)

            @block.tensor
            def _(pe):
                def window(s, i):
                    p = (s + 1) % 2
                    up(pe, 3 * s + 2, i, p, 0)
                    turn(pe, s, i, 1 - p)
                    up(pe, 3 * s + 3, i, p, 1)
                    down(pe, s, 3 * s + 4, i, first=(s == 0 and i is None))

                if layer_norm:
                    for b in range(NB):
                        for g in range(2):
                            for j in range(4):
                                k = 4 * g + j
                                ins = nc.tensor.transpose(self.PS[:, 4 + 2 * b + g, j * P:(j + 1) * P],
                                                          self.X[:, b, k * P:(k + 1) * P], self.ident)
                            ins.then_inc(S.n_tr, 1)
                else:
                    self.norm_tensor(pe, S)
                pe.wait_ge(S.hT_split, 1)
                up(pe, 0, None, 0, 0)
                up(pe, 1, None, 0, 1)
                window(0, None)
                with pe.Fori(0, (FF_STEPS - 3) // WINDOWS) as i:
                    for u in range(WINDOWS):
                        window(1 + u, i)
                window(FF_STEPS - 2, None)
                s = FF_STEPS - 1
                turn(pe, s, None, s % 2)
                down(pe, s, last, None)
                self.taken += 3 * FF_STEPS

            @block.scalar
            def _(act):
                def hi(c, i=None):
                    act.wait_ge(self.w_landed[(base + c) % RING], landed(c, i))
                    if c >= SPLIT:
                        act.wait_ge(self.w_used, count(base + c - SPLIT + 1, i, 3 * WINDOWS))
                    nc.scalar.copy(halves(c)[0], self.ring[:, (base + c) % RING, :]).then_inc(S.w_hi, 1)

                def silu_step(s, i, used):
                    act.wait_ge(self.w_used, count(base + used, i, 3 * WINDOWS))
                    p = 2 * (s % 2)
                    nc.scalar.activation(silu[:], self.PS[:, p:p + 2, 0:FF_COLS], ACT.Silu).then_inc(S.silu_done, 1)

                def hid_hi(s, i):
                    act.wait_ge(S.hid_turned, count(s + 1, i, WINDOWS))
                    nc.scalar.copy(hidT_hi[:].rearrange("p t n -> p (t n)"), self.PS[:, 2 * (s % 2), :]).then_inc(S.hid_hi, 1)

                def window(s, i):
                    silu_step(s, i, 2 if s == 0 else 3 * s + 1)
                    for c in (3 * s + 4, 3 * s + 5):
                        if c <= last:
                            hi(c, i)
                    hid_hi(s, i)
                    if 3 * s + 6 <= last:
                        hi(3 * s + 6, i)

                if layer_norm:
                    for i, v in enumerate(layer_norm):
                        act.dma_start(lnp[:, i, :], v.partition_broadcast(P)).then_inc(ln_landed, 16)
                hi(0)
                hi(1)
                if layer_norm:
                    self.copy_tiles(act, nc.scalar.copy, S, 0)
                else:
                    self.norm_scalar(act, S, gain, None)
                nc.scalar.drain()
                nc.scalar.copy(hT_hi[:, 0:4, :], self.hT[:, 0:4, :]).then_inc(S.hT_hi, 1)
                hi(2)
                hi(3)
                window(0, None)
                with act.Fori(0, (FF_STEPS - 3) // WINDOWS) as i:
                    for u in range(WINDOWS):
                        window(1 + u, i)
                window(FF_STEPS - 2, None)
                window(FF_STEPS - 1, None)

            @block.vector
            def _(ve):
                def lo(c, i=None):
                    ve.wait_ge(S.w_hi, count(c + 1, i, 3 * WINDOWS))
                    slot = self.ring[:, (base + c) % RING, :]
                    nc.vector.tensor_tensor(halves(c)[1], slot, halves(c)[0], ALU.subtract).then_inc(S.w_lo, 1)

                def window(s, i):
                    ve.wait_ge(S.silu_done, count(s + 1, i, WINDOWS))
                    p = 2 * (s % 2)
                    nc.vector.tensor_tensor(hid[:], silu[:], self.PS[:, p:p + 2, FF_COLS:2 * FF_COLS], ALU.mult).then_inc(S.hid_ready, 1)
                    for c in (3 * s + 4, 3 * s + 5):
                        if c <= last:
                            lo(c, i)
                    ve.wait_ge(S.hid_hi, count(s + 1, i, WINDOWS))
                    flat = "p t n -> p (t n)"
                    nc.vector.tensor_tensor(hidT_lo[:].rearrange(flat), self.PS[:, p, :], hidT_hi[:].rearrange(flat),
                                            ALU.subtract).then_inc(S.hid_lo, 1)
                    if 3 * s + 6 <= last:
                        lo(3 * s + 6, i)

                if layer_norm:
                    self.copy_tiles(ve, nc.vector.tensor_copy, S, 1)
                else:
                    self.norm_vector(ve, S, gain, None)
                nc.vector.drain()
                nc.vector.tensor_copy(hT_hi[:, 4:8, :], self.hT[:, 4:8, :])
                nc.vector.drain()
                ve.wait_ge(S.hT_hi, 1)
                nc.vector.tensor_tensor(hT_lo[:], self.hT[:], hT_hi[:], ALU.subtract).then_inc(S.hT_split, 1)
                for c in range(4):
                    lo(c)
                window(0, None)
                with ve.Fori(0, (FF_STEPS - 3) // WINDOWS) as i:
                    for u in range(WINDOWS):
                        window(1 + u, i)
                window(FF_STEPS - 2, None)
                window(FF_STEPS - 1, None)
                ve.wait_ge(self.w_used, base + 3 * FF_STEPS)
                out = self.PS[:, 4:8, :].rearrange("p (b h) n -> p b (h n)", b=NB)
                if not layer_norm:
                    for b in range(NB):
                        nc.vector.scalar_tensor_tensor(self.X[:, b, :], out[:, b, :], 0.5, self.X[:, b, :],
                                                       ALU.mult, ALU.add)
                else:
                    for b in range(NB):
                        nc.vector.tensor_scalar(self.X[:, b, :], self.X[:, b, :], ALPHA, None, ALU.mult)
                    nc.vector.drain()
                    for b in range(NB):
                        nc.vector.scalar_tensor_tensor(self.X[:, b, :], out[:, b, :], 0.5, self.X[:, b, :],
                                                       ALU.mult, ALU.add)
                    nc.vector.drain()
                    ve.wait_ge(ln_landed, 32)
                    self.layer_norm_vector(ve, S, lnp)

            @block.gpsimd
            def _(pool):
                if layer_norm:
                    self.layer_norm_gpsimd(pool, S)
                else:
                    self.norm_gpsimd(pool, S)

    def copy_tiles(self, eng, copy, S, odd):
        for b in range(NB):
            eng.wait_ge(S.n_tr, 2 * b + odd + 1)
            copy(self.hT[:, 4 * odd:4 * odd + 4, b * P:(b + 1) * P],
                 self.PS[:, 4 + 2 * b + odd, :].rearrange("p (k n) -> p k n", k=4)).then_inc(S.n_hT, 1)

    def layer_norm_vector(self, ve, S, lnp):
        nc = self.nc
        nc.vector.reduce_sum(self.mu[:], self.X[:], AX.X)
        nc.vector.drain()
        nc.vector.tensor_scalar(self.negmu[:], self.mu[:], -1.0 / D, None, ALU.mult)
        nc.vector.drain()
        for b in range(NB):
            nc.vector.tensor_scalar(self.X[:, b, :], self.X[:, b, :], self.negmu[:, b:b + 1], None, ALU.add)
        nc.vector.drain()
        for b in range(NB):
            nc.vector.tensor_tensor_reduce(self.xn[:, b, :], self.X[:, b, :], self.X[:, b, :], 1.0 / D, LN_EPS,
                                           ALU.mult, ALU.add, self.ms[:, b:b + 1])
        nc.vector.drain().then_inc(S.l_ms, 1)
        ve.wait_ge(S.l_rstd, 1)
        for b in range(NB):
            nc.vector.scalar_tensor_tensor(self.X[:, b, :], self.X[:, b, :], self.rstd[:, b:b + 1], lnp[:, 0, :],
                                           ALU.mult, ALU.mult)
        nc.vector.drain()
        for b in range(NB):
            nc.vector.tensor_tensor(self.X[:, b, :], self.X[:, b, :], lnp[:, 1, :], ALU.add)

    def layer_norm_gpsimd(self, pool, S):
        pool.wait_ge(S.l_ms, 1)
        self.nc.gpsimd.tensor_tensor(self.rstd[:], self.ms[:], self.neghalf[:, 0:NB], ALU.pow).then_inc(S.l_rstd, 1)

    def final_norm(self, gain):
        nc = self.nc
        with ExitStack() as ctx, self.stage("ms rstd done") as (block, S):
            g = self.sb("final_gain", [P, D], ctx=ctx)
            landed = nc.alloc_semaphore("gain_landed_" + str(self.n_stage))

            @block.scalar
            def _(act):
                act.dma_start(g[:], gain.partition_broadcast(P)).then_inc(landed, 16)

            @block.vector
            def _(ve):
                for b in range(NB):
                    nc.vector.tensor_tensor_reduce(self.xn[:, b, :], self.X[:, b, :], self.X[:, b, :], 1.0 / D, EPS,
                                                   ALU.mult, ALU.add, self.ms[:, b:b + 1])
                nc.vector.drain().then_inc(S.ms, 1)
                ve.wait_ge(S.rstd, 1)
                ve.wait_ge(landed, 16)
                for b in range(NB):
                    nc.vector.scalar_tensor_tensor(self.X[:, b, :], self.X[:, b, :], self.rstd[:, b:b + 1], g[:],
                                                   ALU.mult, ALU.mult)

            @block.gpsimd
            def _(pool):
                pool.wait_ge(S.ms, 1)
                nc.gpsimd.tensor_tensor(self.rstd[:], self.ms[:], self.neghalf[:, 0:NB], ALU.pow).then_inc(S.rstd, 1)

    def store(self, out):
        nc = self.nc
        stored = nc.alloc_semaphore("stored")
        with self.stage("") as (block, S):
            @block.scalar
            def _(act):
                act.dma_start(out[0].rearrange("(b p) d -> p b d", p=P), self.X[:]).then_inc(stored, 16)
                act.wait_ge(stored, 16)

    def mixer(self, l):
        nc, a = self.nc, self.a
        with ExitStack() as ctx:
            U = self.sb("gelu_u", [P, NB, HALF], ctx=ctx)
            V = self.sb("gelu_v", [P, NB, HALF], ctx=ctx)
            QT = self.sb("stick_qT", [P, 4, SEQ], ctx=ctx)
            KT_ = self.sb("stick_kT", [P, 4, SEQ], ctx=ctx)
            SV = self.sb("stick_v", [P, NB, HALF], ctx=ctx)
            Y = self.sb("mixed", [P, NB, D], ctx=ctx)
            vgain = self.sb("v_gain", [P, HALF], ctx=ctx)
            ws = self.sb("gm_w", [P, HEADS, P], ctx=ctx)
            side = nc.alloc_semaphore(f"mixer_side{l}")

            group = KT * SIDE_GROUP
            bias = self.col("ada_b")[:, 6 * KT * l:]
            with self.stage("n_ms n_rstd n_xn n_tr n_hT p_free0 p_free1", f"mix_in{l}", side=2 * group) as (block, S):
                jobs = [("T", 512), ("T", 512), ("F", 512), ("F", 512), ("T", 512)]

                @block.tensor
                def _(pe):
                    self.norm_tensor(pe, S)
                    pe.wait_ge(S.n_hT, self.N_HT)
                    self.project(pe, S, jobs, self.hT, KT)

                @block.scalar
                def _(act):
                    act.dma_start(vgain[:], a["gm_vnorm"][l].partition_broadcast(P)).then_inc(side, 16)
                    act.dma_start(ws[:], a["gm_ws"][l].rearrange("h t s -> t h s")).then_inc(side, 16)
                    for i, v in enumerate((2, 5)):
                        act.dma_start(self.gate[:, i, :], a["ada_b"][l, v * D:(v + 1) * D].partition_broadcast(P)).then_inc(side, 16)
                    self.norm_scalar(act, S, self.modA[:, 0, :], self.mod[:, 0:KT])
                    for j, dst in enumerate((U, V)):
                        self.leave(act, j)
                        for e in range(2):
                            nc.scalar.activation(dst[:, e, :], self.bank(j, e), ACT.Gelu_apprx_tanh).then_inc(self.freed(S, j), 1)
                    self.leave(act, 4)
                    for e in range(2):
                        nc.scalar.copy(SV[:, e, :], self.bank(4, e)).then_inc(self.freed(S, 4), 1)

                @block.vector
                def _(ve):
                    nc.vector.tensor_tensor(self.mod[:, 0:2 * KT], self.first_mod[:], bias[:, 0:2 * KT], ALU.add)
                    nc.vector.drain()
                    nc.vector.scalar_tensor_tensor(self.modA[:, 0, :], self.mod[:, KT:2 * KT], 1.0,
                                                   self.col("norm_mix")[:, KT * l:KT * (l + 1)], ALU.add, ALU.mult)
                    self.norm_vector(ve, S, self.modA[:, 0, :], self.mod[:, 0:KT])
                    left = 2 * group
                    for j, dst, scale in ((2, QT, 0.125), (3, KT_, 1.0)):
                        count = left * 5 // 8 if j == 2 else left // 2
                        self.sum_side(ve, count)
                        left -= count
                        self.leave(ve, j)
                        for e in range(2):
                            nc.vector.tensor_scalar(dst[:, 2 * e:2 * e + 2, :].rearrange("p t n -> p (t n)"),
                                                    self.bank(j, e), scale, None, ALU.mult).then_inc(self.freed(S, j), 1)
                    self.sum_side(ve, left)

                @block.gpsimd
                def _(pool):
                    self.norm_gpsimd(pool, S)

            with self.stage("scores sp keep summed expo att pv wT wT_out v_ms v_rstd v_hat gated gate_sum gate_out ada_sum",
                            side=0 if l == 0 else None) as (block, S):
                wT = self.sb("gm_wT", [P, HEADS, P], ctx=ctx)
                sq = self.sb("v_squares", [P, NB, HALF], ctx=ctx)
                vms = self.sb("v_ms", [P, NB * HEADS], ctx=ctx)
                vrs = self.sb("v_rstd", [P, NB * HEADS], ctx=ctx)
                W3 = 3 * P
                ab = self.sb("stick_abs", [P, 2, W3], ctx=ctx)
                sp = self.sb("stick_softplus", [P, 2, W3], ctx=ctx)
                keep = self.sb("stick_keep", [P, 2, W3], ctx=ctx)
                lg = self.sb("stick_log", [P, 2, W3], ctx=ctx)
                at = self.sb("stick_att", [P, 2, W3], ctx=ctx)
                v3 = lambda t: t.rearrange("p b (h c) -> p (b h) c", h=HEADS)

                @block.tensor
                def _(pe):
                    pe.wait_ge(side, 64)
                    for h in range(HEADS):
                        ins = nc.tensor.transpose(self.PS[:, 4 + h // 4, (h % 4) * P:(h % 4 + 1) * P], ws[:, h, :], self.ident)
                    ins.then_inc(S.wT, 1)

                    def scores(h):
                        r, t, Z = 64 * (h % 2), h // 2, self.PS[:, h % 2, :]
                        if h >= 2:
                            pe.wait_ge(S.expo, h - 1)
                        nc.tensor.matmul(Z[:, 0:SEQ], KT_[r:r + 64, t, 0:P], QT[r:r + 64, t, :], start=True, stop=False,
                                         skip_group_check=True)
                        nc.tensor.matmul(Z[:, SEQ:W3], KT_[r:r + 64, t, P:SEQ], QT[r:r + 64, t, P:SEQ], start=False,
                                         stop=False, skip_group_check=True).then_inc(S.scores, 1)

                    def sums(h):
                        Z, lk = self.PS[:, h % 2, :], keep[:, h % 2, :]
                        pe.wait_ge(S.keep, h + 1)
                        nc.tensor.matmul(Z[:, 0:SEQ], self.from_, lk[:, 0:SEQ], start=False, stop=True, skip_group_check=True)
                        nc.tensor.matmul(Z[:, P:SEQ], self.ones, lk[:, SEQ:W3], start=False, stop=True, skip_group_check=True)
                        nc.tensor.matmul(Z[:, SEQ:W3], self.from_, lk[:, SEQ:W3], start=False, stop=True,
                                         skip_group_check=True).then_inc(S.summed, 1)

                    def values(h):
                        c = slice(64 * h, 64 * h + 64)
                        pe.wait_ge(S.att, h + 1)
                        A = at[:, h % 2, :]
                        nc.tensor.matmul(self.PS[:, 2, c], A[:, 0:P], SV[:, 0, c], start=True, stop=True)
                        nc.tensor.matmul(self.PS[:, 3, c], A[:, P:SEQ], SV[:, 0, c], start=True, stop=False)
                        nc.tensor.matmul(self.PS[:, 3, c], A[:, SEQ:W3], SV[:, 1, c], start=False, stop=True).then_inc(S.pv, 1)

                    scores(0)
                    for h in range(HEADS):
                        if h + 1 < HEADS:
                            scores(h + 1)
                        sums(h)
                        if h >= 1:
                            values(h - 1)
                        if h == 3:
                            pe.wait_ge(S.wT_out, 1)
                            pe.wait_ge(S.v_hat, 1)
                            for b in range(NB):
                                for g in range(HEADS):
                                    c = slice(64 * g, 64 * g + 64)
                                    ins = nc.tensor.matmul(self.PS[:, 6 + b, c], wT[:, g, :], V[:, b, c], start=True, stop=True)
                            ins.then_inc(S.gated, 1)
                            self.sum_spread(4, 2).then_inc(S.gate_sum, 1)
                        if h == 6:
                            pe.wait_ge(S.gate_out, 1)
                            self.sum_spread(4, 5)
                            for i, v in enumerate((3, 4)):
                                ins = self.sum_columns(self.PS[:, 6, i * KT:(i + 1) * KT], v)
                            ins.then_inc(S.ada_sum, 1)
                    values(HEADS - 1)

                @block.scalar
                def _(act):
                    def log_keep(h):
                        i = h % 2
                        act.wait_ge(S.scores, h + 1)
                        nc.scalar.activation(ab[:, i, :], self.PS[:, i, 0:W3], ACT.Abs)
                        nc.scalar.drain()
                        nc.scalar.activation(sp[:, i, :], ab[:, i, :], ACT.Exp, scale=-1.0)
                        nc.scalar.drain()
                        nc.scalar.activation(sp[:, i, :], sp[:, i, :], ACT.Ln, bias=1.0).then_inc(S.sp, 1)

                    def weights(h):
                        act.wait_ge(S.expo, h + 1)
                        if h >= 2:
                            act.wait_ge(S.pv, h - 1)
                        nc.scalar.activation(at[:, h % 2, :], lg[:, h % 2, :], ACT.Exp).then_inc(S.att, 1)

                    nc.scalar.preload_act_table_set("natural_log_exp_and_others")
                    log_keep(0)
                    for h in range(HEADS):
                        if h + 1 < HEADS:
                            log_keep(h + 1)
                        weights(h)

                @block.vector
                def _(ve):
                    def keeps(h):
                        i = h % 2
                        ve.wait_ge(S.sp, h + 1)
                        nc.vector.scalar_tensor_tensor(sp[:, i, :], self.PS[:, i, 0:W3], 0.0, sp[:, i, :], ALU.max, ALU.add)
                        nc.vector.drain()
                        nc.vector.scalar_tensor_tensor(keep[:, i, :], sp[:, i, :], -1.0, self.strict3, ALU.mult,
                                                       ALU.mult).then_inc(S.keep, 1)

                    def exponents(h):
                        ve.wait_ge(S.summed, h + 1)
                        if h >= 2:
                            ve.wait_ge(S.att, h - 1)
                        nc.vector.tensor_tensor(lg[:, h % 2, :], self.PS[:, h % 2, 0:W3], self.strict3_add,
                                                ALU.add).then_inc(S.expo, 1)

                    def gate_inputs():
                        nc.vector.tensor_tensor(sq[:], V[:], V[:], ALU.mult)
                        nc.vector.drain()
                        nc.vector.tensor_reduce(vms[:], v3(sq[:]), AX.X, ALU.add)
                        nc.vector.drain()
                        nc.vector.tensor_scalar(vms[:], vms[:], 1.0 / 64, EPS, ALU.mult, ALU.add).then_inc(S.v_ms, 1)
                        ve.wait_ge(S.wT, 1)
                        nc.vector.tensor_copy(wT[:].rearrange("p (g h) n -> p g (h n)", g=2), self.PS[:, 4:6, :])
                        nc.vector.drain()
                        nc.vector.memset(wT[64:128, :, 0:64], 0.0).then_inc(S.wT_out, 1)

                    def gate_scale():
                        ve.wait_ge(S.v_rstd, 1)
                        nc.vector.tensor_tensor(v3(V[:]), v3(V[:]), vrs[:].unsqueeze(2).to_broadcast([P, NB * HEADS, 64]), ALU.mult)
                        nc.vector.drain()
                        nc.vector.tensor_tensor(V[:], V[:], vgain[:].unsqueeze(1).to_broadcast([P, NB, HALF]),
                                                ALU.mult).then_inc(S.v_hat, 1)

                    def gate_outputs():
                        ve.wait_ge(S.gated, 1)
                        bias = self.col("gm_bs")[:, HEADS * l:HEADS * (l + 1)].unsqueeze(2).to_broadcast([P, HEADS, 64])
                        for b in range(NB):
                            nc.vector.tensor_tensor(sq[:, b, :].rearrange("p (h c) -> p h c", h=HEADS),
                                                    self.PS[:, 6 + b, :].rearrange("p (h c) -> p h c", h=HEADS), bias, ALU.add)
                        nc.vector.drain()
                        nc.vector.tensor_tensor(Y[:, :, 0:HALF], sq[:], U[:], ALU.mult)

                    def residual_gate(i):
                        g = self.gate[:, i, :].rearrange("p (h n) -> p h n", n=BANK)
                        return nc.vector.tensor_tensor(g, self.PS[:, 4:6, :], g, ALU.add)

                    ve.wait_ge(side, 64)
                    gate_inputs()
                    keeps(0)
                    for h in range(HEADS):
                        if h == 1:
                            gate_scale()
                        if h + 1 < HEADS:
                            keeps(h + 1)
                        exponents(h)
                        if h == 4:
                            gate_outputs()
                            ve.wait_ge(S.gate_sum, 1)
                            residual_gate(0).then_inc(S.gate_out, 1)
                    ve.wait_ge(S.ada_sum, 1)
                    residual_gate(1)
                    nc.vector.tensor_tensor(self.mod[:, 3 * KT:5 * KT], self.PS[:, 6, 0:2 * KT], bias[:, 3 * KT:5 * KT], ALU.add)
                    nc.vector.drain()
                    nc.vector.scalar_tensor_tensor(self.modA[:, 1, :], self.mod[:, 4 * KT:5 * KT], 1.0,
                                                   self.col("norm_ffn")[:, KT * l:KT * (l + 1)], ALU.add, ALU.mult)
                    ve.wait_ge(S.pv, HEADS)
                    nc.vector.tensor_copy(Y[:, :, HALF:D], self.PS[:, 2:4, :])

                @block.gpsimd
                def _(pool):
                    pool.wait_ge(S.v_ms, 1)
                    nc.gpsimd.tensor_tensor(vrs[:], vms[:], self.neghalf[:, 0:NB * HEADS], ALU.pow).then_inc(S.v_rstd, 1)

            with self.stage("n_ms n_rstd n_xn n_tr n_hT p_free0 p_free1 summed columns", f"mix_out{l}",
                            side=group if l == 0 else None) as (block, S):
                ms4 = self.sb("group_ms", [P, 4], ctx=ctx)
                rs4 = self.sb("group_rstd", [P, 4], ctx=ctx)
                junk = self.sb("junk", [P, HALF], ctx=ctx)
                halves = Y[:].rearrange("p b (g n) -> p (b g) n", g=2)
                gains = self.sb("group_gains", [P, KT], ctx=ctx)

                @block.tensor
                def _(pe):
                    self.norm_tensor(pe, S, src=Y)
                    pe.wait_ge(S.n_hT, self.N_HT)
                    self.project(pe, S, [("T", 512)] * 2, self.hT, KT)
                    if l == 0:
                        pe.wait_ge(S.summed, 1)
                        self.sum_columns(self.PS[:, 4, 0:KT], 0)
                        self.sum_columns(self.PS[:, 4, KT:2 * KT], 1).then_inc(S.columns, 1)

                @block.scalar
                def _(act):
                    act.wait_ge(S.n_xn, 1)
                    self.norm_scalar(act, S, gains[:], None)
                    if l == 0:
                        act.wait_ge(S.columns, 1)
                        nc.scalar.copy(self.first_mod[:], self.PS[:, 4, 0:2 * KT])

                @block.vector
                def _(ve):
                    for i, name in enumerate(("out_norm_a", "out_norm_b")):
                        nc.vector.tensor_copy(gains[:, 4 * i:4 * i + 4], self.col(name)[:, 4 * l:4 * l + 4])
                    for i in range(4):
                        nc.vector.tensor_tensor_reduce(self.xn[:, i // 2, (i % 2) * HALF:(i % 2 + 1) * HALF], halves[:, i, :], halves[:, i, :], 1.0 / HALF, EPS,
                                                       ALU.mult, ALU.add, ms4[:, i:i + 1])
                    nc.vector.drain().then_inc(S.n_ms, 1)
                    ve.wait_ge(S.n_rstd, 1)
                    for i in range(4):
                        ins = nc.vector.tensor_scalar(halves[:, i, :], halves[:, i, :], rs4[:, i:i + 1], None, ALU.mult)
                        if i % 2:
                            ins.then_inc(S.n_xn, 1)
                    self.evacuate_tiles(ve, nc.vector, S, 1, gains[:], None)
                    if l == 0:
                        self.sum_side(ve, group)
                        nc.vector.drain().then_inc(S.summed, 1)
                    self.gated_residual(ve, S, 0, ctx)

                @block.gpsimd
                def _(pool):
                    pool.wait_ge(S.n_ms, 1)
                    nc.gpsimd.tensor_tensor(rs4[:], ms4[:], self.neghalf[:, 0:4], ALU.pow).then_inc(S.n_rstd, 1)

    def gated_residual(self, ve, S, which, ctx):
        nc = self.nc
        for j in range(2):
            c = slice(j * BANK, (j + 1) * BANK)
            self.leave(ve, j)
            for b in range(NB):
                nc.vector.tensor_tensor(self.xn[:, b, c], self.bank(j, b), self.gate[:, which, c],
                                        ALU.mult).then_inc(self.freed(S, j), 1)
            nc.vector.drain()
            nc.vector.tensor_tensor(self.X[:, :, c], self.X[:, :, c], self.xn[:, :, c], ALU.add)

    def plain_residual(self, ve, S):
        for j in range(2):
            c = slice(j * BANK, (j + 1) * BANK)
            self.leave(ve, j)
            for b in range(NB):
                self.nc.vector.tensor_tensor(self.X[:, b, c], self.bank(j, b), self.X[:, b, c],
                                             ALU.add).then_inc(self.freed(S, j), 1)

    def peer(self, l):
        nc, a = self.nc, self.a
        with ExitStack() as ctx:
            N2 = 2 * HEADS
            H = self.sb("peer_h", [P, NB, D], ctx=ctx)
            keys = self.sb("peer_keys", [P, 2, P], ctx=ctx)
            keysT = self.sb("peer_keysT", [P, 2, P], ctx=ctx)
            SC = self.sb("peer_scores", [P, NB, 2 * HEADS, P], ctx=ctx)
            E = self.sb("peer_ids", [P, NB, P], I32, ctx=ctx)
            G = self.sb("peer_gates", [P, NB, P], ctx=ctx)
            side = nc.alloc_semaphore(f"peer_side{l}")

            LISTS = 2 * PAIR
            PICKS = PAIR * TOPK
            v16 = self.sb("top_values", [P, LISTS, TOPK], ctx=ctx)
            i16 = self.sb("top_indices", [P, LISTS, TOPK], U32, ctx=ctx)
            i16f = self.sb("top_indices_f", [P, LISTS, TOPK], ctx=ctx)
            cand = self.sb("pair_sums", [P, PAIR, TOPK * TOPK], ctx=ctx)
            pick = self.sb("pair_picks", [P, PAIR, TOPK, TOPK], ctx=ctx)
            ts = self.sb("pair_scores", [P, PAIR, TOPK], ctx=ctx)
            tp = self.sb("pair_positions", [P, PAIR, TOPK], U32, ctx=ctx)
            part = self.sb("pair_part", [P, 2, PAIR, TOPK], U32, ctx=ctx)
            partf = self.sb("pair_part_f", [P, 2, PAIR, TOPK], ctx=ctx)
            found = self.sb("pair_found", [P, 2, PAIR, TOPK], ctx=ctx)
            idf = self.sb("expert_f", [P, PICKS], ctx=ctx)
            sums = self.sb("gate_sums", [P, PAIR], ctx=ctx)
            rsum = self.sb("gate_rsums", [P, PAIR], ctx=ctx)
            shifted = self.sb("gate_shifted", [P, PAIR, TOPK], ctx=ctx)

            def top16(values, indices, src, n):
                for half in range(2):
                    c = slice(8 * half, 8 * half + 8)
                    for i in range(n):
                        nc.vector.max(values[:, i, c], src[:, i, :])
                    nc.vector.drain()
                    for i in range(n):
                        nc.vector.max_index(indices[:, i, c], values[:, i, c], src[:, i, :])
                    nc.vector.drain()
                    if half == 0:
                        for i in range(n):
                            nc.vector.match_replace(src[:, i, :], values[:, i, c], src[:, i, :], TAKEN)
                        nc.vector.drain()

            def retrieve(ve, S, b, q, count):
                top16(v16, i16, SC[:, b, LISTS * q:LISTS * (q + 1)], LISTS)
                nc.vector.tensor_copy(i16f[:], i16[:])
                v = v16[:].rearrange("p (h s) k -> p s h k", s=2)
                full = [P, PAIR, TOPK, TOPK]
                nc.vector.tensor_tensor(cand[:].rearrange("p h (x y) -> p h x y", x=TOPK),
                                        v[:, 0].unsqueeze(3).to_broadcast(full), v[:, 1].unsqueeze(2).to_broadcast(full), ALU.add)
                nc.vector.drain()
                top16(ts, tp, cand, PAIR)
                nc.vector.tensor_tensor(shifted[:], ts[:], ts[:, :, 0:1].to_broadcast([P, PAIR, TOPK]),
                                        ALU.subtract).then_inc(S.shifted, 1)
                nc.vector.tensor_scalar(part[:, 0], tp[:], 4, None, ALU.logical_shift_right)
                nc.vector.tensor_scalar(part[:, 1], tp[:], 15, None, ALU.bitwise_and)
                nc.vector.drain()
                nc.vector.tensor_copy(partf[:], part[:])
                nc.vector.drain()
                idx = i16f[:].rearrange("p (h s) k -> p s h k", s=2)
                for s in range(2):
                    nc.vector.tensor_tensor(pick[:], partf[:, s].unsqueeze(3).to_broadcast(full),
                                            self.iota16.unsqueeze(1).unsqueeze(1).to_broadcast(full), ALU.is_equal)
                    nc.vector.drain()
                    nc.vector.tensor_tensor(pick[:], pick[:], idx[:, s].unsqueeze(2).to_broadcast(full), ALU.mult)
                    nc.vector.drain()
                    nc.vector.tensor_reduce(found[:, s], pick[:], AX.X, ALU.add)
                    nc.vector.drain()
                nc.vector.scalar_tensor_tensor(idf[:], found[:, 0].rearrange("p h k -> p (h k)"), float(P),
                                               found[:, 1].rearrange("p h k -> p (h k)"), ALU.mult, ALU.add)
                nc.vector.drain()
                c = slice(PICKS * q, PICKS * (q + 1))
                nc.vector.tensor_scalar(E[:, b, c], idf[:], float(l * P * P), None, ALU.add).then_inc(S.ids, 1)
                ve.wait_ge(S.expd, count)
                g = G[:, b, c].rearrange("p (h k) -> p h k", h=PAIR)
                nc.vector.tensor_reduce(sums[:], g, AX.X, ALU.add)
                nc.vector.drain()
                nc.vector.reciprocal(rsum[:], sums[:])
                nc.vector.drain()
                nc.vector.tensor_tensor(g, g, rsum[:].unsqueeze(2).to_broadcast([P, PAIR, TOPK]), ALU.mult)
                nc.vector.drain()

            def exponentials(act, S, b, q, count):
                act.wait_ge(S.shifted, count)
                nc.scalar.activation(G[:, b, PICKS * q:PICKS * (q + 1)], shifted[:].rearrange("p h k -> p (h k)"),
                                     ACT.Exp).then_inc(S.expd, 1)

            with self.stage(
                    "n_ms n_rstd n_xn n_tr n_hT p_free0 p_free1 back back_out keysT keysT_out scores score_out "
                    "queries shifted expd ids dots gelu weights diag", f"peer_q{l}") as (block, S):
                QT = self.sb("peer_qT", [P, 2, LISTS, SEQ], ctx=ctx)
                rows = self.sb("expert_rows", [P, GRING, D], ctx=ctx)
                turn = self.sb("gather_index", [P, 2, GHALF], I32, ctx=ctx)
                part16 = self.sb("dots16", [P, GRING], ctx=ctx)
                dots = self.sb("dots", [P, P], ctx=ctx)
                wts = self.sb("expert_weights", [P, P], ctx=ctx)
                diag = self.sb("weight_diag", [P, 2 * PE_ROWS, P], ctx=ctx)
                acc = self.xn[:, 0, :]
                shift = self.mod[:, 3 * KT:4 * KT]
                parts = HEADS // PAIR
                rounds = P // GRING
                rounds_part = rounds // parts

                def landed(phase, first, i):
                    return i * 16 + 16 * ((l * 2 * NB + phase) * rounds + first + 1)

                def pe_used(b):
                    return (l * NB + b) * 2 * PE_ROWS * rounds + PE_CREDIT

                def ve_used(phase):
                    done = l * 2 * NB + phase
                    return (-(-done // 2) * GHALF + done // 2 * VE_ROWS) * 2 * rounds + VE_CREDIT

                @block.tensor
                def _(pe):
                    def scores(j):
                        pe.wait_ge(S.queries, j + 1)
                        if j == 0:
                            pe.wait_ge(S.keysT_out, 1)
                            pe.wait_ge(S.back_out, 1)
                        if j >= 2:
                            pe.wait_ge(S.score_out, 2 * (j - 1))
                        for b in range(NB):
                            for i in range(LISTS):
                                ins = nc.tensor.matmul(self.PS[:, 4 + 2 * (j % 2) + b, i * P:(i + 1) * P],
                                                       QT[:, j % 2, i, b * P:(b + 1) * P], keysT[:, i % 2, :],
                                                       start=True, stop=True)
                            ins.then_inc(S.scores, 1)

                    self.norm_tensor(pe, S)
                    pe.wait_ge(side, 32)
                    for i in range(2):
                        ins = nc.tensor.transpose(self.PS[:, 3, i * P:(i + 1) * P], keys[:, i, :], self.ident)
                    ins.then_inc(S.keysT, 1)
                    pe.wait_ge(S.n_hT, self.N_HT)
                    for b in range(NB):
                        for g in range(2):
                            for j in range(4):
                                k = 4 * g + j
                                ins = nc.tensor.transpose(self.PS[:, 4 + 2 * b + g, j * P:(j + 1) * P],
                                                          self.hT[:, k, b * P:(b + 1) * P], self.ident)
                    ins.then_inc(S.back, 1)
                    for j in range(parts):
                        self.project(pe, S, [("F", 512)], self.hT, KT, first=j)
                        scores(j)

                    pe.wait_ge(S.p_free0, 4)
                    pe.wait_ge(S.p_free1, 4)
                    for b in range(NB):
                        for h in range(2):
                            nc.tensor.matmul(self.PS[:, 2 * b + h, :], self.onehot[:, SEQ:SEQ + P], self.cst[:, 0:BANK],
                                             start=True, stop=False, skip_group_check=True)
                        with pe.Fori(0, rounds) as i:
                            for d in range(2 * PE_ROWS):
                                u = d // PE_ROWS * GHALF + VE_ROWS + d % PE_ROWS
                                pe.wait_ge(S.diag, i * (2 * PE_ROWS) + (2 * PE_ROWS * rounds * b + d + 1))
                                pe.wait_ge(self.g_landed[u], landed(2 * b + 1, 0, i))
                                for h in range(2):
                                    ins = nc.tensor.matmul(self.PS[:, 2 * b + h, :], diag[:, d, :], rows[:, u, h * BANK:(h + 1) * BANK],
                                                           start=False, stop=False, skip_group_check=True)
                                ins.then_inc(self.g_used_pe, 1)

                @block.scalar
                def _(act):
                    for i, name in enumerate(("peer_k1", "peer_k2")):
                        act.dma_start(keys[:, i, :], a[name][l]).then_inc(side, 16)
                    self.norm_scalar(act, S, self.modA[:, 1, :], shift)
                    act.wait_ge(S.back, 1)
                    nc.scalar.copy(H[:].rearrange("p b (g n) -> p (b g) n", n=BANK), self.PS[:, 4:8, :]).then_inc(S.back_out, 1)

                    def queries(j):
                        self.leave(act, j)
                        if j >= 2:
                            act.wait_ge(S.scores, 2 * (j - 1))
                        for e in range(2):
                            nc.scalar.copy(QT[:, j % 2, 2 * e:2 * e + 2, :].rearrange("p t n -> p (t n)"),
                                           self.bank(j, e)).then_inc(self.freed(S, j), 1)
                        nc.scalar.drain().then_inc(S.queries, 1)

                    def collect(j):
                        for b in range(NB):
                            act.wait_ge(S.scores, 2 * j + b + 1)
                            nc.scalar.copy(SC[:, b, LISTS * j:LISTS * (j + 1)].rearrange("p i n -> p (i n)"),
                                           self.PS[:, 4 + 2 * (j % 2) + b, :]).then_inc(S.score_out, 1)

                    def gelu(b):
                        act.wait_ge(S.dots, b + 1)
                        nc.scalar.activation(wts[:], dots[:], ACT.Gelu_apprx_tanh).then_inc(S.gelu, 1)
                        act.wait_ge(S.weights, b + 1)

                    def diagonals(b, first, n):
                        with act.Fori(0, n) as i:
                            for d in range(2 * PE_ROWS):
                                u = d // PE_ROWS * GHALF + VE_ROWS + d % PE_ROWS
                                act.wait_ge(self.g_used_pe, i * (2 * PE_ROWS) + (pe_used(b) + 2 * PE_ROWS * (first - 1) + d + 1))
                                nc.scalar.activation(diag[:, d, :], self.ident, ACT.Copy,
                                                     scale=wts[:, bass.ds((i + first) * GRING + u, 1)]).then_inc(S.diag, 1)

                    for j in range(parts):
                        queries(j)
                        collect(j)
                        if j >= 1:
                            exponentials(act, S, 0, j - 1, j)
                    exponentials(act, S, 0, parts - 1, parts)
                    gelu(0)
                    for q in range(parts):
                        exponentials(act, S, 1, q, parts + q + 1)
                        diagonals(0, q * rounds_part, rounds_part)
                    gelu(1)
                    diagonals(1, 0, rounds)

                @block.vector
                def _(ve):
                    def products(b, first, n):
                        with ve.Fori(0, n) as i:
                            for u in range(GRING):
                                ve.wait_ge(self.g_landed[u], landed(2 * b, first, i))
                                nc.vector.tensor_tensor_reduce(rows[:, u, :], rows[:, u, :], H[:, b, :], 1.0, 0.0, ALU.mult,
                                                               ALU.add, part16[:, u:u + 1]).then_inc(self.g_used, 1)
                            nc.vector.drain()
                            nc.vector.tensor_copy(dots[:, bass.ds((i + first) * GRING, GRING)], part16[:])
                            nc.vector.drain()

                    def combine(b, first, n):
                        with ve.Fori(0, n) as i:
                            for u in [*range(VE_ROWS), *range(GHALF, GHALF + VE_ROWS)]:
                                ve.wait_ge(self.g_landed[u], landed(2 * b + 1, first, i))
                                nc.vector.scalar_tensor_tensor(acc, rows[:, u, :], wts[:, bass.ds((i + first) * GRING + u, 1)],
                                                               acc, ALU.mult, ALU.add).then_inc(self.g_used, 1)
                                nc.vector.drain()

                    self.norm_vector(ve, S, self.modA[:, 1, :], shift)
                    ve.wait_ge(S.keysT, 1)
                    nc.vector.tensor_copy(keysT[:].rearrange("p i n -> p (i n)"), self.PS[:, 3, 0:2 * P]).then_inc(S.keysT_out, 1)
                    if l == 0:
                        ve.sem_inc(self.g_used, VE_CREDIT)
                        ve.sem_inc(self.g_used_pe, PE_CREDIT)
                    ve.wait_ge(S.score_out, 1)
                    retrieve(ve, S, 0, 0, 1)
                    ve.wait_ge(S.back_out, 1)
                    for q in range(1, parts):
                        ve.wait_ge(S.score_out, 2 * q + 1)
                        retrieve(ve, S, 0, q, q + 1)
                        products(0, (q - 1) * rounds_part, rounds_part)
                    ve.wait_ge(S.score_out, 2 * parts)
                    products(0, rounds - rounds_part, rounds_part)
                    for b in range(NB):
                        if b == 1:
                            products(1, 0, rounds)
                        nc.vector.memset(acc, 0.0)
                        nc.vector.drain().then_inc(S.dots, 1)
                        ve.wait_ge(S.gelu, b + 1)
                        nc.vector.tensor_tensor(wts[:], wts[:], G[:, b, :], ALU.mult)
                        nc.vector.drain().then_inc(S.weights, 1)
                        if b == 0:
                            for q in range(parts):
                                retrieve(ve, S, 1, q, parts + q + 1)
                                combine(b, q * rounds_part, rounds_part)
                        else:
                            combine(b, 0, rounds)
                        ve.wait_ge(self.g_used_pe, pe_used(b + 1))
                        nc.vector.tensor_tensor(acc.rearrange("p (h n) -> p h n", h=2), acc.rearrange("p (h n) -> p h n", h=2),
                                                self.PS[:, 2 * b:2 * b + 2, :], ALU.add)
                        nc.vector.drain()
                        nc.vector.tensor_tensor(acc, acc, self.gate[:, 1, :], ALU.mult)
                        nc.vector.drain()
                        nc.vector.tensor_tensor(self.X[:, b, :], self.X[:, b, :], acc, ALU.add)
                        nc.vector.drain()

                @block.gpsimd
                def _(pool):
                    def gathers(phase, first, n):
                        b, v = phase // 2, phase % 2
                        table = a[("peer_u", "peer_v")[v]].rearrange("l n d -> (l n) d")
                        used = (GHALF, VE_ROWS)[v]
                        if first == 0 and l + phase > 0:
                            pool.wait_ge(self.g_used, ve_used(phase) - (VE_ROWS, GHALF)[v])
                        with pool.Fori(0, n) as i:
                            for half in range(2):
                                pool.wait_ge(self.g_used, i * (2 * used) + (ve_used(phase) + (2 * first + half - 1) * used))
                                if v:
                                    pool.wait_ge(self.g_used_pe, i * (2 * PE_ROWS) + (pe_used(b) + (2 * first + half - 1) * PE_ROWS))
                                else:
                                    pool.wait_ge(self.g_used_pe, pe_used(b) - (1 - half) * PE_ROWS)
                                nc.gpsimd.sem_inc(self.g_turn, 1)
                                nc.gpsimd.tensor_copy(turn[:, half, :], E[:, b, bass.ds((i + first) * GRING + half * GHALF, GHALF)]
                                                      ).then_inc(self.g_index, 1)
                                pool.wait_ge(self.g_index, i * 2 + (2 * ((l * 2 * NB + phase) * rounds + first) + half + 1))
                                nc.gpsimd.sem_inc(self.g_turn, 1)
                                for u in range(half * GHALF, (half + 1) * GHALF):
                                    pool.indirect_dma_start(rows[:, u, :], None, table,
                                                            bass.IndirectOffsetOnAxis(ap=turn[:, half, u % GHALF:u % GHALF + 1], axis=0)
                                                            ).then_inc(self.g_landed[u], 16)

                    self.norm_gpsimd(pool, S)
                    for q in range(parts):
                        pool.wait_ge(S.ids, q + 1)
                        gathers(0, q * rounds_part, rounds_part)
                    gathers(1, 0, rounds)
                    pool.wait_ge(S.ids, 2 * parts)
                    gathers(2, 0, rounds)
                    gathers(3, 0, rounds)

    def pool_conv(self):
        nc, a = self.nc, self.a
        PAD = KERN - 1
        with ExitStack() as ctx:
            u = self.sb("pool_u", [P, 4, 16 + SEQ], ctx=ctx)
            val = self.sb("conv_value", [P, 4, SEQ], ctx=ctx)
            z = self.sb("conv_z", [P, 4, PAD + SEQ], ctx=ctx)
            YT = self.sb("pool_conv_yT", [P, KT, SEQ], ctx=ctx)
            sig = self.sb("conv_sigmoid", [P, 4, SEQ], ctx=ctx)
            pw = self.sb("pool_w", [P, 4, P], ctx=ctx)
            side = nc.alloc_semaphore("pool_w_landed")
            gain = self.col("mix_norm_2")[:, 0:KT]

            with self.stage("n_ms n_rstd n_xn n_tr n_hT p_free0 p_free1 sig", "ab_in") as (block, S):
                @block.tensor
                def _(pe):
                    self.norm_tensor(pe, S)
                    pe.wait_ge(S.n_hT, self.N_HT)
                    self.project(pe, S, [("F", 512)] * 3, self.hT, KT)

                @block.scalar
                def _(act):
                    act.dma_start(pw[:], a["pool_w_2"][0].rearrange("g c d -> c g d")).then_inc(side, 16)
                    self.norm_scalar(act, S, gain, None)
                    self.leave(act, 2)
                    for e in range(2):
                        nc.scalar.activation(sig[:, 2 * e:2 * e + 2, :].rearrange("p t n -> p (t n)"), self.bank(2, e),
                                             ACT.Sigmoid).then_inc(S.sig, 1)

                @block.vector
                def _(ve):
                    nc.vector.memset(u[:, :, 0:16], 0.0)
                    nc.vector.memset(z[:, :, 0:PAD], 0.0)
                    self.norm_vector(ve, S, gain, None)
                    for j, dst in ((0, u[:, :, 16:]), (1, val[:])):
                        self.leave(ve, j)
                        for e in range(2):
                            nc.vector.tensor_copy(dst[:, 2 * e:2 * e + 2, :],
                                                  self.bank(j, e).rearrange("p (t n) -> p t n", t=2)).then_inc(self.freed(S, j), 1)
                    nc.vector.drain()
                    ve.wait_ge(S.sig, 2)
                    nc.vector.tensor_tensor(z[:, :, PAD:], val[:], sig[:], ALU.mult)

                @block.gpsimd
                def _(pool):
                    self.norm_gpsimd(pool, S)

            with self.stage("diag conv_pe pool_in pool_mm pool_out mean_mm centred var_mm c_var c_rstd c_diag c_spread zn conv_out sq") as (block, S):
                W = 16 + SEQ
                s2 = self.sb("sum2", [P, 4, W], ctx=ctx)
                s4 = self.sb("sum4", [P, 4, W], ctx=ctx)
                diff = self.sb("pool_diff", [P, 4, SEQ], ctx=ctx)
                conv = self.sb("conv_out", [P, 4, SEQ], ctx=ctx)
                NDIAG = 8
                diag = self.sb("tap_diag", [P, NDIAG, P], ctx=ctx)
                row = self.sb("chan_rows", [P, SEQ], ctx=ctx)
                sq = sig
                taps = self.col("conv_w_2").rearrange("p (j c) -> p j c", c=4)
                bias = self.col("conv_b_2")

                @block.scalar
                def _(act):
                    n = 0
                    for c in (2, 3):
                        for j in range(KERN):
                            if n >= NDIAG:
                                act.wait_ge(S.conv_pe, n - NDIAG + 1)
                            nc.scalar.activation(diag[:, n % NDIAG, :], self.ident, ACT.Copy, scale=taps[:, j, c:c + 1]).then_inc(S.diag, 1)
                            n += 1
                        act.wait_ge(S.conv_pe, n)
                        nc.scalar.activation(conv[:, c, :], self.PS[:, c - 2, 0:SEQ], ACT.Identity, bias=bias[:, c:c + 1]).then_inc(S.conv_out, 1)
                    g, b = self.col("conv_ln_g_2"), self.col("conv_ln_b_2")
                    act.wait_ge(S.zn, 1)
                    for c in range(4):
                        nc.scalar.activation(YT[:, 4 + c, :], conv[:, c, :], ACT.Silu, bias=b[:, c:c + 1], scale=g[:, c:c + 1])

                @block.tensor
                def _(pe):
                    pe.wait_ge(side, 16)
                    pe.wait_ge(S.pool_in, 1)
                    for g in range(4):
                        ins = nc.tensor.matmul(self.PS[:, 2 + g // 2, (g % 2) * SEQ:(g % 2 + 1) * SEQ], pw[:, g, :], diff[:, g, :],
                                               start=True, stop=True)
                    ins.then_inc(S.pool_mm, 1)
                    n = 0
                    for c in (2, 3):
                        for j in range(KERN):
                            pe.wait_ge(S.diag, n + 1)
                            nc.tensor.matmul(self.PS[:, c - 2, 0:SEQ], diag[:, n % NDIAG, :], z[:, c, j:j + SEQ],
                                             start=(j == 0), stop=(j == KERN - 1)).then_inc(S.conv_pe, 1)
                            n += 1
                    pe.wait_ge(S.conv_out, 4)
                    for c in range(4):
                        ins = nc.tensor.matmul(self.PS[:, 4, 0:SEQ], self.ones, conv[:, c, :], start=(c == 0), stop=(c == 3))
                    ins.then_inc(S.mean_mm, 1)
                    pe.wait_ge(S.sq, 1)
                    for b in range(NB):
                        for c in range(4):
                            ins = nc.tensor.matmul(self.PS[:, 5, b:b + 1], sq[:, c, b * P:(b + 1) * P], self.ones[:, 0:1],
                                                   start=(c == 0), stop=(c == 3))
                    ins.then_inc(S.var_mm, 1)
                    pe.wait_ge(S.c_diag, 1)
                    for b in range(NB):
                        ins = nc.tensor.matmul(self.PS[:, 6, b * P:(b + 1) * P], self.ones, diag[:, b, :], start=True, stop=True)
                    ins.then_inc(S.c_spread, 1)

                @block.vector
                def _(ve):
                    nc.vector.tensor_tensor(s2[:, :, 1:W], u[:, :, 1:W], u[:, :, 0:W - 1], ALU.add)
                    nc.vector.drain()
                    nc.vector.tensor_tensor(s4[:, 1:4, 4:W], s2[:, 1:4, 4:W], s2[:, 1:4, 2:W - 2], ALU.add)
                    nc.vector.drain()
                    nc.vector.tensor_tensor(s2[:, 2:4, 8:W], s4[:, 2:4, 8:W], s4[:, 2:4, 4:W - 4], ALU.add)
                    nc.vector.drain()
                    nc.vector.tensor_tensor(s4[:, 3, 16:W], s2[:, 3, 16:W], s2[:, 3, 8:W - 8], ALU.add)
                    nc.vector.drain()
                    inv = self.invcount.rearrange("p (g n) -> p g n", g=4)
                    for g, s in enumerate((s2, s4, s2, s4)):
                        nc.vector.tensor_tensor(s[:, g, 16:32], s[:, g, 16:32], inv[:, g, :], ALU.mult)
                        nc.vector.tensor_scalar(s[:, g, 32:W], s[:, g, 32:W], 1.0 / 2 ** (g + 1), None, ALU.mult)
                    nc.vector.drain()
                    for g, s in enumerate((s2, s4, s2, s4)):
                        ins = nc.vector.tensor_tensor(diff[:, g, :], s[:, g, 16:W], u[:, g, 16:W], ALU.subtract)
                    ins.then_inc(S.pool_in, 1)
                    for j in range(KERN):
                        for c in range(2):
                            if j == 0:
                                nc.vector.tensor_scalar(conv[:, c, :], z[:, c, 0:SEQ], taps[:, 0, c:c + 1], bias[:, c:c + 1], ALU.mult, ALU.add)
                            else:
                                nc.vector.scalar_tensor_tensor(conv[:, c, :], z[:, c, j:j + SEQ], taps[:, j, c:c + 1], conv[:, c, :],
                                                               ALU.mult, ALU.add)
                        nc.vector.drain()
                    nc.vector.drain().then_inc(S.conv_out, 2)
                    ve.wait_ge(S.pool_mm, 1)
                    scale = self.col("pool_scale_2")
                    for g in range(4):
                        nc.vector.tensor_scalar(YT[:, g, :], self.PS[:, 2 + g // 2, (g % 2) * SEQ:(g % 2 + 1) * SEQ],
                                                scale[:, g:g + 1], None, ALU.mult)
                    ve.wait_ge(S.mean_mm, 1)
                    nc.vector.tensor_scalar(row[:], self.PS[:, 4, 0:SEQ], 1.0 / HALF, None, ALU.mult)
                    nc.vector.drain()
                    nc.vector.tensor_tensor(conv[:], conv[:], row[:].unsqueeze(1).to_broadcast([P, 4, SEQ]), ALU.subtract)
                    nc.vector.drain()
                    nc.vector.tensor_tensor(sq[:], conv[:], conv[:], ALU.mult).then_inc(S.sq, 1)
                    ve.wait_ge(S.var_mm, 1)
                    nc.vector.tensor_scalar(self.ms[:], self.PS[:, 5, 0:NB], 1.0 / HALF, EPS, ALU.mult, ALU.add).then_inc(S.c_var, 1)
                    ve.wait_ge(S.c_rstd, 1)
                    for b in range(NB):
                        ins = nc.vector.tensor_scalar(diag[:, b, :], self.ident, self.rstd[:, b:b + 1], None, ALU.mult)
                    ins.then_inc(S.c_diag, 1)
                    ve.wait_ge(S.c_spread, 1)
                    nc.vector.tensor_tensor(conv[:], conv[:], self.PS[:, 6, 0:SEQ].unsqueeze(1).to_broadcast([P, 4, SEQ]), ALU.mult).then_inc(S.zn, 1)

                @block.gpsimd
                def _(pool):
                    pool.wait_ge(S.c_var, 1)
                    nc.gpsimd.tensor_tensor(self.rstd[:], self.ms[:], self.neghalf[:, 0:NB], ALU.pow).then_inc(S.c_rstd, 1)

            self.output_projection("ab_out", YT)

    def output_projection(self, name, YT):
        with self.stage("p_free0 p_free1", name) as (block, S):
            @block.tensor
            def _(pe):
                self.project(pe, S, [("T", 512)] * 2, YT, KT)

            @block.vector
            def _(ve):
                self.plain_residual(ve, S)

    def attention(self, block, S, ctx, heads, dh, QT, KT_, V, mask, bias, YT):
        nc = self.nc
        W3 = 3 * P
        lg = self.sb("att_logits", [P, 2, W3], ctx=ctx)
        nmax = self.sb("att_negmax", [P, 2, NB], ctx=ctx)
        sums = self.sb("att_sums", [P, 2, NB], ctx=ctx)
        rsum = self.sb("att_rsums", [P, 2, NB], ctx=ctx)
        pT = self.sb("att_probsT", [P, 2, W3], ctx=ctx)
        per = P // dh

        def rows(h):
            return slice(dh * (h % per), dh * (h % per) + dh)

        @block.tensor
        def _(pe):
            def scores(h):
                L, r, t = self.PS[:, h % 2, :], rows(h), h // per
                if h >= 2:
                    pe.wait_ge(S.a_masked, h - 1)
                nc.tensor.matmul(L[:, 0:P], QT[r, t, 0:P], KT_[r, t, 0:P], start=True, stop=(bias is None), skip_group_check=True)
                ins = nc.tensor.matmul(L[:, P:W3], QT[r, t, P:SEQ], KT_[r, t, :], start=False, stop=(bias is None), skip_group_check=True)
                if bias is not None:
                    nc.tensor.matmul(L[:, 0:P], self.anti, bias[:, h, P:SEQ], start=False, stop=True, skip_group_check=True)
                    ins = nc.tensor.matmul(L[:, P:W3], self.anti, bias[:, h, :], start=False, stop=True, skip_group_check=True)
                ins.then_inc(S.a_scores, 1)

            def turn(h):
                pe.wait_ge(S.a_norm, h + 1)
                if h >= 2:
                    pe.wait_ge(S.a_turned, h - 1)
                T, p = self.PS[:, 2 + h % 2, :], lg[:, h % 2, :]
                nc.tensor.transpose(T[:, 0:P], p[:, 0:P], self.ident)
                nc.tensor.transpose(T[:, P:SEQ], p[:, P:SEQ], self.ident)
                nc.tensor.transpose(T[:, SEQ:W3], p[:, SEQ:W3], self.ident).then_inc(S.a_turn, 1)

            def values(h):
                pe.wait_ge(S.a_turned, h + 1)
                if h >= 2:
                    pe.wait_ge(S.a_out, h - 1)
                O, c = self.PS[rows(h), 4 + h % 2, 0:SEQ], slice(dh * h, dh * h + dh)
                nc.tensor.matmul(O, V[:, 0, c], pT[:, h % 2, 0:SEQ], start=True, stop=False, skip_group_check=True)
                nc.tensor.matmul(O[:, P:SEQ], V[:, 1, c], pT[:, h % 2, SEQ:W3], start=False, stop=True,
                                 skip_group_check=True).then_inc(S.a_val, 1)

            scores(0)
            for h in range(heads):
                if h + 1 < heads:
                    scores(h + 1)
                if h >= 1:
                    values(h - 1)
                turn(h)
            values(heads - 1)

        @block.vector
        def _(ve):
            def masked(h):
                i = h % 2
                ve.wait_ge(S.a_scores, h + 1)
                if h >= 2:
                    ve.wait_ge(S.a_turn, h - 1)
                nc.vector.tensor_tensor(lg[:, i, :], self.PS[:, i, 0:W3], mask, ALU.add).then_inc(S.a_masked, 1)
                nc.vector.drain()
                nc.vector.tensor_reduce(nmax[:, i, 0:1], lg[:, i, 0:P], AX.X, ALU.max, negate=True)
                nc.vector.tensor_reduce(nmax[:, i, 1:2], lg[:, i, P:W3], AX.X, ALU.max, negate=True)
                nc.vector.drain().then_inc(S.a_max, 1)

            def normalised(h):
                i = h % 2
                ve.wait_ge(S.a_exp, h + 1)
                nc.vector.reciprocal(rsum[:, i, :], sums[:, i, :])
                nc.vector.drain()
                nc.vector.tensor_scalar(lg[:, i, 0:P], lg[:, i, 0:P], rsum[:, i, 0:1], None, ALU.mult)
                nc.vector.tensor_scalar(lg[:, i, P:W3], lg[:, i, P:W3], rsum[:, i, 1:2], None, ALU.mult)
                nc.vector.drain().then_inc(S.a_norm, 1)

            masked(0)
            for h in range(heads):
                if h + 1 < heads:
                    masked(h + 1)
                normalised(h)
                if h >= 1:
                    self.attention_out(ve, S, nc.vector.tensor_copy, h - 1, rows, per, YT)
            self.attention_out(ve, S, nc.vector.tensor_copy, heads - 1, rows, per, YT)

        @block.scalar
        def _(act):
            def turned(h):
                act.wait_ge(S.a_turn, h + 1)
                if h >= 2:
                    act.wait_ge(S.a_val, h - 1)
                nc.scalar.copy(pT[:, h % 2, :], self.PS[:, 2 + h % 2, 0:W3]).then_inc(S.a_turned, 1)

            for h in range(heads):
                i = h % 2
                act.wait_ge(S.a_max, h + 1)
                nc.scalar.activation(lg[:, i, 0:P], lg[:, i, 0:P], ACT.Exp, bias=nmax[:, i, 0:1], accum_out=sums[:, i, 0:1])
                nc.scalar.activation(lg[:, i, P:W3], lg[:, i, P:W3], ACT.Exp, bias=nmax[:, i, 1:2], accum_out=sums[:, i, 1:2])
                nc.scalar.drain().then_inc(S.a_exp, 1)
                if h >= 1:
                    turned(h - 1)
            turned(heads - 1)

    ATT = "a_scores a_masked a_max a_exp a_norm a_turn a_turned a_val a_out"

    def attention_out(self, eng, S, copy, h, rows, per, YT):
        eng.wait_ge(S.a_val, h + 1)
        copy(YT[rows(h), h // per, :], self.PS[rows(h), 4 + h % 2, 0:SEQ]).then_inc(S.a_out, 1)

    def sparse_attention(self):
        nc, a = self.nc, self.a
        W3 = 3 * P
        AH = 16
        with ExitStack() as ctx:
            QT = self.sb("dsa_qT", [P, KT, SEQ], ctx=ctx)
            KT_ = self.sb("dsa_kT", [P, KT, SEQ], ctx=ctx)
            V = self.sb("dsa_v", [P, NB, D], ctx=ctx)
            QI = self.sb("dsa_qiT", [P, 4, SEQ], ctx=ctx)
            KI = self.sb("dsa_kiT", [P, SEQ], ctx=ctx)
            WI = self.sb("dsa_wi", [P, NB, 8], ctx=ctx)
            mask = self.sb("dsa_mask", [P, W3], ctx=ctx)
            B = self.sb("dsa_bias", [P, AH, SEQ], ctx=ctx)
            rb = self.sb("rel_bias", [32, AH], ctx=ctx)
            rbT = self.sb("rel_bias_by_distance", [AH, 384], ctx=ctx)
            scratch = nc.dram_tensor("rel_bias_scratch", [AH, 384], F32, kind="Internal").ap()
            side = nc.alloc_semaphore("dsa_side")
            gain = self.col("mix_norm_2")[:, KT:2 * KT]

            with self.stage("n_ms n_rstd n_xn n_tr n_hT p_free0 p_free1 rb rb_out", "c_in") as (block, S):
                jobs = [("F", 512)] * 4 + [("T", 512)] * 2 + [("F", 512)]

                @block.tensor
                def _(pe):
                    self.norm_tensor(pe, S)
                    pe.wait_ge(S.n_hT, self.N_HT)
                    pe.wait_ge(side, 16)
                    nc.tensor.matmul(self.PS[0:AH, 4, 0:384], rb[:], self.onehot[0:32, :], start=True, stop=True).then_inc(S.rb, 1)
                    self.project(pe, S, jobs, self.hT, KT)
                    for g in range(2):
                        slot = self.take(pe)[:, 0:4 * 136].rearrange("p (k n) -> p k n", k=4)
                        for kk in range(4):
                            k = 4 * g + kk
                            st, sp = k == 0, k == KT - 1
                            nc.tensor.matmul(self.PS[:, 5, 0:SEQ], slot[:, kk, 0:P], self.hT[:, k, :], start=st, stop=sp)
                            for b in range(NB):
                                ins = nc.tensor.matmul(self.PS[:, 6 + b, 0:8], self.hT[:, k, b * P:(b + 1) * P],
                                                       slot[:, kk, P:P + 8], start=st, stop=sp)
                        ins.then_inc(self.w_used, 1)

                @block.scalar
                def _(act):
                    act.dma_start(rb[:], a["rel_bias_2"]).then_inc(side, 16)
                    self.norm_scalar(act, S, gain, None)
                    act.wait_ge(S.rb, 1)
                    nc.scalar.copy(rbT[:], self.PS[0:AH, 4, 0:384]).then_inc(S.rb_out, 1)
                    act.wait_ge(S.rb_out, 1)
                    act.dma_start(scratch, rbT[:]).then_inc(side, 16)
                    act.wait_ge(side, 32)
                    act.dma_start(B[:], bass.AP(scratch.tensor, 0, [[1, P], [384, AH], [1, SEQ]])).then_inc(side, 16)
                    for j in (1, 3, 5):
                        dst = {1: QT[:, 4:8], 3: KT_[:, 4:8], 5: V[:, :, BANK:]}[j]
                        self.leave(act, j)
                        for e in range(2):
                            if j == 5:
                                ins = nc.scalar.copy(dst[:, e, :], self.bank(j, e))
                            else:
                                ins = nc.scalar.mul(dst[:, 2 * e:2 * e + 2, :].rearrange("p t n -> p (t n)"), self.bank(j, e),
                                                    0.125 if j == 1 else 1.0)
                            ins.then_inc(self.freed(S, j), 1)

                @block.vector
                def _(ve):
                    self.norm_vector(ve, S, gain, None)
                    for j in (0, 2, 4, 6):
                        dst = {0: QT[:, 0:4], 2: KT_[:, 0:4], 4: V[:, :, 0:BANK], 6: QI[:]}[j]
                        self.leave(ve, j)
                        for e in range(2):
                            if j == 4:
                                ins = nc.vector.tensor_copy(dst[:, e, :], self.bank(j, e))
                            else:
                                ins = nc.vector.tensor_scalar(dst[:, 2 * e:2 * e + 2, :].rearrange("p t n -> p (t n)"), self.bank(j, e),
                                                              0.125 if j == 0 else 1.0, None, ALU.mult)
                            ins.then_inc(self.freed(S, j), 1)
                    self.leave(ve, 7)
                    nc.vector.tensor_copy(KI[:], self.PS[:, 5, 0:SEQ])
                    nc.vector.tensor_copy(WI[:], self.PS[:, 6:8, 0:8])

                @block.gpsimd
                def _(pool):
                    self.norm_gpsimd(pool, S)

            with self.stage("index relu used") as (block, S):
                rel = self.sb("dsa_rel", [P, 2, W3], ctx=ctx)
                sc = self.sb("dsa_scores", [P, W3], ctx=ctx)
                top = self.sb("dsa_top", [P, NB, 8], ctx=ctx)

                @block.tensor
                def _(pe):
                    for h in range(8):
                        r, t, L = slice(64 * (h % 2), 64 * (h % 2) + 64), h // 2, self.PS[:, h % 4, :]
                        if h >= 4:
                            pe.wait_ge(S.relu, h - 3)
                        nc.tensor.matmul(L[:, 0:P], QI[r, t, 0:P], KI[r, 0:P], start=True, stop=True)
                        nc.tensor.matmul(L[:, P:W3], QI[r, t, P:SEQ], KI[r, :], start=True, stop=True).then_inc(S.index, 1)

                @block.scalar
                def _(act):
                    for h in range(8):
                        act.wait_ge(S.index, h + 1)
                        if h >= 2:
                            act.wait_ge(S.used, h - 1)
                        nc.scalar.activation(rel[:, h % 2, :], self.PS[:, h % 4, 0:W3], ACT.Relu).then_inc(S.relu, 1)

                @block.vector
                def _(ve):
                    parts = ((0, slice(0, P)), (1, slice(P, W3)))
                    for h in range(8):
                        ve.wait_ge(S.relu, h + 1)
                        for b, c in parts:
                            if h == 0:
                                nc.vector.tensor_scalar(sc[:, c], rel[:, 0, c], WI[:, b, 0:1], None, ALU.mult)
                            else:
                                nc.vector.scalar_tensor_tensor(sc[:, c], rel[:, h % 2, c], WI[:, b, h:h + 1], sc[:, c], ALU.mult, ALU.add)
                        nc.vector.drain().then_inc(S.used, 1)
                    nc.vector.scalar_tensor_tensor(sc[:], sc[:], float(512 ** -0.5), self.causal3_add, ALU.mult, ALU.add)
                    nc.vector.drain()
                    for _ in range(DSA_TOPK // 8):
                        for b, c in parts:
                            nc.vector.max(top[:, b, :], sc[:, c])
                        nc.vector.drain()
                        for b, c in parts:
                            nc.vector.match_replace(sc[:, c], top[:, b, :], sc[:, c], TAKEN)
                        nc.vector.drain()
                    nc.vector.tensor_scalar(mask[:], sc[:], 0.5 * TAKEN, None, ALU.is_le)
                    nc.vector.drain()
                    nc.vector.tensor_scalar(mask[:], mask[:], 1.0, -NEG, ALU.subtract, ALU.mult)
                    nc.vector.drain()
                    nc.vector.tensor_tensor(mask[:], mask[:], self.causal3_add, ALU.add)

            YT = self.sb("dsa_yT", [P, KT, SEQ], ctx=ctx)
            with self.stage(self.ATT) as (block, S):
                @block.tensor
                def _(pe):
                    pe.wait_ge(side, 48)

                self.attention(block, S, ctx, AH, 64, QT, KT_, V, mask[:], B, YT)
            self.output_projection("c_out", YT)

    def turn_plain(self, pe, S, src):
        for b in range(NB):
            for g in range(2):
                for j in range(4):
                    k = 4 * g + j
                    ins = self.nc.tensor.transpose(self.PS[:, 4 + 2 * b + g, j * P:(j + 1) * P],
                                                   src[:, b, k * P:(k + 1) * P], self.ident)
                ins.then_inc(S.n_tr, 1)

    def hybrid(self):
        nc = self.nc
        with ExitStack() as ctx:
            YS = self.sb("ssm_branch", [P, NB, D], ctx=ctx)
            with ExitStack() as inner:
                self.mamba(inner, YS)
            with ExitStack() as inner:
                self.moba(inner, YS)

    def mamba(self, ctx, YS):
        nc, a = self.nc, self.a
        XS = self.sb("ssm_x", [P, NB, SSM_D], ctx=ctx)
        with ExitStack() as scan:
            CO = self.sb("ssm_conv", [P, 32, SEQ], ctx=scan)
            DT = self.sb("ssm_dt", [P, NB, SSM_H], ctx=scan)
            DA = self.sb("ssm_da", [P, NB, SSM_H], ctx=scan)
            rows = self.sb("ssm_rows", [P, 3, SSM_H], ctx=scan)
            side = nc.alloc_semaphore("ssm_rows_landed")

            with ExitStack() as inner, self.stage("n_tr n_hT p_free0 p_free1 raw conv dt1 dt2 dt3 aexp", "ssm_in") as (block, S):
                XB = self.sb("ssm_raw", [P, 2, 4, 3 + SEQ], ctx=inner)
                dta = self.sb("ssm_dt_abs", [P, NB, SSM_H], ctx=inner)
                ea = self.sb("ssm_ea", [P, SSM_H], ctx=inner)
                taps = self.col("conv_w_3").rearrange("p (j c) -> p j c", c=32)
                bias = self.col("conv_b_3")

                @block.tensor
                def _(pe):
                    self.turn_plain(pe, S, self.X)
                    pe.wait_ge(S.n_hT, self.N_HT)
                    self.project(pe, S, [("F", 512)] * 8 + [("T", SSM_H)], self.hT, KT)

                @block.scalar
                def _(act):
                    for i, name in enumerate(("dt_bias_3", "a_log_3", "d_skip_3")):
                        act.dma_start(rows[:, i, :], a[name].partition_broadcast(P)).then_inc(side, 16)
                    self.copy_tiles(act, nc.scalar.copy, S, 0)

                    def silu(j):
                        act.wait_ge(S.conv, j + 1)
                        c = CO[:, 4 * j:4 * j + 4, :]
                        nc.scalar.activation(c, c, ACT.Silu)

                    for j in range(8):
                        self.leave(act, j)
                        if j >= 2:
                            act.wait_ge(S.conv, j - 1)
                        for e in range(2):
                            nc.scalar.copy(XB[:, j % 2, 2 * e:2 * e + 2, 3:], self.bank(j, e).rearrange("p (t n) -> p t n", t=2)
                                           ).then_inc(self.freed(S, j), 1)
                        nc.scalar.drain().then_inc(S.raw, 1)
                        if j >= 1:
                            silu(j - 1)
                    silu(7)
                    act.wait_ge(S.dt1, 1)
                    nc.scalar.activation(dta[:], DT[:], ACT.Abs)
                    nc.scalar.drain()
                    nc.scalar.activation(dta[:], dta[:], ACT.Exp, scale=-1.0)
                    nc.scalar.drain()
                    nc.scalar.activation(dta[:], dta[:], ACT.Ln, bias=1.0).then_inc(S.dt2, 1)
                    act.wait_ge(side, 48)
                    nc.scalar.activation(ea[:], rows[:, 1, :], ACT.Exp).then_inc(S.aexp, 1)

                @block.vector
                def _(ve):
                    nc.vector.memset(XB[:, :, :, 0:3], 0.0)
                    self.copy_tiles(ve, nc.vector.tensor_copy, S, 1)
                    nc.vector.drain()
                    for j in range(8):
                        ve.wait_ge(S.raw, j + 1)
                        for tap in range(4):
                            for t in range(4):
                                c = 4 * j + t
                                src = XB[:, j % 2, t, tap:tap + SEQ]
                                if tap == 0:
                                    nc.vector.tensor_scalar(CO[:, c, :], src, taps[:, 0, c:c + 1], bias[:, c:c + 1], ALU.mult, ALU.add)
                                else:
                                    nc.vector.scalar_tensor_tensor(CO[:, c, :], src, taps[:, tap, c:c + 1], CO[:, c, :], ALU.mult, ALU.add)
                            ins = nc.vector.drain()
                        ins.then_inc(S.conv, 1)
                    self.leave(ve, 8)
                    ve.wait_ge(side, 48)
                    for b in range(NB):
                        nc.vector.tensor_tensor(DT[:, b, :], self.PS[:, b, 0:SSM_H], rows[:, 0, :], ALU.add)
                    nc.vector.drain().then_inc(S.dt1, 1)
                    ve.wait_ge(S.dt2, 1)
                    nc.vector.scalar_tensor_tensor(DT[:], DT[:], 0.0, dta[:], ALU.max, ALU.add)
                    nc.vector.drain()
                    ve.wait_ge(S.aexp, 1)
                    for b in range(NB):
                        nc.vector.scalar_tensor_tensor(DA[:, b, :], DT[:, b, :], -1.0, ea[:], ALU.mult, ALU.mult)

            XD = self.sb("ssm_xdt", [P, NB, SSM_D], ctx=scan)
            heads = lambda t: t.rearrange("p (h c) -> p h c", c=SSM_P)
            wide = [P, SSM_H, SSM_P]
            BTK = self.sb("ssm_B_tok", [P, SSM_G, P], ctx=scan)
            with self.stage("x_turned x_out b_turned done") as (block, S):
                @block.tensor
                def _(pe):
                    for b in range(NB):
                        for g in range(4):
                            for j in range(4):
                                ins = nc.tensor.transpose(self.PS[:, 4 * b + g, j * P:(j + 1) * P],
                                                          CO[:, 4 * g + j, b * P:(b + 1) * P], self.ident)
                        ins.then_inc(S.x_turned, 1)
                    pe.wait_ge(S.x_out, 1)
                    for g in range(SSM_G):
                        ins = nc.tensor.transpose(self.PS[:, g // 4, (g % 4) * P:(g % 4 + 1) * P], CO[:, 16 + g, 0:P], self.ident)
                    ins.then_inc(S.b_turned, 1)

                @block.scalar
                def _(act):
                    act.wait_ge(S.x_turned, 1)
                    nc.scalar.copy(XS[:, 0, :].rearrange("p (g n) -> p g n", g=4), self.PS[:, 0:4, :]).then_inc(S.x_out, 1)
                    act.wait_ge(S.b_turned, 1)
                    nc.scalar.copy(BTK[:].rearrange("p (g i) n -> p g (i n)", g=2), self.PS[:, 0:2, :])

                @block.vector
                def _(ve):
                    ve.wait_ge(S.x_turned, 2)
                    nc.vector.tensor_copy(XS[:, 1, :].rearrange("p (g n) -> p g n", g=4), self.PS[:, 4:8, :])
                    nc.vector.drain()
                    ve.wait_ge(S.x_out, 1)
                    for b in range(NB):
                        nc.vector.tensor_tensor(heads(XD[:, b, :]), heads(XS[:, b, :]), DT[:, b, :].unsqueeze(2).to_broadcast(wide), ALU.mult)
                    nc.vector.drain()
                    for b in range(NB):
                        nc.vector.tensor_tensor(heads(XS[:, b, :]), heads(XS[:, b, :]), rows[:, 2, :].unsqueeze(2).to_broadcast(wide), ALU.mult)

            with ExitStack() as inner, self.stage(
                    "cums cum_exp decayed states states_out0 states_out cb cbm lhs seg segx m y y_out") as (block, S):
                ecum = self.sb("ssm_exp_cum", [P, 2, SSM_H], ctx=inner)
                XDD = self.sb("ssm_xdt_decayed", [P, SSM_D], ctx=inner)
                ST = self.sb("ssm_state", [P, SSM_G, SSM_R * SSM_P], ctx=inner)
                cbm = self.sb("ssm_cb", [P, 2, P], ctx=inner)
                lhs = self.sb("ssm_seg_lhs", [P, 2, SSM_R, P], ctx=inner)
                ex = self.sb("ssm_seg_exp", [P, 2, SSM_R, P], ctx=inner)
                inter = self.sb("ssm_inter", [P, SSM_R * SSM_P], ctx=inner)
                W = SSM_R * SSM_P
                work = [(c, g) for c in range(NB) for g in range(SSM_G)]

                @block.gpsimd
                def _(pool):
                    for n, (c, g) in enumerate(work):
                        if n >= 2:
                            pool.wait_ge(S.seg, n - 1)
                        for r in range(SSM_R):
                            h = SSM_R * g + r
                            ins = nc.gpsimd.tensor_scalar(lhs[:, n % 2, r, :], self.after, DA[:, c, h:h + 1], None, ALU.mult)
                        ins.then_inc(S.lhs, 1)

                @block.tensor
                def _(pe):
                    nc.tensor.matmul(self.PS[:, 6, 0:SSM_H], self.after, DA[:, 0, :], start=True, stop=True)
                    nc.tensor.matmul(self.PS[:, 6, SSM_H:2 * SSM_H], self.upto, DA[:, 1, :], start=True, stop=True).then_inc(S.cums, 1)

                    def first(n):
                        c, g = work[n]
                        t = slice(c * P, (c + 1) * P)
                        if n >= 2:
                            pe.wait_ge(S.cbm, n - 1)
                            pe.wait_ge(S.segx, n - 1)
                        nc.tensor.matmul(self.PS[:, n % 2, 0:P], CO[:, 16 + g, t], CO[:, 24 + g, t], start=True, stop=True).then_inc(S.cb, 1)
                        pe.wait_ge(S.lhs, n + 1)
                        for r in range(SSM_R):
                            ins = nc.tensor.matmul(self.PS[:, 2 + n % 2, r * P:(r + 1) * P], lhs[:, n % 2, r, :], self.upto,
                                                   start=True, stop=True)
                        ins.then_inc(S.seg, 1)

                    def second(n):
                        c, g = work[n]
                        pe.wait_ge(S.m, n + 1)
                        if n >= 2:
                            pe.wait_ge(S.y_out, n - 1)
                        if n == SSM_G:
                            pe.wait_ge(S.states_out, 1)
                        Yb = self.PS[:, 4 + n % 2, :]
                        for r in range(SSM_R):
                            q = (SSM_R * g + r) * SSM_P
                            ins = nc.tensor.matmul(Yb[:, r * SSM_P:(r + 1) * SSM_P], ex[:, n % 2, r, :], XD[:, c, q:q + SSM_P],
                                                   start=True, stop=True)
                        if c == 1:
                            ins = nc.tensor.matmul(Yb[:, W:2 * W], CO[:, 24 + g, P:SEQ], ST[:, g, :], start=True, stop=True)
                        ins.then_inc(S.y, 1)

                    first(0)
                    for n in range(len(work)):
                        if n + 1 < len(work):
                            first(n + 1)
                        second(n)
                        if n < SSM_G:
                            if n == 0:
                                pe.wait_ge(S.decayed, 1)
                            if n >= 2:
                                pe.wait_ge(S.states_out0, n - 1)
                            nc.tensor.matmul(self.PS[:, 6 + n % 2, 0:W], BTK[:, n, :], XDD[:, n * W:(n + 1) * W], start=True,
                                             stop=True).then_inc(S.states, 1)

                @block.scalar
                def _(act):
                    act.wait_ge(S.cums, 1)
                    nc.scalar.activation(ecum[:].rearrange("p i h -> p (i h)"), self.PS[:, 6, 0:2 * SSM_H], ACT.Exp).then_inc(S.cum_exp, 1)
                    for n in range(len(work)):
                        act.wait_ge(S.seg, n + 1)
                        if n >= 2:
                            act.wait_ge(S.y, n - 1)
                        nc.scalar.activation(ex[:, n % 2].rearrange("p r n -> p (r n)"), self.PS[:, 2 + n % 2, :], ACT.Exp).then_inc(S.segx, 1)
                        if n < SSM_G:
                            act.wait_ge(S.states, n + 1)
                            ins = nc.scalar.copy(ST[:, n, :], self.PS[:, 6 + n % 2, 0:W]).then_inc(S.states_out0, 1)
                            if n == SSM_G - 1:
                                nc.scalar.drain().then_inc(S.states_out, 1)

                @block.vector
                def _(ve):
                    ve.wait_ge(S.cum_exp, 1)
                    nc.vector.tensor_tensor(heads(XDD[:]), heads(XD[:, 0, :]), ecum[:, 0, :].unsqueeze(2).to_broadcast(wide), ALU.mult
                                            ).then_inc(S.decayed, 1)

                    def weights(n):
                        ve.wait_ge(S.cb, n + 1)
                        nc.vector.tensor_tensor(cbm[:, n % 2, :], self.PS[:, n % 2, 0:P], self.upto, ALU.mult).then_inc(S.cbm, 1)
                        nc.vector.drain()
                        ve.wait_ge(S.segx, n + 1)
                        nc.vector.tensor_tensor(ex[:, n % 2], ex[:, n % 2], cbm[:, n % 2, :].unsqueeze(1).to_broadcast([P, SSM_R, P]),
                                                ALU.mult).then_inc(S.m, 1)

                    def collect(n):
                        c, g = work[n]
                        ve.wait_ge(S.y, n + 1)
                        out = XS[:, c, g * W:(g + 1) * W]
                        Yb = self.PS[:, 4 + n % 2, :]
                        if c == 1:
                            h4 = ecum[:, 1, SSM_R * g:SSM_R * (g + 1)].unsqueeze(2).to_broadcast([P, SSM_R, SSM_P])
                            nc.vector.tensor_tensor(heads(inter[:]), heads(Yb[:, W:2 * W]), h4, ALU.mult)
                        nc.vector.tensor_tensor(out, out, Yb[:, 0:W], ALU.add).then_inc(S.y_out, 1)
                        if c == 1:
                            nc.vector.drain()
                            nc.vector.tensor_tensor(out, out, inter[:], ALU.add)
                            nc.vector.drain()

                    weights(0)
                    for n in range(len(work)):
                        if n + 1 < len(work):
                            weights(n + 1)
                        collect(n)

        YT = self.sb("ssm_yT", [P, 16, SEQ], ctx=ctx)
        with ExitStack() as inner, self.stage("p_free0 p_free1 z z_used g_ms g_rstd g_y turned0 turned1 out0 out1", "ssm_z") as (block, S):
            Z = self.sb("ssm_silu_z", [P, 2, NB, BANK], ctx=inner)
            gms = self.sb("ssm_group_ms", [P, NB * SSM_G], ctx=inner)
            grs = self.sb("ssm_group_rstd", [P, NB * SSM_G], ctx=inner)
            junk = self.sb("junk", [P, 256], ctx=inner)
            w = self.col("ssm_norm_w_3")
            groups = XS[:].rearrange("p b (g n) -> p (b g) n", g=SSM_G)

            @block.tensor
            def _(pe):
                self.project(pe, S, [("T", 512)] * 4, self.hT, KT)
                pe.wait_ge(S.g_y, 1)
                for i in range(8):
                    b, g = i // 4, i % 4
                    for j in range(4):
                        k = 4 * g + j
                        ins = nc.tensor.transpose(self.PS[:, 4 + i % 4, j * P:(j + 1) * P], XS[:, b, k * P:(k + 1) * P], self.ident)
                    ins.then_inc((S.turned0, S.turned1)[i % 2], 1)
                    if i == 3:
                        pe.wait_ge(S.out0, 2)
                        pe.wait_ge(S.out1, 2)

            def turned(eng, ops, odd):
                for i in range(odd, 8, 2):
                    b, g = i // 4, i % 4
                    eng.wait_ge((S.turned0, S.turned1)[odd], i // 2 + 1)
                    for j in range(4):
                        k = 4 * g + j
                        out, src = YT[:, k, b * P:(b + 1) * P], self.PS[:, 4 + i % 4, j * P:(j + 1) * P]
                        if odd:
                            ins = ops.tensor_scalar(out, src, w[:, k:k + 1], None, ALU.mult)
                        else:
                            ins = ops.activation(out, src, ACT.Copy, scale=w[:, k:k + 1])
                    ins.then_inc((S.out0, S.out1)[odd], 1)

            @block.scalar
            def _(act):
                for j in range(4):
                    self.leave(act, j)
                    if j >= 2:
                        act.wait_ge(S.z_used, j - 1)
                    for e in range(2):
                        nc.scalar.activation(Z[:, j % 2, e, :], self.bank(j, e), ACT.Silu).then_inc(self.freed(S, j), 1)
                    nc.scalar.drain().then_inc(S.z, 1)
                turned(act, nc.scalar, 0)

            @block.vector
            def _(ve):
                for j in range(4):
                    ve.wait_ge(S.z, j + 1)
                    c = slice(j * BANK, (j + 1) * BANK)
                    nc.vector.tensor_tensor(XS[:, :, c], XS[:, :, c], Z[:, j % 2], ALU.mult).then_inc(S.z_used, 1)
                nc.vector.drain()
                for i in range(NB * SSM_G):
                    nc.vector.tensor_tensor_reduce(self.xn[:].rearrange("p b (g n) -> p (b g) n", n=256)[:, i % 8, :] if i < 8 else
                                                   YT[:, i - 8, :], groups[:, i, :], groups[:, i, :], 1.0 / 256,
                                                   LN_EPS, ALU.mult, ALU.add, gms[:, i:i + 1])
                nc.vector.drain().then_inc(S.g_ms, 1)
                ve.wait_ge(S.g_rstd, 1)
                nc.vector.tensor_tensor(groups, groups, grs[:].unsqueeze(2).to_broadcast([P, NB * SSM_G, 256]), ALU.mult).then_inc(S.g_y, 1)
                turned(ve, nc.vector, 1)

            @block.gpsimd
            def _(pool):
                pool.wait_ge(S.g_ms, 1)
                nc.gpsimd.tensor_tensor(grs[:], gms[:], self.neghalf[:, 0:NB * SSM_G], ALU.pow).then_inc(S.g_rstd, 1)

        with self.stage("p_free0 p_free1", "ssm_out") as (block, S):
            @block.tensor
            def _(pe):
                self.project(pe, S, [("T", 512)] * 2, YT, 16)

            @block.scalar
            def _(act):
                for j in range(2):
                    self.leave(act, j, per=4)
                    for e in range(2):
                        nc.scalar.copy(YS[:, e, j * BANK:(j + 1) * BANK], self.bank(j, e)).then_inc(self.freed(S, j), 1)

    def moba(self, ctx, YS):
        nc, a = self.nc, self.a
        AH = 8
        QT = self.sb("moba_qT", [P, KT, SEQ], ctx=ctx)
        KT_ = self.sb("moba_kT", [P, KT, SEQ], ctx=ctx)
        V = self.sb("moba_v", [P, NB, D], ctx=ctx)
        YT = self.sb("moba_yT", [P, KT, SEQ], ctx=ctx)
        YA = self.sb("moba_branch", [P, NB, D], ctx=ctx)
        bg = self.sb("b_gate", [P, 2 * D], ctx=ctx)
        lnp = self.sb("ln2_params", [P, 2, D], ctx=ctx)
        side = nc.alloc_semaphore("moba_side")
        scale = 1.0 / math.sqrt(P)

        with self.stage("p_free0 p_free1", "att_in") as (block, S):
            @block.tensor
            def _(pe):
                self.project(pe, S, [("F", 512)] * 4 + [("T", 512)] * 2, self.hT, KT)

            @block.scalar
            def _(act):
                act.dma_start(bg[:], a["b_gate_3"].partition_broadcast(P)).then_inc(side, 16)
                act.dma_start(lnp[:, 0, :], a["ln2_g_3"].partition_broadcast(P)).then_inc(side, 16)
                act.dma_start(lnp[:, 1, :], a["ln2_b_3"].partition_broadcast(P)).then_inc(side, 16)
                for j in (1, 3, 5):
                    self.leave(act, j)
                    for e in range(2):
                        if j == 5:
                            ins = nc.scalar.copy(V[:, e, BANK:], self.bank(j, e))
                        else:
                            dst = (QT if j == 1 else KT_)[:, 4 + 2 * e:6 + 2 * e, :].rearrange("p t n -> p (t n)")
                            ins = nc.scalar.mul(dst, self.bank(j, e), scale if j == 1 else 1.0)
                        ins.then_inc(self.freed(S, j), 1)

            @block.vector
            def _(ve):
                for j in (0, 2, 4):
                    self.leave(ve, j)
                    for e in range(2):
                        if j == 4:
                            ins = nc.vector.tensor_copy(V[:, e, 0:BANK], self.bank(j, e))
                        else:
                            dst = (QT if j == 0 else KT_)[:, 2 * e:2 * e + 2, :].rearrange("p t n -> p (t n)")
                            ins = nc.vector.tensor_scalar(dst, self.bank(j, e), scale if j == 0 else 1.0, None, ALU.mult)
                        ins.then_inc(self.freed(S, j), 1)

        with self.stage(self.ATT) as (block, S):
            self.attention(block, S, ctx, AH, P, QT, KT_, V, self.causal3_add, None, YT)

        with self.stage("p_free0 p_free1 pre sig mixed", "att_out") as (block, S):
            pre = self.sb("gate_pre", [P, 2, NB, BANK], ctx=ctx)

            @block.tensor
            def _(pe):
                self.project(pe, S, [("T", 512)] * 2, YT, KT)
                self.project(pe, S, [("T", 512)] * 4, self.hT, KT, first=2)

            @block.scalar
            def _(act):
                for j in range(2):
                    self.leave(act, j)
                    for e in range(2):
                        nc.scalar.copy(YA[:, e, j * BANK:(j + 1) * BANK], self.bank(j, e)).then_inc(self.freed(S, j), 1)
                nc.scalar.drain()
                for i in range(4):
                    act.wait_ge(S.pre, i + 1)
                    nc.scalar.activation(pre[:, i % 2], pre[:, i % 2], ACT.Sigmoid).then_inc(S.sig, 1)

            @block.vector
            def _(ve):
                ve.wait_ge(side, 48)
                for i in range(4):
                    j = i + 2
                    self.leave(ve, j)
                    for e in range(2):
                        nc.vector.tensor_tensor(pre[:, i % 2, e, :], self.bank(j, e), bg[:, i * BANK:(i + 1) * BANK],
                                                ALU.add).then_inc(self.freed(S, j), 1)
                    nc.vector.drain().then_inc(S.pre, 1)
                    ve.wait_ge(S.sig, i + 1)
                    branch = (YS if i < 2 else YA)[:, :, (i % 2) * BANK:(i % 2 + 1) * BANK]
                    nc.vector.tensor_tensor(branch, branch, pre[:, i % 2], ALU.mult)
                    nc.vector.drain()
                nc.vector.tensor_tensor(YA[:], YA[:], YS[:], ALU.add)

        with self.stage("n_tr n_hT p_free0 p_free1 l_ms l_rstd", "mix3_out") as (block, S):
            @block.tensor
            def _(pe):
                self.turn_plain(pe, S, YA)
                pe.wait_ge(S.n_hT, self.N_HT)
                self.project(pe, S, [("T", 512)] * 2, self.hT, KT)

            @block.scalar
            def _(act):
                self.copy_tiles(act, nc.scalar.copy, S, 0)

            @block.vector
            def _(ve):
                for b in range(NB):
                    nc.vector.tensor_scalar(self.X[:, b, :], self.X[:, b, :], ALPHA, None, ALU.mult)
                self.copy_tiles(ve, nc.vector.tensor_copy, S, 1)
                nc.vector.drain()
                self.plain_residual(ve, S)
                nc.vector.drain()
                self.layer_norm_vector(ve, S, lnp)

            @block.gpsimd
            def _(pool):
                self.layer_norm_gpsimd(pool, S)

    def build(self, out):
        a = self.a
        with self.ctx:
            self.place()
            self.plan()
            self.plan_side()
            group = KT * SIDE_GROUP
            for l in range(2):
                with ExitStack() as ada:
                    self.place_side(ada, (4 - 2 * l) * group)
                    if l == 0:
                        self.load_constants()
                        self.ada_start()
                    self.mixer(l)
                self.peer(l)
            self.final_norm(a["final_norm"])
            for l in range(2):
                cols = slice(KT * l, KT * (l + 1))
                self.ffn(f"ffn1_{l}", self.col("ffn1_norm_2")[:, cols])
                if l == 0:
                    self.pool_conv()
                else:
                    self.sparse_attention()
                self.ffn(f"ffn2_{l}", self.col("ffn2_norm_2")[:, cols])
            self.final_norm(a["final_norm_2"])
            self.ffn("ffn1_3", layer_norm=(a["ln1_g_3"], a["ln1_b_3"]))
            self.hybrid()
            self.ffn("ffn2_3", layer_norm=(a["ln3_g_3"], a["ln3_b_3"]))
            self.store(out)


def kernel(**inputs):
    import concourse.bacc as bacc
    from concourse.bass_utils import run_bass_kernel_spmd

    nc = bacc.Bacc("TRN2", target_bir_lowering=False, num_devices=1)
    arrays, args = {}, {}
    inputs = {**inputs, "shape_consts": shape_constants()[0]}
    for name, value in inputs.items():
        value = np.ascontiguousarray(value)
        arrays[f"in_{name}_dram"] = value
        args[name] = nc.dram_tensor(f"in_{name}_dram", value.shape, mybir.dt.from_np(value.dtype), kind="ExternalInput").ap()
    out = nc.dram_tensor("out_dram", (1, SEQ, D), F32, kind="ExternalOutput").ap()
    Program(nc, args).build(out)
    return run_bass_kernel_spmd(nc, [arrays], core_ids=[0]).results[0]["out_dram"]
```

```python
from collections import namedtuple
from contextlib import ExitStack, contextmanager
import math

import numpy as np
import concourse.bass as bass
from concourse import mybir

ALU = mybir.AluOpType
ACT = mybir.ActivationFunctionType
AX = mybir.AxisListType
F32 = mybir.dt.float32
F32R = mybir.dt.float32r
I32 = mybir.dt.int32
U32 = mybir.dt.uint32

P = 128
D = 1024
KT = D // P
SEQ = 256
NB = SEQ // P
HALF = D // 2
RING = 6
SLOT = 2048
BANK = 512
DFF = 2816
FF_COLS = 256
FF_STEPS = DFF // FF_COLS
EPS = 1e-6
LN_EPS = 1e-5
NEG = -1e30
TAKEN = -3e38
HEADS = 8
TOPK = 16
SIDE_RING = 6
SIDE_COLS = 1024
SIDE_GROUP = 2
SPLIT = 4
PAIR = 2
GRING = 16
GHALF = GRING // 2
PE_ROWS = 3
VE_ROWS = GHALF - PE_ROWS
PE_CREDIT = 2 * PE_ROWS + 2
VE_CREDIT = GHALF + 1
DSA_TOPK = 64
KERN = 31
ALPHA = 2 ** 0.25
SSM_D = 2048
SSM_G = 8
SSM_R = 4
SSM_H = SSM_G * SSM_R
SSM_P = 64


def shape_constants():
    i = np.arange(P)
    eye = np.eye(P)
    before = i[:, None] < i[None, :]
    upto = i[:, None] <= i[None, :]
    strict3 = np.concatenate([before, np.ones((P, P)), before], 1)
    count = np.minimum(np.arange(SEQ)[None] + 1, np.array([2, 4, 8, 16])[:, None])
    dist = 255 - np.arange(384)
    d = np.maximum(dist, 16).astype(np.float32)
    big = 16 + (np.log(d / np.float32(16)) / np.float32(math.log(8)) * np.float32(16)).astype(np.int32)
    bucket = np.where(dist < 16, dist, np.minimum(big, 31))
    onehot = np.zeros((P, 384))
    for c in range(256):
        onehot[bucket[c], c] = 1.0
    causal = np.where(i[None, :] > i[:, None], NEG, 0.0)
    parts = {
        "ident": eye,
        "anti": eye[::-1],
        "upto": upto,
        "after": i[:, None] > i[None, :],
        "from_": i[:, None] >= i[None, :],
        "ones": np.ones((P, P)),
        "strict3": strict3,
        "strict3_add": np.where(strict3 > 0, 0.0, NEG),
        "causal3_add": np.concatenate([causal, np.zeros((P, P)), causal], 1),
        "iota16": np.tile(np.arange(16), (P, 1)),
        "neghalf": np.full((P, 32), -0.5),
        "invcount": np.tile((1.0 / count[:, :16]).reshape(1, -1), (P, 1)),
        "onehot": onehot,
    }
    at, where = 0, {}
    for name, a in parts.items():
        where[name] = (at, at + a.shape[1])
        at += a.shape[1]
    return np.concatenate([np.asarray(a, np.float32) for a in parts.values()], 1), where


PARAM_GROUPS = [
    [("norm_mix", 16), ("norm_ffn", 16)],
    [("conv_w_3", 128)],
    [("conv_w_2", KERN * 4)],
    [("gm_bs", 16), ("out_norm_a", 8), ("out_norm_b", 8), ("ffn1_norm_2", 16), ("mix_norm_2", 16),
     ("ffn2_norm_2", 16), ("conv_b_2", 4), ("conv_ln_g_2", 4), ("conv_ln_b_2", 4), ("pool_scale_2", 4)],
    [("ssm_norm_w_3", 16), ("conv_b_3", 32), ("c", 8)],
    [("ada_b", 96)],
]


class Program:
    def __init__(self, nc, a):
        self.nc, self.a = nc, a
        self.ctx = ExitStack()
        self.n_stage = 0

    def sb(self, name, shape, dt=F32, ctx=None):
        if ctx is not None:
            name = f"{name}_{self.n_stage}"
        return (ctx or self.ctx).enter_context(self.nc.sbuf_tensor(name, shape, dt))

    def place(self):
        nc = self.nc
        consts, where = shape_constants()
        self.X = self.sb("X", [P, NB, D])
        self.hT = self.sb("hT", [P, KT, SEQ])
        self.ring = self.sb("ring", [P, RING, SLOT])
        self.cst = self.sb("cst", [P, consts.shape[1]])

        def table(name):
            lo, hi = where[name]
            return self.cst[:, lo:hi]
        self.ident = table("ident")
        self.anti = table("anti")
        self.upto = table("upto")
        self.after = table("after")
        self.from_ = table("from_")
        self.ones = table("ones")
        self.strict3 = table("strict3")
        self.strict3_add = table("strict3_add")
        self.causal3_add = table("causal3_add")
        self.iota16 = table("iota16")
        self.neghalf = table("neghalf")
        self.invcount = table("invcount")
        self.onehot = table("onehot")
        self.prm = self.sb("prm", [P, len(PARAM_GROUPS), P])
        self.ms = self.sb("ms", [P, NB])
        self.rstd = self.sb("rstd", [P, NB])
        self.mu = self.sb("mu", [P, NB])
        self.negmu = self.sb("negmu", [P, NB])
        self.xn = self.sb("xn", [P, NB, D])
        self.cact = self.sb("cact", [P, KT])
        self.first_mod = self.sb("first_mod", [P, 2 * KT])
        self.mod = self.sb("mod", [P, 48])
        self.modA = self.sb("modA", [P, 2, KT])
        self.gate = self.sb("gate", [P, 2, D])
        self.PS = self.ctx.enter_context(nc.psum_tensor("PS", [P, 8, BANK], F32))
        self.banks = [[nc.alloc_semaphore(f"stage{b}_{i}") for i in range(24)] for b in range(2)]
        self.w_landed = [nc.alloc_semaphore(f"w_landed{i}") for i in range(RING)]
        self.w_used = nc.alloc_semaphore("w_used")
        self.side_landed = [nc.alloc_semaphore(f"ada_landed{i}") for i in range(SIDE_RING)]
        self.side_used = nc.alloc_semaphore("ada_used")
        self.g_landed = [nc.alloc_semaphore(f"g_landed{i}") for i in range(GRING)]
        self.g_used = nc.alloc_semaphore("g_used_ve")
        self.g_used_pe = nc.alloc_semaphore("g_used_pe")
        self.g_index = nc.alloc_semaphore("g_index")
        self.g_turn = nc.alloc_semaphore("g_turn")

    def col(self, name, j=0):
        for g, rows in enumerate(PARAM_GROUPS):
            at = 0
            for n, count in rows:
                if n == name:
                    return self.prm[:, g, at + j:at + count]
                at += count
        raise KeyError(name)

    def plan(self):
        a = self.a

        def lin(w, jobs):
            out = []
            for cols in jobs:
                cols = [cols] if isinstance(cols, tuple) else cols
                width = sum(n for _, n in cols)
                for g in range(w.shape[0] // 512):
                    rows = w[g * 512:(g + 1) * 512, :].rearrange("(k p) n -> p k n", p=P)
                    at, pieces = 0, []
                    for c0, n in cols:
                        pieces.append((at, n, width, rows[:, :, c0:c0 + n]))
                        at += n
                    out.append(("lin", pieces))
            return out

        def full(n):
            return [(c, 512) for c in range(0, n, 512)]

        def ffn(wg, wu, wd):
            def up(i):
                return [("lin", [(256 * m, 256, 512, w[512 * g:512 * (g + 1), i * 256:(i + 1) * 256]
                                  .rearrange("(k p) n -> p k n", p=P)) for m, w in enumerate((wg, wu))]) for g in range(2)]

            def down(i):
                return [("down", wd[i * 256:(i + 1) * 256, :].rearrange("(k p) n -> p k n", p=P))]
            out = up(0)
            for i in range(FF_STEPS):
                out += (up(i + 1) if i + 1 < FF_STEPS else []) + down(i)
            return out

        stages = []
        for l in range(2):
            stages += [(f"mix_in{l}", lin(a["w_in"][l], full(2560))),
                       (f"mix_out{l}", lin(a["w_out"][l], full(D))),
                       (f"peer_q{l}", lin(a["peer_wq"][l], full(2048)))]
        for l in range(2):
            stages.append((f"ffn1_{l}", ffn(a["ffn1_w_gate_2"][l], a["ffn1_w_up_2"][l], a["ffn1_w_down_2"][l])))
            if l == 0:
                stages += [("ab_in", lin(a["ab_w_in_2"][0], full(1536))),
                           ("ab_out", lin(a["ab_w_out_2"][0], full(D)))]
            else:
                stages += [("c_in", lin(a["c_w_in_2"][0], [(3072, 512), [(3584, 64), (3584, 64), (3648, 8)]] + full(3072))),
                           ("c_out", lin(a["c_w_out_2"][0], full(D)))]
            stages.append((f"ffn2_{l}", ffn(a["ffn2_w_gate_2"][l], a["ffn2_w_up_2"][l], a["ffn2_w_down_2"][l])))
        w3 = a["w_in_3"]
        stages += [("ffn1_3", ffn(a["ffn1_w_gate_3"], a["ffn1_w_up_3"], a["ffn1_w_down_3"])),
                   ("ssm_in", lin(w3, [(6144, 32)] + [(2048 + c, 512) for c in range(0, 4096, 512)])),
                   ("ssm_z", lin(w3, full(2048) + [(6176, 512), (6688, 512)])),
                   ("ssm_out", lin(a["w_ssm_out_3"], full(D))),
                   ("att_in", lin(w3, [(7200 + c, 512) for c in range(0, 2048, 512)])),
                   ("att_out", lin(a["w_att_out_3"], full(D)) + lin(w3, [(9248 + c, 512) for c in range(0, 2048, 512)])),
                   ("mix3_out", lin(a["w_o_3"], full(D))),
                   ("ffn2_3", ffn(a["ffn2_w_gate_3"], a["ffn2_w_up_3"], a["ffn2_w_down_3"]))]
        self.chunks, self.chunk_end = [], {}
        for name, chunks in stages:
            self.chunks += chunks
            self.chunk_end[name] = len(self.chunks)
        self.landed_at, total = [], [0] * RING
        for n, chunk in enumerate(self.chunks):
            total[n % RING] += 16 * (len(chunk[1]) if chunk[0] == "lin" else 1)
            self.landed_at.append(total[n % RING])
        self.issued = self.taken = 0

    def load_weights(self, sp, name, side=None):
        end = self.chunk_end.get(name, self.taken)
        last = min(len(self.chunks), end + RING)
        side_last = min(self.side_end, self.side_taken + side + SIDE_RING) if side is not None else self.side_issued
        side_first, first = self.side_issued, self.issued
        for n in range(first, last):
            due = side_last if name == "ahead" else side_first + -(-(side_last - side_first) * 3 * (n - first + 1) // (2 * (last - first)))
            self.load_side(sp, min(due, side_last))
            if n >= RING:
                sp.wait_ge(self.w_used, n - RING + 1)
            slot = self.ring[:, n % RING, :]
            kind, what = self.chunks[n]
            if kind == "lin":
                for at, w, width, src in what:
                    dst = slot[:, 0:4 * width].rearrange("p (k n) -> p k n", k=4)[:, :, at:at + w]
                    sp.dma_start(dst, src).then_inc(self.w_landed[n % RING], 16)
            else:
                dst = slot.rearrange("p (k n) -> p k n", k=2)
                sp.dma_start(dst, what).then_inc(self.w_landed[n % RING], 16)
        self.load_side(sp, side_last)
        self.issued = max(first, last)

    def plan_side(self):
        order = [(0, 0), (0, 1), (0, 2), (1, 0), (1, 1), (1, 2)]
        self.side_chunks = [(l, g, k, h) for l, g in order for k in range(KT) for h in range(SIDE_GROUP)]
        self.side_issued = self.side_taken = self.side_end = 0

    def load_side(self, sp, upto):
        for n in range(self.side_issued, upto):
            if n >= SIDE_RING:
                sp.wait_ge(self.side_used, n - SIDE_RING + 1)
            l, g, k, h = self.side_chunks[n]
            c = (SIDE_GROUP * g + h) * SIDE_COLS
            sp.dma_start(self.side_ring[:, n % SIDE_RING, :],
                         self.a["ada_w"][l, k * P:(k + 1) * P, c:c + SIDE_COLS]).then_inc(self.side_landed[n % SIDE_RING], 16)
        self.side_issued = max(self.side_issued, upto)

    def sum_side(self, ve, count):
        for n in range(self.side_taken, self.side_taken + count):
            l, g, k, h = self.side_chunks[n]
            ve.wait_ge(self.side_landed[n % SIDE_RING], 16 * (n // SIDE_RING + 1))
            slot, acc, c = self.side_ring[:, n % SIDE_RING, :], self.side_acc[:, SIDE_GROUP * g + h, :], self.cact[:, k:k + 1]
            if k == 0:
                self.nc.vector.tensor_scalar(acc, slot, c, None, ALU.mult).then_inc(self.side_used, 1)
            else:
                self.nc.vector.scalar_tensor_tensor(acc, slot, c, acc, ALU.mult, ALU.add).then_inc(self.side_used, 1)
            if h == SIDE_GROUP - 1:
                self.nc.vector.drain()
        self.side_taken += count

    def sum_columns(self, out, v):
        for k in range(KT):
            ins = self.nc.tensor.matmul(out[:, k:k + 1], self.side_acc[:, v, k * P:(k + 1) * P], self.ones[:, 0:1],
                                        start=True, stop=True, skip_group_check=True)
        return ins

    def sum_spread(self, bank, v):
        for h in range(2):
            ins = self.nc.tensor.matmul(self.PS[:, bank + h, :], self.ones, self.side_acc[:, v, h * BANK:(h + 1) * BANK],
                                        start=True, stop=True)
        return ins

    def place_side(self, ctx, count):
        self.side_ring = self.sb("ada_ring", [P, SIDE_RING, SIDE_COLS], ctx=ctx)
        self.side_acc = self.sb("ada_sums", [P, 6, D], ctx=ctx)
        self.side_end += count

    def take(self, pe):
        n = self.taken
        self.taken += 1
        pe.wait_ge(self.w_landed[n % RING], self.landed_at[n])
        return self.ring[:, n % RING, :]

    @contextmanager
    def stage(self, names, weights=None, side=None):
        nc = self.nc
        mine, other = self.banks[self.n_stage % 2], self.banks[(self.n_stage + 1) % 2]
        self.n_stage += 1
        self.base = self.taken
        names = names.split()
        assert len(names) <= len(mine)
        with nc.Block(no_gpsimd_drain=True) as block:
            @block.gpsimd
            def _(pool):
                nc.gpsimd.sem_clear(range(other[0].num, other[-1].num + 1))

            if weights or side is not None:
                @block.sync
                def _(sp):
                    self.load_weights(sp, weights, side)

            yield block, namedtuple("StageSemaphores", names)(*mine[:len(names)])

    def norm_vector(self, ve, S, scale, shift, between=None):
        nc = self.nc
        for b in range(NB):
            nc.vector.tensor_tensor_reduce(self.xn[:, b, :], self.X[:, b, :], self.X[:, b, :], 1.0 / D, EPS,
                                           ALU.mult, ALU.add, self.ms[:, b:b + 1])
        nc.vector.drain().then_inc(S.n_ms, 1)
        ve.wait_ge(S.n_rstd, 1)
        for b in range(NB):
            nc.vector.tensor_scalar(self.xn[:, b, :], self.X[:, b, :], self.rstd[:, b:b + 1], None,
                                    ALU.mult).then_inc(S.n_xn, 1)
        if between:
            between()
        self.evacuate_tiles(ve, nc.vector, S, 1, scale, shift)

    def norm_gpsimd(self, pool, S):
        pool.wait_ge(S.n_ms, 1)
        self.nc.gpsimd.tensor_tensor(self.rstd[:], self.ms[:], self.neghalf[:, 0:NB], ALU.pow).then_inc(S.n_rstd, 1)

    def norm_tensor(self, pe, S, src=None):
        nc = self.nc
        for b in range(NB):
            pe.wait_ge(S.n_xn, b + 1)
            for g in range(2):
                for j in range(4):
                    k = 4 * g + j
                    ins = nc.tensor.transpose(self.PS[:, 4 + 2 * b + g, j * P:(j + 1) * P],
                                              (src or self.xn)[:, b, k * P:(k + 1) * P], self.ident)
                ins.then_inc(S.n_tr, 1)

    def evacuate_tiles(self, eng, ops, S, odd, scale, shift):
        for b in range(NB):
            for g in (odd,):
                eng.wait_ge(S.n_tr, 2 * b + g + 1)
                for j in range(4):
                    k = 4 * g + j
                    out = self.hT[:, k, b * P:(b + 1) * P]
                    src = self.PS[:, 4 + 2 * b + g, j * P:(j + 1) * P]
                    bias = shift[:, k:k + 1] if shift is not None else 0.0
                    if odd:
                        if shift is None:
                            ins = ops.tensor_scalar(out, src, scale[:, k:k + 1], None, ALU.mult)
                        else:
                            ins = ops.tensor_scalar(out, src, scale[:, k:k + 1], bias, ALU.mult, ALU.add)
                    elif shift is None:
                        ins = ops.activation(out, src, ACT.Copy, scale=scale[:, k:k + 1])
                    else:
                        ins = ops.activation(out, src, ACT.Identity, bias=bias, scale=scale[:, k:k + 1])
                ins.then_inc(S.n_hT, 1)

    def norm_scalar(self, act, S, scale, shift):
        self.evacuate_tiles(act, self.nc.scalar, S, 0, scale, shift)

    N_HT = 4

    def project(self, pe, S, jobs, actT, kts, first=0):
        nc = self.nc
        for j, (kind, w) in enumerate(jobs, first):
            pair = 2 * (j % 2)
            if j >= 2:
                pe.wait_ge((S.p_free0, S.p_free1)[j % 2], 2 * (j // 2))
            for g in range(kts // 4):
                slot = self.take(pe)[:, 0:4 * w].rearrange("p (k n) -> p k n", k=4)
                for kk in range(4):
                    k = 4 * g + kk
                    if kind == "T":
                        for b in range(NB):
                            ins = nc.tensor.matmul(self.PS[:, pair + b, 0:w], actT[:, k, b * P:(b + 1) * P],
                                                   slot[:, kk, :], start=(k == 0), stop=(k == kts - 1),
                                                   skip_group_check=True)
                    else:
                        for t in range(w // P):
                            ins = nc.tensor.matmul(
                                self.PS[:, pair + t // 2, (t % 2) * SEQ:(t % 2 + 1) * SEQ],
                                slot[:, kk, t * P:(t + 1) * P], actT[:, k, :],
                                start=(k == 0 and t % 2 == 0), stop=(k == kts - 1), skip_group_check=True)
                ins.then_inc(self.w_used, 1)

    def leave(self, eng, j, per=2):
        eng.wait_ge(self.w_used, self.base + (j + 1) * per)

    def bank(self, j, e):
        return self.PS[:, 2 * (j % 2) + e, :]

    def freed(self, S, j):
        return (S.p_free0, S.p_free1)[j % 2]

    def load_constants(self):
        nc, a = self.nc, self.a
        with ExitStack() as ctx, self.stage("rows turned turned_out") as (block, S):
            rows = self.sb("param_rows", [P, len(PARAM_GROUPS), P], ctx=ctx)
            loads = nc.alloc_semaphore("const_landed")
            dmas = [(self.cst[:], a["shape_consts"])] + [
                (self.X[:], a["x"][0].rearrange("(b p) d -> p b d", p=P))]
            for g, group in enumerate(PARAM_GROUPS):
                at = 0
                for name, count in group:
                    src = a[name]
                    flat = src.rearrange(" ".join("abc"[:len(src.shape)]) + " -> (" + " ".join("abc"[:len(src.shape)]) + ")")
                    dmas.append((rows[at:at + count, g, :], flat.rearrange("(r p) -> r p", p=P)))
                    at += count

            @block.sync
            def _(sp):
                sp.wait_ge(loads, 16 * len(dmas))
                self.load_side(sp, SIDE_RING)

            @block.vector
            def _(ve):
                nc.vector.memset(rows[:], 0.0).then_inc(S.rows, 1)
                ve.wait_ge(S.turned, 1)
                for g in range(len(PARAM_GROUPS)):
                    ins = nc.vector.tensor_copy(self.prm[:, g, :], self.PS[:, g, 0:P])
                ins.then_inc(S.turned_out, 1)

            @block.scalar
            def _(act):
                act.wait_ge(S.rows, 1)
                for dst, src in dmas:
                    act.dma_start(dst, src).then_inc(loads, 16)
                act.wait_ge(loads, 16 * len(dmas))

            @block.tensor
            def _(pe):
                pe.wait_ge(loads, 16 * len(dmas))
                for g in range(len(PARAM_GROUPS)):
                    ins = nc.tensor.transpose(self.PS[:, g, 0:P], rows[:, g, :], self.ident)
                ins.then_inc(S.turned, 1)

    def ada_start(self):
        nc = self.nc
        group = KT * SIDE_GROUP
        with self.stage("silu summed columns", "ahead", side=group) as (block, S):
            @block.scalar
            def _(act):
                nc.scalar.activation(self.cact[:], self.col("c"), ACT.Silu).then_inc(S.silu, 1)
                act.wait_ge(S.columns, 1)
                nc.scalar.copy(self.first_mod[:], self.PS[:, 0, 0:2 * KT])

            @block.vector
            def _(ve):
                ve.wait_ge(S.silu, 1)
                self.sum_side(ve, group)
                nc.vector.drain().then_inc(S.summed, 1)

            @block.tensor
            def _(pe):
                pe.wait_ge(S.summed, 1)
                self.sum_columns(self.PS[:, 0, 0:KT], 0)
                self.sum_columns(self.PS[:, 0, KT:2 * KT], 1).then_inc(S.columns, 1)

    def ffn(self, name, gain=None, layer_norm=None):
        nc = self.nc
        with ExitStack() as ctx, self.stage(
                "n_ms n_rstd n_xn n_tr n_hT hT_hi hT_split w_hi w_lo silu_done hid_ready hid_turned hid_hi hid_lo l_ms l_rstd", name) as (block, S):
            silu = self.sb("silu_gate", [P, NB, FF_COLS], ctx=ctx)
            hid = self.sb("hidden", [P, NB, FF_COLS], ctx=ctx)
            hidT_hi = self.sb("hiddenT_hi", [P, 2, SEQ], F32R, ctx=ctx)
            hidT_lo = self.sb("hiddenT_lo", [P, 2, SEQ], F32R, ctx=ctx)
            hT_hi = self.sb("hT_hi", [P, KT, SEQ], F32R, ctx=ctx)
            hT_lo = self.sb("hT_lo", [P, KT, SEQ], F32R, ctx=ctx)
            ring_hi = self.sb("ring_hi", [P, SPLIT, SLOT], F32R, ctx=ctx)
            ring_lo = self.sb("ring_lo", [P, SPLIT, SLOT], F32R, ctx=ctx)
            WINDOWS = 4
            if layer_norm:
                lnp = self.sb("ln_params", [P, 2, D], ctx=ctx)
                ln_landed = nc.alloc_semaphore("ln_landed_" + name)
            base = self.taken
            last = 3 * FF_STEPS - 1

            def landed(c, i):
                per = self.landed_at[base + c + 3 * WINDOWS] - self.landed_at[base + c] if i is not None else 0
                return self.landed_at[base + c] if i is None else i * per + self.landed_at[base + c]

            def count(n, i, per):
                return n if i is None else i * per + n

            def product(out, left, right, start, stop):
                for a_, b_ in ((0, 0), (0, 1), (1, 0)):
                    ins = nc.tensor.matmul(out, left[a_], right[b_], start=start and a_ + b_ == 0, stop=stop and a_ == 1,
                                           skip_group_check=True)
                return ins

            def halves(c):
                return ring_hi[:, c % SPLIT, :], ring_lo[:, c % SPLIT, :]

            def up(pe, c, i, parity, half):
                pe.wait_ge(S.w_lo, count(c + 1, i, 3 * WINDOWS))
                parts = [x.rearrange("p (k n) -> p k n", k=4) for x in halves(c)]
                for kk in range(4):
                    k = 4 * half + kk
                    for b in range(NB):
                        tok = slice(b * P, (b + 1) * P)
                        ins = product(self.PS[:, 2 * parity + b, :], [hT_hi[:, k, tok], hT_lo[:, k, tok]],
                                      [x[:, kk, :] for x in parts], k == 0, k == KT - 1)
                ins.then_inc(self.w_used, 1)

            def turn(pe, s, i, parity):
                pe.wait_ge(S.hid_ready, count(s + 1, i, WINDOWS))
                for t in range(2):
                    for b in range(NB):
                        ins = nc.tensor.transpose(self.PS[:, 2 * parity, t * SEQ + b * P:t * SEQ + (b + 1) * P],
                                                  hid[:, b, t * P:(t + 1) * P], self.ident)
                ins.then_inc(S.hid_turned, 1)

            def down(pe, s, c, i, first=False):
                pe.wait_ge(S.w_lo, count(c + 1, i, 3 * WINDOWS))
                pe.wait_ge(S.hid_lo, count(s + 1, i, WINDOWS))
                parts = [x.rearrange("p (t n) -> p t n", t=2) for x in halves(c)]
                for t in range(2):
                    for b in range(NB):
                        tok = slice(b * P, (b + 1) * P)
                        for h in range(2):
                            ins = product(self.PS[:, 4 + 2 * b + h, :], [hidT_hi[:, t, tok], hidT_lo[:, t, tok]],
                                          [x[:, t, h * BANK:(h + 1) * BANK] for x in parts],
                                          first and t == 0, c == last and t == 1)
                ins.then_inc(self.w_used, 1)

            @block.tensor
            def _(pe):
                def window(s, i):
                    p = (s + 1) % 2
                    up(pe, 3 * s + 2, i, p, 0)
                    turn(pe, s, i, 1 - p)
                    up(pe, 3 * s + 3, i, p, 1)
                    down(pe, s, 3 * s + 4, i, first=(s == 0 and i is None))

                if layer_norm:
                    for b in range(NB):
                        for g in range(2):
                            for j in range(4):
                                k = 4 * g + j
                                ins = nc.tensor.transpose(self.PS[:, 4 + 2 * b + g, j * P:(j + 1) * P],
                                                          self.X[:, b, k * P:(k + 1) * P], self.ident)
                            ins.then_inc(S.n_tr, 1)
                else:
                    self.norm_tensor(pe, S)
                pe.wait_ge(S.hT_split, 1)
                up(pe, 0, None, 0, 0)
                pe.wait_ge(S.hT_split, 2)
                up(pe, 1, None, 0, 1)
                window(0, None)
                with pe.Fori(0, (FF_STEPS - 3) // WINDOWS) as i:
                    for u in range(WINDOWS):
                        window(1 + u, i)
                window(FF_STEPS - 2, None)
                s = FF_STEPS - 1
                turn(pe, s, None, s % 2)
                down(pe, s, last, None)
                self.taken += 3 * FF_STEPS

            @block.scalar
            def _(act):
                def hi(c, i=None):
                    act.wait_ge(self.w_landed[(base + c) % RING], landed(c, i))
                    if c >= SPLIT:
                        act.wait_ge(self.w_used, count(base + c - SPLIT + 1, i, 3 * WINDOWS))
                    nc.scalar.copy(halves(c)[0], self.ring[:, (base + c) % RING, :]).then_inc(S.w_hi, 1)

                def silu_step(s, i, used):
                    act.wait_ge(self.w_used, count(base + used, i, 3 * WINDOWS))
                    p = 2 * (s % 2)
                    nc.scalar.activation(silu[:], self.PS[:, p:p + 2, 0:FF_COLS], ACT.Silu).then_inc(S.silu_done, 1)

                def hid_hi(s, i):
                    act.wait_ge(S.hid_turned, count(s + 1, i, WINDOWS))
                    nc.scalar.copy(hidT_hi[:].rearrange("p t n -> p (t n)"), self.PS[:, 2 * (s % 2), :]).then_inc(S.hid_hi, 1)

                def window(s, i):
                    silu_step(s, i, 2 if s == 0 else 3 * s + 1)
                    for c in (3 * s + 4, 3 * s + 5):
                        if c <= last:
                            hi(c, i)
                    hid_hi(s, i)
                    if 3 * s + 6 <= last:
                        hi(3 * s + 6, i)

                if layer_norm:
                    for i, v in enumerate(layer_norm):
                        act.dma_start(lnp[:, i, :], v.partition_broadcast(P)).then_inc(ln_landed, 16)
                hi(0)
                hi(1)
                if layer_norm:
                    self.copy_tiles(act, nc.scalar.copy, S, 0)
                else:
                    self.norm_scalar(act, S, gain, None)
                nc.scalar.drain()
                nc.scalar.copy(hT_hi[:, 0:4, :], self.hT[:, 0:4, :]).then_inc(S.hT_hi, 1)
                hi(2)
                hi(3)
                window(0, None)
                with act.Fori(0, (FF_STEPS - 3) // WINDOWS) as i:
                    for u in range(WINDOWS):
                        window(1 + u, i)
                window(FF_STEPS - 2, None)
                window(FF_STEPS - 1, None)

            @block.vector
            def _(ve):
                def lo(c, i=None):
                    ve.wait_ge(S.w_hi, count(c + 1, i, 3 * WINDOWS))
                    slot = self.ring[:, (base + c) % RING, :]
                    nc.vector.tensor_tensor(halves(c)[1], slot, halves(c)[0], ALU.subtract).then_inc(S.w_lo, 1)

                def window(s, i):
                    ve.wait_ge(S.silu_done, count(s + 1, i, WINDOWS))
                    p = 2 * (s % 2)
                    nc.vector.tensor_tensor(hid[:], silu[:], self.PS[:, p:p + 2, FF_COLS:2 * FF_COLS], ALU.mult).then_inc(S.hid_ready, 1)
                    for c in (3 * s + 4, 3 * s + 5):
                        if c <= last:
                            lo(c, i)
                    ve.wait_ge(S.hid_hi, count(s + 1, i, WINDOWS))
                    flat = "p t n -> p (t n)"
                    nc.vector.tensor_tensor(hidT_lo[:].rearrange(flat), self.PS[:, p, :], hidT_hi[:].rearrange(flat),
                                            ALU.subtract).then_inc(S.hid_lo, 1)
                    if 3 * s + 6 <= last:
                        lo(3 * s + 6, i)

                if layer_norm:
                    lo(0)
                    self.copy_tiles(ve, nc.vector.tensor_copy, S, 1)
                else:
                    self.norm_vector(ve, S, gain, None, between=lambda: lo(0))
                nc.vector.drain()
                ve.wait_ge(S.hT_hi, 1)
                nc.vector.tensor_tensor(hT_lo[:, 0:4, :], self.hT[:, 0:4, :], hT_hi[:, 0:4, :], ALU.subtract).then_inc(S.hT_split, 1)
                nc.vector.tensor_copy(hT_hi[:, 4:8, :], self.hT[:, 4:8, :])
                nc.vector.drain()
                nc.vector.tensor_tensor(hT_lo[:, 4:8, :], self.hT[:, 4:8, :], hT_hi[:, 4:8, :], ALU.subtract).then_inc(S.hT_split, 1)
                for c in range(1, 4):
                    lo(c)
                window(0, None)
                with ve.Fori(0, (FF_STEPS - 3) // WINDOWS) as i:
                    for u in range(WINDOWS):
                        window(1 + u, i)
                window(FF_STEPS - 2, None)
                window(FF_STEPS - 1, None)
                ve.wait_ge(self.w_used, base + 3 * FF_STEPS)
                out = self.PS[:, 4:8, :].rearrange("p (b h) n -> p b (h n)", b=NB)
                if not layer_norm:
                    for b in range(NB):
                        nc.vector.scalar_tensor_tensor(self.X[:, b, :], out[:, b, :], 0.5, self.X[:, b, :],
                                                       ALU.mult, ALU.add)
                else:
                    for b in range(NB):
                        nc.vector.tensor_scalar(self.X[:, b, :], self.X[:, b, :], ALPHA, None, ALU.mult)
                    nc.vector.drain()
                    for b in range(NB):
                        nc.vector.scalar_tensor_tensor(self.X[:, b, :], out[:, b, :], 0.5, self.X[:, b, :],
                                                       ALU.mult, ALU.add)
                    nc.vector.drain()
                    ve.wait_ge(ln_landed, 32)
                    self.layer_norm_vector(ve, S, lnp)

            @block.gpsimd
            def _(pool):
                if layer_norm:
                    self.layer_norm_gpsimd(pool, S)
                else:
                    self.norm_gpsimd(pool, S)

    def copy_tiles(self, eng, copy, S, odd):
        for b in range(NB):
            eng.wait_ge(S.n_tr, 2 * b + odd + 1)
            copy(self.hT[:, 4 * odd:4 * odd + 4, b * P:(b + 1) * P],
                 self.PS[:, 4 + 2 * b + odd, :].rearrange("p (k n) -> p k n", k=4)).then_inc(S.n_hT, 1)

    def layer_norm_vector(self, ve, S, lnp):
        nc = self.nc
        nc.vector.reduce_sum(self.mu[:], self.X[:], AX.X)
        nc.vector.drain()
        nc.vector.tensor_scalar(self.negmu[:], self.mu[:], -1.0 / D, None, ALU.mult)
        nc.vector.drain()
        for b in range(NB):
            nc.vector.tensor_scalar(self.X[:, b, :], self.X[:, b, :], self.negmu[:, b:b + 1], None, ALU.add)
        nc.vector.drain()
        for b in range(NB):
            nc.vector.tensor_tensor_reduce(self.xn[:, b, :], self.X[:, b, :], self.X[:, b, :], 1.0 / D, LN_EPS,
                                           ALU.mult, ALU.add, self.ms[:, b:b + 1])
        nc.vector.drain().then_inc(S.l_ms, 1)
        ve.wait_ge(S.l_rstd, 1)
        for b in range(NB):
            nc.vector.scalar_tensor_tensor(self.X[:, b, :], self.X[:, b, :], self.rstd[:, b:b + 1], lnp[:, 0, :],
                                           ALU.mult, ALU.mult)
        nc.vector.drain()
        for b in range(NB):
            nc.vector.tensor_tensor(self.X[:, b, :], self.X[:, b, :], lnp[:, 1, :], ALU.add)

    def layer_norm_gpsimd(self, pool, S):
        pool.wait_ge(S.l_ms, 1)
        self.nc.gpsimd.tensor_tensor(self.rstd[:], self.ms[:], self.neghalf[:, 0:NB], ALU.pow).then_inc(S.l_rstd, 1)

    def final_norm(self, gain):
        nc = self.nc
        with ExitStack() as ctx, self.stage("ms rstd done") as (block, S):
            g = self.sb("final_gain", [P, D], ctx=ctx)
            landed = nc.alloc_semaphore("gain_landed_" + str(self.n_stage))

            @block.scalar
            def _(act):
                act.dma_start(g[:], gain.partition_broadcast(P)).then_inc(landed, 16)

            @block.vector
            def _(ve):
                for b in range(NB):
                    nc.vector.tensor_tensor_reduce(self.xn[:, b, :], self.X[:, b, :], self.X[:, b, :], 1.0 / D, EPS,
                                                   ALU.mult, ALU.add, self.ms[:, b:b + 1])
                nc.vector.drain().then_inc(S.ms, 1)
                ve.wait_ge(S.rstd, 1)
                ve.wait_ge(landed, 16)
                for b in range(NB):
                    nc.vector.scalar_tensor_tensor(self.X[:, b, :], self.X[:, b, :], self.rstd[:, b:b + 1], g[:],
                                                   ALU.mult, ALU.mult)

            @block.gpsimd
            def _(pool):
                pool.wait_ge(S.ms, 1)
                nc.gpsimd.tensor_tensor(self.rstd[:], self.ms[:], self.neghalf[:, 0:NB], ALU.pow).then_inc(S.rstd, 1)

    def store(self, out):
        nc = self.nc
        stored = nc.alloc_semaphore("stored")
        with self.stage("") as (block, S):
            @block.scalar
            def _(act):
                act.dma_start(out[0].rearrange("(b p) d -> p b d", p=P), self.X[:]).then_inc(stored, 16)
                act.wait_ge(stored, 16)

    def mixer(self, l):
        nc, a = self.nc, self.a
        with ExitStack() as ctx:
            U = self.sb("gelu_u", [P, NB, HALF], ctx=ctx)
            V = self.sb("gelu_v", [P, NB, HALF], ctx=ctx)
            QT = self.sb("stick_qT", [P, 4, SEQ], ctx=ctx)
            KT_ = self.sb("stick_kT", [P, 4, SEQ], ctx=ctx)
            SV = self.sb("stick_v", [P, NB, HALF], ctx=ctx)
            Y = self.sb("mixed", [P, NB, D], ctx=ctx)
            vgain = self.sb("v_gain", [P, HALF], ctx=ctx)
            ws = self.sb("gm_w", [P, HEADS, P], ctx=ctx)
            side = nc.alloc_semaphore(f"mixer_side{l}")

            group = KT * SIDE_GROUP
            bias = self.col("ada_b")[:, 6 * KT * l:]
            with self.stage("n_ms n_rstd n_xn n_tr n_hT p_free0 p_free1", f"mix_in{l}", side=2 * group) as (block, S):
                jobs = [("T", 512), ("T", 512), ("F", 512), ("F", 512), ("T", 512)]

                @block.tensor
                def _(pe):
                    self.norm_tensor(pe, S)
                    pe.wait_ge(S.n_hT, self.N_HT)
                    self.project(pe, S, jobs, self.hT, KT)

                @block.scalar
                def _(act):
                    act.dma_start(vgain[:], a["gm_vnorm"][l].partition_broadcast(P)).then_inc(side, 16)
                    act.dma_start(ws[:], a["gm_ws"][l].rearrange("h t s -> t h s")).then_inc(side, 16)
                    for i, v in enumerate((2, 5)):
                        act.dma_start(self.gate[:, i, :], a["ada_b"][l, v * D:(v + 1) * D].partition_broadcast(P)).then_inc(side, 16)
                    self.norm_scalar(act, S, self.modA[:, 0, :], self.mod[:, 0:KT])
                    for j, dst in enumerate((U, V)):
                        self.leave(act, j)
                        for e in range(2):
                            nc.scalar.activation(dst[:, e, :], self.bank(j, e), ACT.Gelu_apprx_tanh).then_inc(self.freed(S, j), 1)
                    self.leave(act, 4)
                    for e in range(2):
                        nc.scalar.copy(SV[:, e, :], self.bank(4, e)).then_inc(self.freed(S, 4), 1)

                @block.vector
                def _(ve):
                    nc.vector.tensor_tensor(self.mod[:, 0:2 * KT], self.first_mod[:], bias[:, 0:2 * KT], ALU.add)
                    nc.vector.drain()
                    nc.vector.scalar_tensor_tensor(self.modA[:, 0, :], self.mod[:, KT:2 * KT], 1.0,
                                                   self.col("norm_mix")[:, KT * l:KT * (l + 1)], ALU.add, ALU.mult)
                    self.norm_vector(ve, S, self.modA[:, 0, :], self.mod[:, 0:KT])
                    left = 2 * group
                    for j, dst, scale in ((2, QT, 0.125), (3, KT_, 1.0)):
                        count = left * 5 // 8 if j == 2 else left // 2
                        self.sum_side(ve, count)
                        left -= count
                        self.leave(ve, j)
                        for e in range(2):
                            nc.vector.tensor_scalar(dst[:, 2 * e:2 * e + 2, :].rearrange("p t n -> p (t n)"),
                                                    self.bank(j, e), scale, None, ALU.mult).then_inc(self.freed(S, j), 1)
                    self.sum_side(ve, left)

                @block.gpsimd
                def _(pool):
                    self.norm_gpsimd(pool, S)

            with ExitStack() as inner, self.stage("scores sp keep summed expo att pv wT wT_out v_ms v_rstd v_hat gated gated_out gate_sum gate_out ada_sum",
                            side=0 if l == 0 else None) as (block, S):
                wT = self.sb("gm_wT", [P, HEADS, P], ctx=inner)
                sq = self.sb("v_squares", [P, NB, HALF], ctx=inner)
                vms = self.sb("v_ms", [P, NB * HEADS], ctx=inner)
                vrs = self.sb("v_rstd", [P, NB * HEADS], ctx=inner)
                W3 = 3 * P
                AHEAD = 4
                z_banks = (0, 1, 6, 7)
                ab = self.sb("stick_abs", [P, AHEAD, W3], ctx=inner)
                sp = self.sb("stick_softplus", [P, AHEAD, W3], ctx=inner)
                keep = self.sb("stick_keep", [P, AHEAD, W3], ctx=inner)
                lg = self.sb("stick_log", [P, 2, W3], ctx=inner)
                at = self.sb("stick_att", [P, 2, W3], ctx=inner)
                v3 = lambda t: t.rearrange("p b (h c) -> p (b h) c", h=HEADS)

                @block.tensor
                def _(pe):
                    def scores(h):
                        r, t, Z = 64 * (h % 2), h // 2, self.PS[:, z_banks[h % AHEAD], :]
                        if h >= AHEAD:
                            pe.wait_ge(S.expo, h - AHEAD + 1)
                        nc.tensor.matmul(Z[:, 0:SEQ], KT_[r:r + 64, t, 0:P], QT[r:r + 64, t, :], start=True, stop=False,
                                         skip_group_check=True)
                        nc.tensor.matmul(Z[:, SEQ:W3], KT_[r:r + 64, t, P:SEQ], QT[r:r + 64, t, P:SEQ], start=False,
                                         stop=False, skip_group_check=True).then_inc(S.scores, 1)

                    def sums(h):
                        Z, lk = self.PS[:, z_banks[h % AHEAD], :], keep[:, h % AHEAD, :]
                        pe.wait_ge(S.keep, h + 1)
                        nc.tensor.matmul(Z[:, 0:SEQ], self.from_, lk[:, 0:SEQ], start=False, stop=True, skip_group_check=True)
                        nc.tensor.matmul(Z[:, P:SEQ], self.ones, lk[:, SEQ:W3], start=False, stop=True, skip_group_check=True)
                        nc.tensor.matmul(Z[:, SEQ:W3], self.from_, lk[:, SEQ:W3], start=False, stop=True,
                                         skip_group_check=True).then_inc(S.summed, 1)

                    def values(h):
                        c = slice(64 * h, 64 * h + 64)
                        pe.wait_ge(S.att, h + 1)
                        A = at[:, h % 2, :]
                        nc.tensor.matmul(self.PS[:, 2, c], A[:, 0:P], SV[:, 0, c], start=True, stop=True)
                        nc.tensor.matmul(self.PS[:, 3, c], A[:, P:SEQ], SV[:, 0, c], start=True, stop=False)
                        nc.tensor.matmul(self.PS[:, 3, c], A[:, SEQ:W3], SV[:, 1, c], start=False, stop=True).then_inc(S.pv, 1)

                    for h in range(AHEAD - 1):
                        scores(h)
                    pe.wait_ge(side, 64)
                    for h in range(HEADS):
                        ins = nc.tensor.transpose(self.PS[:, 4 + h // 4, (h % 4) * P:(h % 4 + 1) * P], ws[:, h, :], self.ident)
                    ins.then_inc(S.wT, 1)
                    for h in range(HEADS):
                        if h + AHEAD - 1 < HEADS:
                            scores(h + AHEAD - 1)
                        sums(h)
                        if h >= 1:
                            values(h - 1)
                        if h == 3:
                            pe.wait_ge(S.wT_out, 1)
                            pe.wait_ge(S.v_hat, 1)
                            for b in range(NB):
                                for g in range(HEADS):
                                    c = slice(64 * g, 64 * g + 64)
                                    ins = nc.tensor.matmul(self.PS[:, 4 + b, c], wT[:, g, :], V[:, b, c], start=True, stop=True)
                            ins.then_inc(S.gated, 1)
                        if h == 5:
                            pe.wait_ge(S.gated_out, 1)
                            self.sum_spread(4, 2).then_inc(S.gate_sum, 1)
                        if h == 7:
                            pe.wait_ge(S.expo, 5)
                            for i, v in enumerate((3, 4)):
                                self.sum_columns(self.PS[:, 0, i * KT:(i + 1) * KT], v)
                            pe.wait_ge(S.gate_out, 1)
                            self.sum_spread(4, 5).then_inc(S.ada_sum, 1)
                    values(HEADS - 1)

                @block.scalar
                def _(act):
                    def log_keep(h):
                        i = h % AHEAD
                        act.wait_ge(S.scores, h + 1)
                        nc.scalar.activation(ab[:, i, :], self.PS[:, z_banks[i], 0:W3], ACT.Abs)
                        nc.scalar.drain()
                        nc.scalar.activation(sp[:, i, :], ab[:, i, :], ACT.Exp, scale=-1.0)
                        nc.scalar.drain()
                        nc.scalar.activation(sp[:, i, :], sp[:, i, :], ACT.Ln, bias=1.0).then_inc(S.sp, 1)

                    def weights(h):
                        act.wait_ge(S.expo, h + 1)
                        if h >= 2:
                            act.wait_ge(S.pv, h - 1)
                        nc.scalar.activation(at[:, h % 2, :], lg[:, h % 2, :], ACT.Exp).then_inc(S.att, 1)

                    nc.scalar.preload_act_table_set("natural_log_exp_and_others")
                    log_keep(0)
                    log_keep(1)
                    for h in range(HEADS):
                        if h + 2 < HEADS:
                            log_keep(h + 2)
                        weights(h)

                @block.vector
                def _(ve):
                    def keeps(h):
                        i = h % AHEAD
                        ve.wait_ge(S.sp, h + 1)
                        nc.vector.scalar_tensor_tensor(sp[:, i, :], self.PS[:, z_banks[i], 0:W3], 0.0, sp[:, i, :], ALU.max, ALU.add)
                        nc.vector.drain()
                        nc.vector.scalar_tensor_tensor(keep[:, i, :], sp[:, i, :], -1.0, self.strict3, ALU.mult,
                                                       ALU.mult).then_inc(S.keep, 1)

                    def exponents(h):
                        ve.wait_ge(S.summed, h + 1)
                        if h >= 2:
                            ve.wait_ge(S.att, h - 1)
                        nc.vector.tensor_tensor(lg[:, h % 2, :], self.PS[:, z_banks[h % AHEAD], 0:W3], self.strict3_add,
                                                ALU.add).then_inc(S.expo, 1)

                    def gate_inputs():
                        nc.vector.tensor_tensor(sq[:], V[:], V[:], ALU.mult)
                        nc.vector.drain()
                        nc.vector.tensor_reduce(vms[:], v3(sq[:]), AX.X, ALU.add)
                        nc.vector.drain()
                        nc.vector.tensor_scalar(vms[:], vms[:], 1.0 / 64, EPS, ALU.mult, ALU.add).then_inc(S.v_ms, 1)
                        ve.wait_ge(S.wT, 1)
                        nc.vector.tensor_copy(wT[:].rearrange("p (g h) n -> p g (h n)", g=2), self.PS[:, 4:6, :])
                        nc.vector.drain()
                        nc.vector.memset(wT[64:128, :, 0:64], 0.0).then_inc(S.wT_out, 1)

                    def gate_scale():
                        ve.wait_ge(S.v_rstd, 1)
                        nc.vector.tensor_tensor(v3(V[:]), v3(V[:]), vrs[:].unsqueeze(2).to_broadcast([P, NB * HEADS, 64]), ALU.mult)
                        nc.vector.drain()
                        nc.vector.tensor_tensor(V[:], V[:], vgain[:].unsqueeze(1).to_broadcast([P, NB, HALF]),
                                                ALU.mult).then_inc(S.v_hat, 1)

                    def gate_outputs():
                        ve.wait_ge(S.gated, 1)
                        bias = self.col("gm_bs")[:, HEADS * l:HEADS * (l + 1)].unsqueeze(2).to_broadcast([P, HEADS, 64])
                        for b in range(NB):
                            nc.vector.tensor_tensor(sq[:, b, :].rearrange("p (h c) -> p h c", h=HEADS),
                                                    self.PS[:, 4 + b, :].rearrange("p (h c) -> p h c", h=HEADS), bias, ALU.add)
                        nc.vector.drain().then_inc(S.gated_out, 1)
                        nc.vector.tensor_tensor(Y[:, :, 0:HALF], sq[:], U[:], ALU.mult)

                    def residual_gate(i):
                        g = self.gate[:, i, :].rearrange("p (h n) -> p h n", n=BANK)
                        return nc.vector.tensor_tensor(g, self.PS[:, 4:6, :], g, ALU.add)

                    keeps(0)
                    keeps(1)
                    gate_inputs()
                    for h in range(HEADS):
                        if h == 1:
                            ve.wait_ge(side, 64)
                            gate_scale()
                        if h + 2 < HEADS:
                            keeps(h + 2)
                        exponents(h)
                        if h == 4:
                            gate_outputs()
                        if h == 6:
                            ve.wait_ge(S.gate_sum, 1)
                            residual_gate(0).then_inc(S.gate_out, 1)
                    ve.wait_ge(S.ada_sum, 1)
                    residual_gate(1)
                    nc.vector.tensor_tensor(self.mod[:, 3 * KT:5 * KT], self.PS[:, 0, 0:2 * KT], bias[:, 3 * KT:5 * KT], ALU.add)
                    nc.vector.drain()
                    nc.vector.scalar_tensor_tensor(self.modA[:, 1, :], self.mod[:, 4 * KT:5 * KT], 1.0,
                                                   self.col("norm_ffn")[:, KT * l:KT * (l + 1)], ALU.add, ALU.mult)
                    ve.wait_ge(S.pv, HEADS)
                    nc.vector.tensor_copy(Y[:, :, HALF:D], self.PS[:, 2:4, :])

                @block.gpsimd
                def _(pool):
                    pool.wait_ge(S.v_ms, 1)
                    nc.gpsimd.tensor_tensor(vrs[:], vms[:], self.neghalf[:, 0:NB * HEADS], ALU.pow).then_inc(S.v_rstd, 1)

            with self.stage("n_ms n_rstd n_xn n_tr n_hT p_free0 p_free1 summed columns", f"mix_out{l}",
                            side=group if l == 0 else None) as (block, S):
                ms4 = self.sb("group_ms", [P, 4], ctx=ctx)
                rs4 = self.sb("group_rstd", [P, 4], ctx=ctx)
                halves = Y[:].rearrange("p b (g n) -> p (b g) n", g=2)
                gains = self.sb("group_gains", [P, KT], ctx=ctx)

                @block.tensor
                def _(pe):
                    self.norm_tensor(pe, S, src=Y)
                    pe.wait_ge(S.n_hT, self.N_HT)
                    self.project(pe, S, [("T", 512)] * 2, self.hT, KT)
                    if l == 0:
                        pe.wait_ge(S.summed, 1)
                        self.sum_columns(self.PS[:, 4, 0:KT], 0)
                        self.sum_columns(self.PS[:, 4, KT:2 * KT], 1).then_inc(S.columns, 1)

                @block.scalar
                def _(act):
                    act.wait_ge(S.n_xn, 1)
                    self.norm_scalar(act, S, gains[:], None)
                    if l == 0:
                        act.wait_ge(S.columns, 1)
                        nc.scalar.copy(self.first_mod[:], self.PS[:, 4, 0:2 * KT])

                @block.vector
                def _(ve):
                    for i, name in enumerate(("out_norm_a", "out_norm_b")):
                        nc.vector.tensor_copy(gains[:, 4 * i:4 * i + 4], self.col(name)[:, 4 * l:4 * l + 4])
                    for i in range(4):
                        nc.vector.tensor_tensor_reduce(self.xn[:, i // 2, (i % 2) * HALF:(i % 2 + 1) * HALF], halves[:, i, :], halves[:, i, :], 1.0 / HALF, EPS,
                                                       ALU.mult, ALU.add, ms4[:, i:i + 1])
                    nc.vector.drain().then_inc(S.n_ms, 1)
                    ve.wait_ge(S.n_rstd, 1)
                    for i in range(4):
                        ins = nc.vector.tensor_scalar(halves[:, i, :], halves[:, i, :], rs4[:, i:i + 1], None, ALU.mult)
                        if i % 2:
                            ins.then_inc(S.n_xn, 1)
                    self.evacuate_tiles(ve, nc.vector, S, 1, gains[:], None)
                    if l == 0:
                        self.sum_side(ve, group)
                        nc.vector.drain().then_inc(S.summed, 1)
                    self.gated_residual(ve, S, 0, ctx)

                @block.gpsimd
                def _(pool):
                    pool.wait_ge(S.n_ms, 1)
                    nc.gpsimd.tensor_tensor(rs4[:], ms4[:], self.neghalf[:, 0:4], ALU.pow).then_inc(S.n_rstd, 1)

    def gated_residual(self, ve, S, which, ctx):
        nc = self.nc
        for j in range(2):
            c = slice(j * BANK, (j + 1) * BANK)
            self.leave(ve, j)
            for b in range(NB):
                nc.vector.tensor_tensor(self.xn[:, b, c], self.bank(j, b), self.gate[:, which, c],
                                        ALU.mult).then_inc(self.freed(S, j), 1)
            nc.vector.drain()
            nc.vector.tensor_tensor(self.X[:, :, c], self.X[:, :, c], self.xn[:, :, c], ALU.add)

    def plain_residual(self, ve, S):
        for j in range(2):
            c = slice(j * BANK, (j + 1) * BANK)
            self.leave(ve, j)
            for b in range(NB):
                self.nc.vector.tensor_tensor(self.X[:, b, c], self.bank(j, b), self.X[:, b, c],
                                             ALU.add).then_inc(self.freed(S, j), 1)

    def peer(self, l):
        nc, a = self.nc, self.a
        with ExitStack() as ctx:
            N2 = 2 * HEADS
            H = self.sb("peer_h", [P, NB, D], ctx=ctx)
            keys = self.sb("peer_keys", [P, 2, P], ctx=ctx)
            keysT = self.sb("peer_keysT", [P, 2, P], ctx=ctx)
            SC = self.sb("peer_scores", [P, NB, 2 * HEADS, P], ctx=ctx)
            E = self.sb("peer_ids", [P, NB, P], I32, ctx=ctx)
            G = self.sb("peer_gates", [P, NB, P], ctx=ctx)
            side = nc.alloc_semaphore(f"peer_side{l}")

            LISTS = 2 * PAIR
            PICKS = PAIR * TOPK
            v16 = self.sb("top_values", [P, LISTS, TOPK], ctx=ctx)
            i16 = self.sb("top_indices", [P, LISTS, TOPK], U32, ctx=ctx)
            i16f = self.sb("top_indices_f", [P, LISTS, TOPK], ctx=ctx)
            cand = self.sb("pair_sums", [P, PAIR, TOPK * TOPK], ctx=ctx)
            pick = self.sb("pair_picks", [P, PAIR, TOPK, TOPK], ctx=ctx)
            ts = self.sb("pair_scores", [P, PAIR, TOPK], ctx=ctx)
            tp = self.sb("pair_positions", [P, PAIR, TOPK], U32, ctx=ctx)
            part = self.sb("pair_part", [P, 2, PAIR, TOPK], U32, ctx=ctx)
            partf = self.sb("pair_part_f", [P, 2, PAIR, TOPK], ctx=ctx)
            found = self.sb("pair_found", [P, 2, PAIR, TOPK], ctx=ctx)
            idf = self.sb("expert_f", [P, PICKS], ctx=ctx)
            sums = self.sb("gate_sums", [P, PAIR], ctx=ctx)
            rsum = self.sb("gate_rsums", [P, PAIR], ctx=ctx)
            shifted = self.sb("gate_shifted", [P, PAIR, TOPK], ctx=ctx)

            def top16(values, indices, src, n):
                for half in range(2):
                    c = slice(8 * half, 8 * half + 8)
                    for i in range(n):
                        nc.vector.max(values[:, i, c], src[:, i, :])
                    nc.vector.drain()
                    for i in range(n):
                        nc.vector.max_index(indices[:, i, c], values[:, i, c], src[:, i, :])
                    nc.vector.drain()
                    if half == 0:
                        for i in range(n):
                            nc.vector.match_replace(src[:, i, :], values[:, i, c], src[:, i, :], TAKEN)
                        nc.vector.drain()

            def lists(b, q):
                top16(v16, i16, SC[:, b, LISTS * q:LISTS * (q + 1)], LISTS)
                nc.vector.tensor_copy(i16f[:], i16[:])
                v = v16[:].rearrange("p (h s) k -> p s h k", s=2)
                full = [P, PAIR, TOPK, TOPK]
                nc.vector.tensor_tensor(cand[:].rearrange("p h (x y) -> p h x y", x=TOPK),
                                        v[:, 0].unsqueeze(3).to_broadcast(full), v[:, 1].unsqueeze(2).to_broadcast(full), ALU.add)
                nc.vector.drain()

            def pairs(ve, S, b, q, count):
                full = [P, PAIR, TOPK, TOPK]
                top16(ts, tp, cand, PAIR)
                if count > 1:
                    ve.wait_ge(S.expd, count - 1)
                nc.vector.tensor_tensor(shifted[:], ts[:], ts[:, :, 0:1].to_broadcast([P, PAIR, TOPK]),
                                        ALU.subtract).then_inc(S.shifted, 1)
                nc.vector.tensor_scalar(part[:, 0], tp[:], 4, None, ALU.logical_shift_right)
                nc.vector.tensor_scalar(part[:, 1], tp[:], 15, None, ALU.bitwise_and)
                nc.vector.drain()
                nc.vector.tensor_copy(partf[:], part[:])
                nc.vector.drain()
                idx = i16f[:].rearrange("p (h s) k -> p s h k", s=2)
                for s in range(2):
                    nc.vector.tensor_tensor(pick[:], partf[:, s].unsqueeze(3).to_broadcast(full),
                                            self.iota16.unsqueeze(1).unsqueeze(1).to_broadcast(full), ALU.is_equal)
                    nc.vector.drain()
                    nc.vector.tensor_tensor(pick[:], pick[:], idx[:, s].unsqueeze(2).to_broadcast(full), ALU.mult)
                    nc.vector.drain()
                    nc.vector.tensor_reduce(found[:, s], pick[:], AX.X, ALU.add)
                    nc.vector.drain()
                nc.vector.scalar_tensor_tensor(idf[:], found[:, 0].rearrange("p h k -> p (h k)"), float(P),
                                               found[:, 1].rearrange("p h k -> p (h k)"), ALU.mult, ALU.add)
                nc.vector.drain()
                c = slice(PICKS * q, PICKS * (q + 1))
                nc.vector.tensor_scalar(E[:, b, c], idf[:], float(l * P * P), None, ALU.add).then_inc(S.ids, 1)

            def gates(ve, S, b, q, count):
                c = slice(PICKS * q, PICKS * (q + 1))
                ve.wait_ge(S.expd, count)
                g = G[:, b, c].rearrange("p (h k) -> p h k", h=PAIR)
                nc.vector.tensor_reduce(sums[:], g, AX.X, ALU.add)
                nc.vector.drain()
                nc.vector.reciprocal(rsum[:], sums[:])
                nc.vector.drain()
                nc.vector.tensor_tensor(g, g, rsum[:].unsqueeze(2).to_broadcast([P, PAIR, TOPK]), ALU.mult)
                nc.vector.drain()

            def exponentials(act, S, b, q, count):
                act.wait_ge(S.shifted, count)
                nc.scalar.activation(G[:, b, PICKS * q:PICKS * (q + 1)], shifted[:].rearrange("p h k -> p (h k)"),
                                     ACT.Exp).then_inc(S.expd, 1)

            with self.stage(
                    "n_ms n_rstd n_xn n_tr n_hT p_free0 p_free1 back back_out keysT keysT_out scores score_out "
                    "queries shifted expd ids dots gelu weights diag", f"peer_q{l}") as (block, S):
                QT = self.sb("peer_qT", [P, 2, LISTS, SEQ], ctx=ctx)
                rows = self.sb("expert_rows", [P, GRING, D], ctx=ctx)
                turn = self.sb("gather_index", [P, 2, GHALF], I32, ctx=ctx)
                part16 = self.sb("dots16", [P, GRING], ctx=ctx)
                dots = self.sb("dots", [P, P], ctx=ctx)
                wts = self.sb("expert_weights", [P, P], ctx=ctx)
                diag = self.sb("weight_diag", [P, 2 * PE_ROWS, P], ctx=ctx)
                acc = self.xn[:, 0, :]
                shift = self.mod[:, 3 * KT:4 * KT]
                parts = HEADS // PAIR
                rounds = PICKS // GRING
                work = [(b, q) for b in range(NB) for q in range(parts)]

                def landed(phase, i):
                    return i * 16 + 16 * ((l * 2 * len(work) + phase) * rounds + 1)

                def pe_used(p):
                    return (l * len(work) + p) * 2 * PE_ROWS * rounds + PE_CREDIT

                def ve_used(phase):
                    done = l * 2 * len(work) + phase
                    return (-(-done // 2) * GHALF + done // 2 * VE_ROWS) * 2 * rounds + VE_CREDIT

                @block.tensor
                def _(pe):
                    def scores(j):
                        pe.wait_ge(S.queries, j + 1)
                        if j == 0:
                            pe.wait_ge(S.keysT_out, 1)
                        if j >= 2:
                            pe.wait_ge(S.score_out, 2 * (j - 1))
                        for b in range(NB):
                            for i in range(LISTS):
                                ins = nc.tensor.matmul(self.PS[:, 4 + 2 * (j % 2) + b, i * P:(i + 1) * P],
                                                       QT[:, j % 2, i, b * P:(b + 1) * P], keysT[:, i % 2, :],
                                                       start=True, stop=True)
                            ins.then_inc(S.scores, 1)

                    self.norm_tensor(pe, S)
                    pe.wait_ge(side, 32)
                    for i in range(2):
                        ins = nc.tensor.transpose(self.PS[:, 3, i * P:(i + 1) * P], keys[:, i, :], self.ident)
                    ins.then_inc(S.keysT, 1)
                    pe.wait_ge(S.n_hT, self.N_HT)
                    for j in range(parts):
                        self.project(pe, S, [("F", 512)], self.hT, KT, first=j)
                        if j == 1:
                            pe.wait_ge(S.back_out, 1)
                        scores(j)
                        if j == 0:
                            pe.wait_ge(S.score_out, 2)
                            for b in range(NB):
                                for g in range(2):
                                    for i in range(4):
                                        k = 4 * g + i
                                        ins = nc.tensor.transpose(self.PS[:, 4 + 2 * b + g, i * P:(i + 1) * P],
                                                                  self.hT[:, k, b * P:(b + 1) * P], self.ident)
                            ins.then_inc(S.back, 1)

                    pe.wait_ge(S.p_free0, 4)
                    pe.wait_ge(S.p_free1, 4)
                    for p, (b, q) in enumerate(work):
                        if q == 0:
                            for h in range(2):
                                nc.tensor.matmul(self.PS[:, 2 * b + h, :], self.onehot[:, SEQ:SEQ + P], self.cst[:, 0:BANK],
                                                 start=True, stop=False, skip_group_check=True)
                        with pe.Fori(0, rounds) as i:
                            for d in range(2 * PE_ROWS):
                                u = d // PE_ROWS * GHALF + VE_ROWS + d % PE_ROWS
                                pe.wait_ge(S.diag, i * (2 * PE_ROWS) + (2 * PE_ROWS * rounds * p + d + 1))
                                pe.wait_ge(self.g_landed[u], landed(2 * p + 1, i))
                                for h in range(2):
                                    ins = nc.tensor.matmul(self.PS[:, 2 * b + h, :], diag[:, d, :], rows[:, u, h * BANK:(h + 1) * BANK],
                                                           start=False, stop=False, skip_group_check=True)
                                ins.then_inc(self.g_used_pe, 1)

                @block.scalar
                def _(act):
                    for i, name in enumerate(("peer_k1", "peer_k2")):
                        act.dma_start(keys[:, i, :], a[name][l]).then_inc(side, 16)
                    self.norm_scalar(act, S, self.modA[:, 1, :], shift)
                    def queries(j):
                        self.leave(act, j)
                        if j >= 2:
                            act.wait_ge(S.scores, 2 * (j - 1))
                        for e in range(2):
                            nc.scalar.copy(QT[:, j % 2, 2 * e:2 * e + 2, :].rearrange("p t n -> p (t n)"),
                                           self.bank(j, e)).then_inc(self.freed(S, j), 1)
                        nc.scalar.drain().then_inc(S.queries, 1)

                    def collect(j):
                        for b in range(NB):
                            act.wait_ge(S.scores, 2 * j + b + 1)
                            nc.scalar.copy(SC[:, b, LISTS * j:LISTS * (j + 1)].rearrange("p i n -> p (i n)"),
                                           self.PS[:, 4 + 2 * (j % 2) + b, :]).then_inc(S.score_out, 1)

                    for j in range(parts):
                        queries(j)
                        collect(j)
                        if j == 0:
                            act.wait_ge(S.back, 1)
                            nc.scalar.copy(H[:].rearrange("p b (g n) -> p (b g) n", n=BANK), self.PS[:, 4:8, :]).then_inc(S.back_out, 1)
                        if j == 1:
                            exponentials(act, S, 0, 0, 1)
                    for p, (b, q) in enumerate(work):
                        c = slice(PICKS * q, PICKS * (q + 1))
                        act.wait_ge(S.dots, p + 1)
                        nc.scalar.activation(wts[:, c], dots[:, c], ACT.Gelu_apprx_tanh).then_inc(S.gelu, 1)
                        act.wait_ge(S.weights, p + 1)
                        with act.Fori(0, rounds) as i:
                            for d in range(2 * PE_ROWS):
                                u = d // PE_ROWS * GHALF + VE_ROWS + d % PE_ROWS
                                act.wait_ge(self.g_used_pe, i * (2 * PE_ROWS) + (pe_used(p) - 2 * PE_ROWS + d + 1))
                                nc.scalar.activation(diag[:, d, :], self.ident, ACT.Copy,
                                                     scale=wts[:, bass.ds(i * GRING + (PICKS * q + u), 1)]).then_inc(S.diag, 1)
                        if p + 1 < len(work):
                            exponentials(act, S, *work[p + 1], p + 2)

                @block.vector
                def _(ve):
                    def products(p):
                        b, q = work[p]
                        with ve.Fori(0, rounds) as i:
                            for u in range(GRING):
                                ve.wait_ge(self.g_landed[u], landed(2 * p, i))
                                nc.vector.tensor_tensor_reduce(rows[:, u, :], rows[:, u, :], H[:, b, :], 1.0, 0.0, ALU.mult,
                                                               ALU.add, part16[:, u:u + 1]).then_inc(self.g_used, 1)
                            nc.vector.drain()
                            nc.vector.tensor_copy(dots[:, bass.ds(i * GRING + PICKS * q, GRING)], part16[:])
                            nc.vector.drain()

                    def combine(p, i):
                        for u in [*range(VE_ROWS), *range(GHALF, GHALF + VE_ROWS)]:
                            e = PICKS * work[p][1] + GRING * i + u
                            ve.wait_ge(self.g_landed[u], landed(2 * p + 1, i))
                            nc.vector.scalar_tensor_tensor(acc, rows[:, u, :], wts[:, e:e + 1], acc, ALU.mult, ALU.add
                                                           ).then_inc(self.g_used, 1)
                            nc.vector.drain()

                    self.norm_vector(ve, S, self.modA[:, 1, :], shift)
                    ve.wait_ge(S.keysT, 1)
                    nc.vector.tensor_copy(keysT[:].rearrange("p i n -> p (i n)"), self.PS[:, 3, 0:2 * P]).then_inc(S.keysT_out, 1)
                    if l == 0:
                        ve.sem_inc(self.g_used, VE_CREDIT)
                        ve.sem_inc(self.g_used_pe, PE_CREDIT)
                    ve.wait_ge(S.score_out, 1)
                    lists(0, 0)
                    pairs(ve, S, 0, 0, 1)
                    ve.wait_ge(S.back_out, 1)
                    for p, (b, q) in enumerate(work):
                        products(p)
                        if q == 0:
                            nc.vector.memset(acc, 0.0)
                        nc.vector.drain().then_inc(S.dots, 1)
                        if p + 1 < len(work):
                            b1, q1 = work[p + 1]
                            ve.wait_ge(S.score_out, 2 * q1 + b1 + 1)
                            lists(b1, q1)
                        gates(ve, S, b, q, p + 1)
                        c = slice(PICKS * q, PICKS * (q + 1))
                        ve.wait_ge(S.gelu, p + 1)
                        nc.vector.tensor_tensor(wts[:, c], wts[:, c], G[:, b, c], ALU.mult)
                        nc.vector.drain().then_inc(S.weights, 1)
                        for i in range(rounds):
                            if i == 1 and p + 1 < len(work):
                                pairs(ve, S, b1, q1, p + 2)
                            combine(p, i)
                        if q + 1 < parts:
                            continue
                        ve.wait_ge(self.g_used_pe, pe_used(p + 1))
                        nc.vector.tensor_tensor(acc.rearrange("p (h n) -> p h n", h=2), acc.rearrange("p (h n) -> p h n", h=2),
                                                self.PS[:, 2 * b:2 * b + 2, :], ALU.add)
                        nc.vector.drain()
                        nc.vector.tensor_tensor(acc, acc, self.gate[:, 1, :], ALU.mult)
                        nc.vector.drain()
                        nc.vector.tensor_tensor(self.X[:, b, :], self.X[:, b, :], acc, ALU.add)
                        nc.vector.drain()

                @block.gpsimd
                def _(pool):
                    def gathers(phase):
                        p, v = phase // 2, phase % 2
                        b, q = work[p]
                        table = a[("peer_u", "peer_v")[v]].rearrange("l n d -> (l n) d")
                        used = (GHALF, VE_ROWS)[v]
                        if l + phase > 0:
                            pool.wait_ge(self.g_used, ve_used(phase) - (VE_ROWS, GHALF)[v])
                        with pool.Fori(0, rounds) as i:
                            for half in range(2):
                                pool.wait_ge(self.g_used, i * (2 * used) + (ve_used(phase) + (half - 1) * used))
                                if v:
                                    pool.wait_ge(self.g_used_pe, i * (2 * PE_ROWS) + (pe_used(p) + (half - 1) * PE_ROWS))
                                else:
                                    pool.wait_ge(self.g_used_pe, pe_used(p) - (1 - half) * PE_ROWS)
                                nc.gpsimd.sem_inc(self.g_turn, 1)
                                nc.gpsimd.tensor_copy(turn[:, half, :], E[:, b, bass.ds(i * GRING + (PICKS * q + half * GHALF), GHALF)]
                                                      ).then_inc(self.g_index, 1)
                                pool.wait_ge(self.g_index, i * 2 + (2 * (l * 2 * len(work) + phase) * rounds + half + 1))
                                nc.gpsimd.sem_inc(self.g_turn, 1)
                                for u in range(half * GHALF, (half + 1) * GHALF):
                                    pool.indirect_dma_start(rows[:, u, :], None, table,
                                                            bass.IndirectOffsetOnAxis(ap=turn[:, half, u % GHALF:u % GHALF + 1], axis=0)
                                                            ).then_inc(self.g_landed[u], 16)

                    self.norm_gpsimd(pool, S)
                    for p in range(len(work)):
                        pool.wait_ge(S.ids, p + 1)
                        gathers(2 * p)
                        gathers(2 * p + 1)

    def pool_conv(self):
        nc, a = self.nc, self.a
        PAD = KERN - 1
        with ExitStack() as ctx:
            u = self.sb("pool_u", [P, 4, 16 + SEQ], ctx=ctx)
            val = self.sb("conv_value", [P, 4, SEQ], ctx=ctx)
            z = self.sb("conv_z", [P, 4, PAD + SEQ], ctx=ctx)
            YT = self.sb("pool_conv_yT", [P, KT, SEQ], ctx=ctx)
            sig = self.sb("conv_sigmoid", [P, 4, SEQ], ctx=ctx)
            pw = self.sb("pool_w", [P, 4, P], ctx=ctx)
            side = nc.alloc_semaphore("pool_w_landed")
            gain = self.col("mix_norm_2")[:, 0:KT]

            with self.stage("n_ms n_rstd n_xn n_tr n_hT p_free0 p_free1 sig", "ab_in") as (block, S):
                @block.tensor
                def _(pe):
                    self.norm_tensor(pe, S)
                    pe.wait_ge(S.n_hT, self.N_HT)
                    self.project(pe, S, [("F", 512)] * 3, self.hT, KT)

                @block.scalar
                def _(act):
                    act.dma_start(pw[:], a["pool_w_2"][0].rearrange("g c d -> c g d")).then_inc(side, 16)
                    self.norm_scalar(act, S, gain, None)
                    self.leave(act, 2)
                    for e in range(2):
                        nc.scalar.activation(sig[:, 2 * e:2 * e + 2, :].rearrange("p t n -> p (t n)"), self.bank(2, e),
                                             ACT.Sigmoid).then_inc(S.sig, 1)

                @block.vector
                def _(ve):
                    nc.vector.memset(u[:, :, 0:16], 0.0)
                    nc.vector.memset(z[:, :, 0:PAD], 0.0)
                    self.norm_vector(ve, S, gain, None)
                    for j, dst in ((0, u[:, :, 16:]), (1, val[:])):
                        self.leave(ve, j)
                        for e in range(2):
                            nc.vector.tensor_copy(dst[:, 2 * e:2 * e + 2, :],
                                                  self.bank(j, e).rearrange("p (t n) -> p t n", t=2)).then_inc(self.freed(S, j), 1)
                    nc.vector.drain()
                    ve.wait_ge(S.sig, 2)
                    nc.vector.tensor_tensor(z[:, :, PAD:], val[:], sig[:], ALU.mult)

                @block.gpsimd
                def _(pool):
                    self.norm_gpsimd(pool, S)

            with self.stage("diag conv_pe pool_in pool_mm pool_out mean_mm centred var_mm c_var c_rstd c_diag c_spread zn conv_out sq") as (block, S):
                W = 16 + SEQ
                s2 = self.sb("sum2", [P, 4, W], ctx=ctx)
                s4 = self.sb("sum4", [P, 4, W], ctx=ctx)
                diff = self.sb("pool_diff", [P, 4, SEQ], ctx=ctx)
                conv = self.sb("conv_out", [P, 4, SEQ], ctx=ctx)
                NDIAG = 8
                diag = self.sb("tap_diag", [P, NDIAG, P], ctx=ctx)
                row = self.sb("chan_rows", [P, SEQ], ctx=ctx)
                sq = sig
                taps = self.col("conv_w_2").rearrange("p (j c) -> p j c", c=4)
                bias = self.col("conv_b_2")

                @block.scalar
                def _(act):
                    n = 0
                    for c in (2, 3):
                        for j in range(KERN):
                            if n >= NDIAG:
                                act.wait_ge(S.conv_pe, n - NDIAG + 1)
                            nc.scalar.activation(diag[:, n % NDIAG, :], self.ident, ACT.Copy, scale=taps[:, j, c:c + 1]).then_inc(S.diag, 1)
                            n += 1
                        act.wait_ge(S.conv_pe, n)
                        nc.scalar.activation(conv[:, c, :], self.PS[:, c - 2, 0:SEQ], ACT.Identity, bias=bias[:, c:c + 1]).then_inc(S.conv_out, 1)
                    g, b = self.col("conv_ln_g_2"), self.col("conv_ln_b_2")
                    act.wait_ge(S.zn, 1)
                    for c in range(4):
                        nc.scalar.activation(YT[:, 4 + c, :], conv[:, c, :], ACT.Silu, bias=b[:, c:c + 1], scale=g[:, c:c + 1])

                @block.tensor
                def _(pe):
                    n = 0
                    for c in (2, 3):
                        for j in range(KERN):
                            pe.wait_ge(S.diag, n + 1)
                            nc.tensor.matmul(self.PS[:, c - 2, 0:SEQ], diag[:, n % NDIAG, :], z[:, c, j:j + SEQ],
                                             start=(j == 0), stop=(j == KERN - 1)).then_inc(S.conv_pe, 1)
                            n += 1
                        if c == 2:
                            pe.wait_ge(side, 16)
                            pe.wait_ge(S.pool_in, 1)
                            for g in range(4):
                                ins = nc.tensor.matmul(self.PS[:, 2 + g // 2, (g % 2) * SEQ:(g % 2 + 1) * SEQ], pw[:, g, :], diff[:, g, :],
                                                       start=True, stop=True)
                            ins.then_inc(S.pool_mm, 1)
                    pe.wait_ge(S.conv_out, 4)
                    for c in range(4):
                        ins = nc.tensor.matmul(self.PS[:, 4, 0:SEQ], self.ones, conv[:, c, :], start=(c == 0), stop=(c == 3))
                    ins.then_inc(S.mean_mm, 1)
                    pe.wait_ge(S.sq, 1)
                    for b in range(NB):
                        for c in range(4):
                            ins = nc.tensor.matmul(self.PS[:, 5, b:b + 1], sq[:, c, b * P:(b + 1) * P], self.ones[:, 0:1],
                                                   start=(c == 0), stop=(c == 3))
                    ins.then_inc(S.var_mm, 1)
                    pe.wait_ge(S.c_diag, 1)
                    for b in range(NB):
                        ins = nc.tensor.matmul(self.PS[:, 6, b * P:(b + 1) * P], self.ones, diag[:, b, :], start=True, stop=True)
                    ins.then_inc(S.c_spread, 1)

                @block.vector
                def _(ve):
                    nc.vector.tensor_tensor(s2[:, :, 1:W], u[:, :, 1:W], u[:, :, 0:W - 1], ALU.add)
                    nc.vector.drain()
                    nc.vector.tensor_tensor(s4[:, 1:4, 4:W], s2[:, 1:4, 4:W], s2[:, 1:4, 2:W - 2], ALU.add)
                    nc.vector.drain()
                    nc.vector.tensor_tensor(s2[:, 2:4, 8:W], s4[:, 2:4, 8:W], s4[:, 2:4, 4:W - 4], ALU.add)
                    nc.vector.drain()
                    nc.vector.tensor_tensor(s4[:, 3, 16:W], s2[:, 3, 16:W], s2[:, 3, 8:W - 8], ALU.add)
                    nc.vector.drain()
                    inv = self.invcount.rearrange("p (g n) -> p g n", g=4)
                    for g, s in enumerate((s2, s4, s2, s4)):
                        nc.vector.tensor_tensor(s[:, g, 16:32], s[:, g, 16:32], inv[:, g, :], ALU.mult)
                        nc.vector.tensor_scalar(s[:, g, 32:W], s[:, g, 32:W], 1.0 / 2 ** (g + 1), None, ALU.mult)
                    nc.vector.drain()
                    for g, s in enumerate((s2, s4, s2, s4)):
                        ins = nc.vector.tensor_tensor(diff[:, g, :], s[:, g, 16:W], u[:, g, 16:W], ALU.subtract)
                    ins.then_inc(S.pool_in, 1)
                    for j in range(KERN):
                        for c in range(2):
                            if j == 0:
                                nc.vector.tensor_scalar(conv[:, c, :], z[:, c, 0:SEQ], taps[:, 0, c:c + 1], bias[:, c:c + 1], ALU.mult, ALU.add)
                            else:
                                nc.vector.scalar_tensor_tensor(conv[:, c, :], z[:, c, j:j + SEQ], taps[:, j, c:c + 1], conv[:, c, :],
                                                               ALU.mult, ALU.add)
                        nc.vector.drain()
                    nc.vector.drain().then_inc(S.conv_out, 2)
                    ve.wait_ge(S.pool_mm, 1)
                    scale = self.col("pool_scale_2")
                    for g in range(4):
                        nc.vector.tensor_scalar(YT[:, g, :], self.PS[:, 2 + g // 2, (g % 2) * SEQ:(g % 2 + 1) * SEQ],
                                                scale[:, g:g + 1], None, ALU.mult)
                    ve.wait_ge(S.mean_mm, 1)
                    nc.vector.tensor_scalar(row[:], self.PS[:, 4, 0:SEQ], 1.0 / HALF, None, ALU.mult)
                    nc.vector.drain()
                    nc.vector.tensor_tensor(conv[:], conv[:], row[:].unsqueeze(1).to_broadcast([P, 4, SEQ]), ALU.subtract)
                    nc.vector.drain()
                    nc.vector.tensor_tensor(sq[:], conv[:], conv[:], ALU.mult).then_inc(S.sq, 1)
                    ve.wait_ge(S.var_mm, 1)
                    nc.vector.tensor_scalar(self.ms[:], self.PS[:, 5, 0:NB], 1.0 / HALF, EPS, ALU.mult, ALU.add).then_inc(S.c_var, 1)
                    ve.wait_ge(S.c_rstd, 1)
                    for b in range(NB):
                        ins = nc.vector.tensor_scalar(diag[:, b, :], self.ident, self.rstd[:, b:b + 1], None, ALU.mult)
                    ins.then_inc(S.c_diag, 1)
                    ve.wait_ge(S.c_spread, 1)
                    nc.vector.tensor_tensor(conv[:], conv[:], self.PS[:, 6, 0:SEQ].unsqueeze(1).to_broadcast([P, 4, SEQ]), ALU.mult).then_inc(S.zn, 1)

                @block.gpsimd
                def _(pool):
                    pool.wait_ge(S.c_var, 1)
                    nc.gpsimd.tensor_tensor(self.rstd[:], self.ms[:], self.neghalf[:, 0:NB], ALU.pow).then_inc(S.c_rstd, 1)

            self.output_projection("ab_out", YT)

    def output_projection(self, name, YT):
        with self.stage("p_free0 p_free1", name) as (block, S):
            @block.tensor
            def _(pe):
                self.project(pe, S, [("T", 512)] * 2, YT, KT)

            @block.vector
            def _(ve):
                self.plain_residual(ve, S)

    def attention(self, block, S, ctx, heads, dh, QT, KT_, V, mask, bias, YT):
        nc = self.nc
        W3 = 3 * P
        AHEAD = 4
        logit_banks = (0, 1, 6, 7)
        lg = self.sb("att_logits", [P, AHEAD, W3], ctx=ctx)
        nmax = self.sb("att_negmax", [P, AHEAD, NB], ctx=ctx)
        sums = self.sb("att_sums", [P, AHEAD, NB], ctx=ctx)
        rsum = self.sb("att_rsums", [P, AHEAD, NB], ctx=ctx)
        pT = self.sb("att_probsT", [P, 2, W3], ctx=ctx)
        per = P // dh

        def rows(h):
            return slice(dh * (h % per), dh * (h % per) + dh)

        @block.tensor
        def _(pe):
            def scores(h):
                L, r, t = self.PS[:, logit_banks[h % AHEAD], :], rows(h), h // per
                if h >= AHEAD:
                    pe.wait_ge(S.a_masked, h - AHEAD + 1)
                nc.tensor.matmul(L[:, 0:P], QT[r, t, 0:P], KT_[r, t, 0:P], start=True, stop=(bias is None), skip_group_check=True)
                ins = nc.tensor.matmul(L[:, P:W3], QT[r, t, P:SEQ], KT_[r, t, :], start=False, stop=(bias is None), skip_group_check=True)
                if bias is not None:
                    nc.tensor.matmul(L[:, 0:P], self.anti, bias[:, h, P:SEQ], start=False, stop=True, skip_group_check=True)
                    ins = nc.tensor.matmul(L[:, P:W3], self.anti, bias[:, h, :], start=False, stop=True, skip_group_check=True)
                ins.then_inc(S.a_scores, 1)

            def turn(h):
                pe.wait_ge(S.a_norm, h + 1)
                if h >= 2:
                    pe.wait_ge(S.a_turned, h - 1)
                T, p = self.PS[:, 2 + h % 2, :], lg[:, h % AHEAD, :]
                nc.tensor.transpose(T[:, 0:P], p[:, 0:P], self.ident)
                nc.tensor.transpose(T[:, P:SEQ], p[:, P:SEQ], self.ident)
                nc.tensor.transpose(T[:, SEQ:W3], p[:, SEQ:W3], self.ident).then_inc(S.a_turn, 1)

            def values(h):
                pe.wait_ge(S.a_turned, h + 1)
                if h >= 2:
                    pe.wait_ge(S.a_out, h - 1)
                O, c = self.PS[rows(h), 4 + h % 2, 0:SEQ], slice(dh * h, dh * h + dh)
                nc.tensor.matmul(O, V[:, 0, c], pT[:, h % 2, 0:SEQ], start=True, stop=False, skip_group_check=True)
                nc.tensor.matmul(O[:, P:SEQ], V[:, 1, c], pT[:, h % 2, SEQ:W3], start=False, stop=True,
                                 skip_group_check=True).then_inc(S.a_val, 1)

            for h in range(AHEAD - 1):
                scores(h)
            for h in range(heads):
                if h + AHEAD - 1 < heads:
                    scores(h + AHEAD - 1)
                turn(h)
                if h >= 1:
                    values(h - 1)
            values(heads - 1)

        @block.vector
        def _(ve):
            def masked(h):
                i = h % AHEAD
                ve.wait_ge(S.a_scores, h + 1)
                if h >= AHEAD:
                    ve.wait_ge(S.a_turn, h - AHEAD + 1)
                nc.vector.tensor_tensor(lg[:, i, :], self.PS[:, logit_banks[i], 0:W3], mask, ALU.add).then_inc(S.a_masked, 1)
                nc.vector.drain()
                nc.vector.tensor_reduce(nmax[:, i, 0:1], lg[:, i, 0:P], AX.X, ALU.max, negate=True)
                nc.vector.tensor_reduce(nmax[:, i, 1:2], lg[:, i, P:W3], AX.X, ALU.max, negate=True)
                nc.vector.drain().then_inc(S.a_max, 1)

            def normalised(h):
                i = h % AHEAD
                ve.wait_ge(S.a_exp, h + 1)
                nc.vector.reciprocal(rsum[:, i, :], sums[:, i, :])
                nc.vector.drain()
                nc.vector.tensor_scalar(lg[:, i, 0:P], lg[:, i, 0:P], rsum[:, i, 0:1], None, ALU.mult)
                nc.vector.tensor_scalar(lg[:, i, P:W3], lg[:, i, P:W3], rsum[:, i, 1:2], None, ALU.mult)
                nc.vector.drain().then_inc(S.a_norm, 1)

            masked(0)
            masked(1)
            for h in range(heads):
                if h + 2 < heads:
                    masked(h + 2)
                normalised(h)
                if h >= 2:
                    self.attention_out(ve, S, nc.vector.tensor_copy, h - 2, rows, per, YT)
            for h in (heads - 2, heads - 1):
                self.attention_out(ve, S, nc.vector.tensor_copy, h, rows, per, YT)

        @block.scalar
        def _(act):
            def exponentials(h):
                i = h % AHEAD
                act.wait_ge(S.a_max, h + 1)
                nc.scalar.activation(lg[:, i, 0:P], lg[:, i, 0:P], ACT.Exp, bias=nmax[:, i, 0:1], accum_out=sums[:, i, 0:1])
                nc.scalar.activation(lg[:, i, P:W3], lg[:, i, P:W3], ACT.Exp, bias=nmax[:, i, 1:2], accum_out=sums[:, i, 1:2])
                nc.scalar.drain().then_inc(S.a_exp, 1)

            def turned(h):
                act.wait_ge(S.a_turn, h + 1)
                if h >= 2:
                    act.wait_ge(S.a_val, h - 1)
                nc.scalar.copy(pT[:, h % 2, :], self.PS[:, 2 + h % 2, 0:W3]).then_inc(S.a_turned, 1)

            exponentials(0)
            for h in range(heads):
                if h + 1 < heads:
                    exponentials(h + 1)
                turned(h)

    ATT = "a_scores a_masked a_max a_exp a_norm a_turn a_turned a_val a_out"

    def attention_out(self, eng, S, copy, h, rows, per, YT):
        eng.wait_ge(S.a_val, h + 1)
        copy(YT[rows(h), h // per, :], self.PS[rows(h), 4 + h % 2, 0:SEQ]).then_inc(S.a_out, 1)

    def sparse_attention(self):
        nc, a = self.nc, self.a
        W3 = 3 * P
        AH = 16
        with ExitStack() as ctx:
            QT = self.sb("dsa_qT", [P, KT, SEQ], ctx=ctx)
            KT_ = self.sb("dsa_kT", [P, KT, SEQ], ctx=ctx)
            V = self.sb("dsa_v", [P, NB, D], ctx=ctx)
            QI = self.sb("dsa_qiT", [P, 4, SEQ], ctx=ctx)
            KI = self.sb("dsa_kiT", [P, SEQ], ctx=ctx)
            WI = self.sb("dsa_wi", [P, NB, 8], ctx=ctx)
            mask = self.sb("dsa_mask", [P, W3], ctx=ctx)
            B = self.sb("dsa_bias", [P, AH, SEQ], ctx=ctx)
            rb = self.sb("rel_bias", [32, AH], ctx=ctx)
            rbT = self.sb("rel_bias_by_distance", [AH, 384], ctx=ctx)
            scratch = nc.dram_tensor("rel_bias_scratch", [AH, 384], F32, kind="Internal").ap()
            side = nc.alloc_semaphore("dsa_side")
            gain = self.col("mix_norm_2")[:, KT:2 * KT]

            with self.stage("n_ms n_rstd n_xn n_tr n_hT p_free0 p_free1 rb rb_out index relu used", "c_in") as (block, S):
                rel = self.sb("dsa_rel", [P, 2, W3], ctx=ctx)
                sc = self.sb("dsa_scores", [P, W3], ctx=ctx)
                top = self.sb("dsa_top", [P, NB, 8], ctx=ctx)

                @block.tensor
                def _(pe):
                    self.norm_tensor(pe, S)
                    pe.wait_ge(S.n_hT, self.N_HT)
                    pe.wait_ge(side, 16)
                    nc.tensor.matmul(self.PS[0:AH, 4, 0:384], rb[:], self.onehot[0:32, :], start=True, stop=True).then_inc(S.rb, 1)
                    self.project(pe, S, [("F", 512)], self.hT, KT)
                    pe.wait_ge(S.rb_out, 1)
                    for g in range(2):
                        slot = self.take(pe)[:, 0:4 * 136].rearrange("p (k n) -> p k n", k=4)
                        for kk in range(4):
                            k = 4 * g + kk
                            st, sp = k == 0, k == KT - 1
                            nc.tensor.matmul(self.PS[:, 5, 0:SEQ], slot[:, kk, 0:P], self.hT[:, k, :], start=st, stop=sp)
                            for b in range(NB):
                                ins = nc.tensor.matmul(self.PS[:, 6 + b, 0:8], self.hT[:, k, b * P:(b + 1) * P],
                                                       slot[:, kk, P:P + 8], start=st, stop=sp)
                        ins.then_inc(self.w_used, 1)
                    self.project(pe, S, [("F", 512)], self.hT, KT, first=2)
                    pe.wait_ge(S.p_free0, 2)
                    pe.wait_ge(S.p_free1, 2)
                    for h in range(8):
                        r, t, L = slice(64 * (h % 2), 64 * (h % 2) + 64), h // 2, self.PS[:, 4 + h % 4, :]
                        if h >= 4:
                            pe.wait_ge(S.relu, h - 3)
                        nc.tensor.matmul(L[:, 0:P], QI[r, t, 0:P], KI[r, 0:P], start=True, stop=True)
                        nc.tensor.matmul(L[:, P:W3], QI[r, t, P:SEQ], KI[r, :], start=True, stop=True).then_inc(S.index, 1)
                    self.project(pe, S, [("F", 512)] * 3 + [("T", 512)] * 2, self.hT, KT, first=3)

                @block.scalar
                def _(act):
                    act.dma_start(rb[:], a["rel_bias_2"]).then_inc(side, 16)
                    self.norm_scalar(act, S, gain, None)
                    act.wait_ge(S.rb, 1)
                    nc.scalar.copy(rbT[:], self.PS[0:AH, 4, 0:384]).then_inc(S.rb_out, 1)
                    act.wait_ge(S.rb_out, 1)
                    act.dma_start(scratch, rbT[:]).then_inc(side, 16)
                    act.wait_ge(side, 32)
                    act.dma_start(B[:], bass.AP(scratch.tensor, 0, [[1, P], [384, AH], [1, SEQ]])).then_inc(side, 16)
                    for h in range(8):
                        act.wait_ge(S.index, h + 1)
                        if h >= 2:
                            act.wait_ge(S.used, h - 1)
                        nc.scalar.activation(rel[:, h % 2, :], self.PS[:, 4 + h % 4, 0:W3], ACT.Relu).then_inc(S.relu, 1)
                    for j in (3, 5, 7):
                        dst = {3: QT[:, 4:8], 5: KT_[:, 4:8], 7: V[:, :, BANK:]}[j]
                        self.leave(act, j)
                        for e in range(2):
                            if j == 7:
                                ins = nc.scalar.copy(dst[:, e, :], self.bank(j, e))
                            else:
                                ins = nc.scalar.mul(dst[:, 2 * e:2 * e + 2, :].rearrange("p t n -> p (t n)"), self.bank(j, e),
                                                    0.125 if j == 3 else 1.0)
                            ins.then_inc(self.freed(S, j), 1)

                @block.vector
                def _(ve):
                    self.norm_vector(ve, S, gain, None)
                    self.leave(ve, 0)
                    for e in range(2):
                        nc.vector.tensor_copy(QI[:, 2 * e:2 * e + 2, :].rearrange("p t n -> p (t n)"),
                                              self.bank(0, e)).then_inc(S.p_free0, 1)
                    self.leave(ve, 1)
                    nc.vector.tensor_copy(KI[:], self.PS[:, 5, 0:SEQ]).then_inc(S.p_free1, 1)
                    nc.vector.tensor_copy(WI[:], self.PS[:, 6:8, 0:8]).then_inc(S.p_free1, 1)
                    nc.vector.drain()

                    def evacuate(j):
                        dst = {2: QT[:, 0:4], 4: KT_[:, 0:4], 6: V[:, :, 0:BANK]}[j]
                        self.leave(ve, j)
                        for e in range(2):
                            if j == 6:
                                ins = nc.vector.tensor_copy(dst[:, e, :], self.bank(j, e))
                            else:
                                ins = nc.vector.tensor_scalar(dst[:, 2 * e:2 * e + 2, :].rearrange("p t n -> p (t n)"), self.bank(j, e),
                                                              0.125 if j == 2 else 1.0, None, ALU.mult)
                            ins.then_inc(self.freed(S, j), 1)

                    parts = ((0, slice(0, P)), (1, slice(P, W3)))

                    def take_largest(rounds):
                        for _ in range(rounds):
                            for b, c in parts:
                                nc.vector.max(top[:, b, :], sc[:, c])
                            nc.vector.drain()
                            for b, c in parts:
                                nc.vector.match_replace(sc[:, c], top[:, b, :], sc[:, c], TAKEN)
                            nc.vector.drain()

                    evacuate(2)
                    for h in range(8):
                        ve.wait_ge(S.relu, h + 1)
                        for b, c in parts:
                            if h == 0:
                                nc.vector.tensor_scalar(sc[:, c], rel[:, 0, c], WI[:, b, 0:1], None, ALU.mult)
                            else:
                                nc.vector.scalar_tensor_tensor(sc[:, c], rel[:, h % 2, c], WI[:, b, h:h + 1], sc[:, c], ALU.mult, ALU.add)
                        nc.vector.drain().then_inc(S.used, 1)
                    nc.vector.scalar_tensor_tensor(sc[:], sc[:], float(512 ** -0.5), self.causal3_add, ALU.mult, ALU.add)
                    nc.vector.drain()
                    take_largest(DSA_TOPK // 16)
                    evacuate(4)
                    take_largest(DSA_TOPK // 16)
                    nc.vector.tensor_scalar(mask[:], sc[:], 0.5 * TAKEN, None, ALU.is_le)
                    nc.vector.drain()
                    nc.vector.tensor_scalar(mask[:], mask[:], 1.0, -NEG, ALU.subtract, ALU.mult)
                    nc.vector.drain()
                    nc.vector.tensor_tensor(mask[:], mask[:], self.causal3_add, ALU.add)
                    evacuate(6)

                @block.gpsimd
                def _(pool):
                    self.norm_gpsimd(pool, S)

            YT = self.sb("dsa_yT", [P, KT, SEQ], ctx=ctx)
            with self.stage(self.ATT) as (block, S):
                @block.tensor
                def _(pe):
                    pe.wait_ge(side, 48)

                self.attention(block, S, ctx, AH, 64, QT, KT_, V, mask[:], B, YT)
            self.output_projection("c_out", YT)

    def turn_plain(self, pe, S, src):
        for b in range(NB):
            for g in range(2):
                for j in range(4):
                    k = 4 * g + j
                    ins = self.nc.tensor.transpose(self.PS[:, 4 + 2 * b + g, j * P:(j + 1) * P],
                                                   src[:, b, k * P:(k + 1) * P], self.ident)
                ins.then_inc(S.n_tr, 1)

    def hybrid(self):
        nc = self.nc
        with ExitStack() as ctx:
            YS = self.sb("ssm_branch", [P, NB, D], ctx=ctx)
            QT = self.sb("moba_qT", [P, KT, SEQ], ctx=ctx)
            with ExitStack() as inner:
                self.mamba(inner, YS, QT)
            with ExitStack() as inner:
                self.moba(inner, YS, QT)

    def mamba(self, ctx, YS, QT):
        nc, a = self.nc, self.a
        XS = self.sb("ssm_x", [P, NB, SSM_D], ctx=ctx)
        with ExitStack() as scan:
            CO = self.sb("ssm_conv", [P, 32, SEQ], ctx=scan)
            DT = self.sb("ssm_dt", [P, NB, SSM_H], ctx=scan)
            DA = self.sb("ssm_da", [P, NB, SSM_H], ctx=scan)
            rows = self.sb("ssm_rows", [P, 3, SSM_H], ctx=scan)
            side = nc.alloc_semaphore("ssm_rows_landed")

            XD = self.sb("ssm_xdt", [P, NB, SSM_D], ctx=scan)
            heads = lambda t: t.rearrange("p (h c) -> p h c", c=SSM_P)
            wide = [P, SSM_H, SSM_P]
            BTK = self.sb("ssm_B_tok", [P, SSM_G, P], ctx=scan)
            with ExitStack() as inner, self.stage(
                    "n_tr n_hT p_free0 p_free1 raw conv silu dt1 dt2 aexp turned turned_out", "ssm_in") as (block, S):
                XB = self.sb("ssm_raw", [P, 2, 4, 3 + SEQ], ctx=inner)
                dta = self.sb("ssm_dt_abs", [P, NB, SSM_H], ctx=inner)
                ea = self.sb("ssm_ea", [P, SSM_H], ctx=inner)
                taps = self.col("conv_w_3").rearrange("p (j c) -> p j c", c=32)
                bias = self.col("conv_b_3")
                TURNS = 6

                @block.tensor
                def _(pe):
                    def turn(i):
                        pe.wait_ge(S.silu, i + 1)
                        if i >= 2:
                            pe.wait_ge(S.turned_out, i - 1)
                        for b in range(NB if i < 4 else 1):
                            for t in range(4):
                                ins = nc.tensor.transpose(self.PS[:, 4 + 2 * (i % 2) + b, t * P:(t + 1) * P],
                                                          CO[:, 4 * i + t, b * P:(b + 1) * P], self.ident)
                        ins.then_inc(S.turned, 1)

                    self.turn_plain(pe, S, self.X)
                    pe.wait_ge(S.n_hT, self.N_HT)
                    self.project(pe, S, [("T", SSM_H)] + [("F", 512)] * 2, self.hT, KT)
                    for i in range(TURNS):
                        self.project(pe, S, [("F", 512)], self.hT, KT, first=i + 3)
                        turn(i)

                @block.scalar
                def _(act):
                    for i, name in enumerate(("dt_bias_3", "a_log_3", "d_skip_3")):
                        act.dma_start(rows[:, i, :], a[name].partition_broadcast(P)).then_inc(side, 16)
                    self.copy_tiles(act, nc.scalar.copy, S, 0)
                    nc.scalar.preload_act_table_set("natural_log_exp_and_others")
                    act.wait_ge(side, 48)
                    nc.scalar.activation(ea[:], rows[:, 1, :], ACT.Exp).then_inc(S.aexp, 1)
                    act.wait_ge(S.dt1, 1)
                    nc.scalar.activation(dta[:], DT[:], ACT.Abs)
                    nc.scalar.drain()
                    nc.scalar.activation(dta[:], dta[:], ACT.Exp, scale=-1.0)
                    nc.scalar.drain()
                    nc.scalar.activation(dta[:], dta[:], ACT.Ln, bias=1.0).then_inc(S.dt2, 1)

                    def silu(i):
                        act.wait_ge(S.conv, i + 1)
                        c = CO[:, 4 * i:4 * i + 4, :]
                        nc.scalar.activation(c, c, ACT.Silu).then_inc(S.silu, 1)

                    def turned(i):
                        act.wait_ge(S.turned, i + 1)
                        if i < 4:
                            nc.scalar.copy(XS[:, :, i * BANK:(i + 1) * BANK], self.PS[:, 4 + 2 * (i % 2):6 + 2 * (i % 2), :]
                                           ).then_inc(S.turned_out, 1)
                        else:
                            nc.scalar.copy(BTK[:, 4 * (i - 4):4 * (i - 3), :].rearrange("p i n -> p (i n)"), self.PS[:, 4 + 2 * (i % 2), :]
                                           ).then_inc(S.turned_out, 1)

                    for i in range(8):
                        self.leave(act, i + 1)
                        if i >= 2:
                            act.wait_ge(S.conv, i - 1)
                        for e in range(2):
                            nc.scalar.copy(XB[:, i % 2, 2 * e:2 * e + 2, 3:], self.bank(i + 1, e).rearrange("p (t n) -> p t n", t=2)
                                           ).then_inc(self.freed(S, i + 1), 1)
                        nc.scalar.drain().then_inc(S.raw, 1)
                        if i >= 1:
                            silu(i - 1)
                        if i >= 3:
                            turned(i - 3)
                    silu(7)
                    turned(5)

                @block.vector
                def _(ve):
                    nc.vector.memset(XB[:, :, :, 0:3], 0.0)
                    self.copy_tiles(ve, nc.vector.tensor_copy, S, 1)
                    nc.vector.drain()
                    self.leave(ve, 0)
                    ve.wait_ge(side, 48)
                    for b in range(NB):
                        nc.vector.tensor_tensor(DT[:, b, :], self.PS[:, b, 0:SSM_H], rows[:, 0, :], ALU.add).then_inc(S.p_free0, 1)
                    nc.vector.drain().then_inc(S.dt1, 1)
                    ve.wait_ge(S.dt2, 1)
                    nc.vector.scalar_tensor_tensor(DT[:], DT[:], 0.0, dta[:], ALU.max, ALU.add)
                    nc.vector.drain()
                    ve.wait_ge(S.aexp, 1)
                    for b in range(NB):
                        nc.vector.scalar_tensor_tensor(DA[:, b, :], DT[:, b, :], -1.0, ea[:], ALU.mult, ALU.mult)

                    def scaled(i):
                        ve.wait_ge(S.turned_out, i + 1)
                        c, h = slice(i * BANK, (i + 1) * BANK), slice(8 * i, 8 * i + 8)
                        for b in range(NB):
                            nc.vector.tensor_tensor(heads(XD[:, b, c]), heads(XS[:, b, c]),
                                                    DT[:, b, h].unsqueeze(2).to_broadcast([P, 8, SSM_P]), ALU.mult)
                        nc.vector.drain()
                        for b in range(NB):
                            nc.vector.tensor_tensor(heads(XS[:, b, c]), heads(XS[:, b, c]),
                                                    rows[:, 2, h].unsqueeze(2).to_broadcast([P, 8, SSM_P]), ALU.mult)

                    for i in range(8):
                        ve.wait_ge(S.raw, i + 1)
                        for tap in range(4):
                            for t in range(4):
                                c = 4 * i + t
                                src = XB[:, i % 2, t, tap:tap + SEQ]
                                if tap == 0:
                                    nc.vector.tensor_scalar(CO[:, c, :], src, taps[:, 0, c:c + 1], bias[:, c:c + 1], ALU.mult, ALU.add)
                                else:
                                    nc.vector.scalar_tensor_tensor(CO[:, c, :], src, taps[:, tap, c:c + 1], CO[:, c, :], ALU.mult, ALU.add)
                            ins = nc.vector.drain()
                        ins.then_inc(S.conv, 1)
                        if 3 <= i < 7:
                            scaled(i - 3)

            with ExitStack() as inner, self.stage(
                    "cums cum_exp decayed states states_out0 states_out cb cbm lhs lhs_act seg segx m y y_out") as (block, S):
                ecum = self.sb("ssm_exp_cum", [P, 2, SSM_H], ctx=inner)
                XDD = self.sb("ssm_xdt_decayed", [P, SSM_D], ctx=inner)
                ST = self.sb("ssm_state", [P, SSM_G, SSM_R * SSM_P], ctx=inner)
                cbm = self.sb("ssm_cb", [P, 2, P], ctx=inner)
                lhs = self.sb("ssm_seg_lhs", [P, 2, SSM_R, P], ctx=inner)
                ex = self.sb("ssm_seg_exp", [P, 2, SSM_R, P], ctx=inner)
                inter = self.sb("ssm_inter", [P, SSM_R * SSM_P], ctx=inner)
                W = SSM_R * SSM_P
                work = [(c, g) for c in range(NB) for g in range(SSM_G)]

                @block.gpsimd
                def _(pool):
                    for n, (c, g) in enumerate(work):
                        if n >= 2:
                            pool.wait_ge(S.seg, n - 1)
                        for r in range(SSM_R // 2):
                            h = SSM_R * g + r
                            ins = nc.gpsimd.tensor_scalar(lhs[:, n % 2, r, :], self.after, DA[:, c, h:h + 1], None, ALU.mult)
                        ins.then_inc(S.lhs, 1)

                @block.tensor
                def _(pe):
                    nc.tensor.matmul(self.PS[:, 6, 0:SSM_H], self.after, DA[:, 0, :], start=True, stop=True)
                    nc.tensor.matmul(self.PS[:, 6, SSM_H:2 * SSM_H], self.upto, DA[:, 1, :], start=True, stop=True).then_inc(S.cums, 1)

                    def first(n):
                        c, g = work[n]
                        t = slice(c * P, (c + 1) * P)
                        if n >= 2:
                            pe.wait_ge(S.cbm, n - 1)
                            pe.wait_ge(S.segx, n - 1)
                        nc.tensor.matmul(self.PS[:, n % 2, 0:P], CO[:, 16 + g, t], CO[:, 24 + g, t], start=True, stop=True).then_inc(S.cb, 1)
                        pe.wait_ge(S.lhs, n + 1)
                        pe.wait_ge(S.lhs_act, n + 1)
                        for r in range(SSM_R):
                            ins = nc.tensor.matmul(self.PS[:, 2 + n % 2, r * P:(r + 1) * P], lhs[:, n % 2, r, :], self.upto,
                                                   start=True, stop=True)
                        ins.then_inc(S.seg, 1)

                    def second(n):
                        c, g = work[n]
                        pe.wait_ge(S.m, n + 1)
                        if n >= 2:
                            pe.wait_ge(S.y_out, n - 1)
                        if n == SSM_G:
                            pe.wait_ge(S.states_out, 1)
                        Yb = self.PS[:, 4 + n % 2, :]
                        for r in range(SSM_R):
                            q = (SSM_R * g + r) * SSM_P
                            ins = nc.tensor.matmul(Yb[:, r * SSM_P:(r + 1) * SSM_P], ex[:, n % 2, r, :], XD[:, c, q:q + SSM_P],
                                                   start=True, stop=True)
                        if c == 1:
                            ins = nc.tensor.matmul(Yb[:, W:2 * W], CO[:, 24 + g, P:SEQ], ST[:, g, :], start=True, stop=True)
                        ins.then_inc(S.y, 1)

                    first(0)
                    for n in range(len(work)):
                        if n + 1 < len(work):
                            first(n + 1)
                        second(n)
                        if n < SSM_G:
                            if n == 0:
                                pe.wait_ge(S.decayed, 1)
                            if n >= 2:
                                pe.wait_ge(S.states_out0, n - 1)
                            nc.tensor.matmul(self.PS[:, 6 + n % 2, 0:W], BTK[:, n, :], XDD[:, n * W:(n + 1) * W], start=True,
                                             stop=True).then_inc(S.states, 1)

                @block.scalar
                def _(act):
                    def operands(n):
                        if n >= 2:
                            act.wait_ge(S.seg, n - 1)
                        c, g = work[n]
                        for r in range(SSM_R // 2, SSM_R):
                            h = SSM_R * g + r
                            ins = nc.scalar.activation(lhs[:, n % 2, r, :], self.after, ACT.Copy, scale=DA[:, c, h:h + 1])
                        ins.then_inc(S.lhs_act, 1)

                    operands(0)
                    operands(1)
                    act.wait_ge(S.cums, 1)
                    nc.scalar.activation(ecum[:].rearrange("p i h -> p (i h)"), self.PS[:, 6, 0:2 * SSM_H], ACT.Exp).then_inc(S.cum_exp, 1)
                    for n in range(len(work)):
                        if 1 <= n < len(work) - 1:
                            operands(n + 1)
                        act.wait_ge(S.seg, n + 1)
                        if n >= 2:
                            act.wait_ge(S.y, n - 1)
                        nc.scalar.activation(ex[:, n % 2].rearrange("p r n -> p (r n)"), self.PS[:, 2 + n % 2, :], ACT.Exp).then_inc(S.segx, 1)
                        if 1 <= n <= SSM_G:
                            act.wait_ge(S.states, n)
                            nc.scalar.copy(ST[:, n - 1, :], self.PS[:, 6 + (n - 1) % 2, 0:W]).then_inc(S.states_out0, 1)
                            if n == SSM_G:
                                nc.scalar.drain().then_inc(S.states_out, 1)

                @block.vector
                def _(ve):
                    ve.wait_ge(S.cum_exp, 1)
                    nc.vector.tensor_tensor(heads(XDD[:]), heads(XD[:, 0, :]), ecum[:, 0, :].unsqueeze(2).to_broadcast(wide), ALU.mult
                                            ).then_inc(S.decayed, 1)

                    def weights(n):
                        ve.wait_ge(S.cb, n + 1)
                        nc.vector.tensor_tensor(cbm[:, n % 2, :], self.PS[:, n % 2, 0:P], self.upto, ALU.mult).then_inc(S.cbm, 1)
                        nc.vector.drain()
                        ve.wait_ge(S.segx, n + 1)
                        nc.vector.tensor_tensor(ex[:, n % 2], ex[:, n % 2], cbm[:, n % 2, :].unsqueeze(1).to_broadcast([P, SSM_R, P]),
                                                ALU.mult).then_inc(S.m, 1)

                    def collect(n):
                        c, g = work[n]
                        ve.wait_ge(S.y, n + 1)
                        out = XS[:, c, g * W:(g + 1) * W]
                        Yb = self.PS[:, 4 + n % 2, :]
                        if c == 1:
                            h4 = ecum[:, 1, SSM_R * g:SSM_R * (g + 1)].unsqueeze(2).to_broadcast([P, SSM_R, SSM_P])
                            nc.vector.tensor_tensor(heads(inter[:]), heads(Yb[:, W:2 * W]), h4, ALU.mult)
                        nc.vector.tensor_tensor(out, out, Yb[:, 0:W], ALU.add).then_inc(S.y_out, 1)
                        if c == 1:
                            nc.vector.drain()
                            nc.vector.tensor_tensor(out, out, inter[:], ALU.add)
                            nc.vector.drain()

                    weights(0)
                    for n in range(len(work)):
                        if n + 1 < len(work):
                            weights(n + 1)
                        collect(n)

        YT = self.sb("ssm_yT", [P, 16, SEQ], ctx=ctx)
        with ExitStack() as inner, self.stage("p_free0 p_free1 z z_used g_ms g_rstd g_y turned0 turned1 out0 out1", "ssm_z") as (block, S):
            Z = self.sb("ssm_silu_z", [P, 2, NB, BANK], ctx=inner)
            gms = self.sb("ssm_group_ms", [P, NB * SSM_G], ctx=inner)
            grs = self.sb("ssm_group_rstd", [P, NB * SSM_G], ctx=inner)
            w = self.col("ssm_norm_w_3")
            groups = XS[:].rearrange("p b (g n) -> p (b g) n", g=SSM_G)

            @block.tensor
            def _(pe):
                self.project(pe, S, [("T", 512)] * 4 + [("F", 512)] * 2, self.hT, KT)
                pe.wait_ge(S.g_y, 1)
                for i in range(8):
                    b, g = i // 4, i % 4
                    for j in range(4):
                        k = 4 * g + j
                        ins = nc.tensor.transpose(self.PS[:, 4 + i % 4, j * P:(j + 1) * P], XS[:, b, k * P:(k + 1) * P], self.ident)
                    ins.then_inc((S.turned0, S.turned1)[i % 2], 1)
                    if i == 3:
                        pe.wait_ge(S.out0, 2)
                        pe.wait_ge(S.out1, 2)

            def turned(eng, ops, odd):
                for i in range(odd, 8, 2):
                    b, g = i // 4, i % 4
                    eng.wait_ge((S.turned0, S.turned1)[odd], i // 2 + 1)
                    for j in range(4):
                        k = 4 * g + j
                        out, src = YT[:, k, b * P:(b + 1) * P], self.PS[:, 4 + i % 4, j * P:(j + 1) * P]
                        if odd:
                            ins = ops.tensor_scalar(out, src, w[:, k:k + 1], None, ALU.mult)
                        else:
                            ins = ops.activation(out, src, ACT.Copy, scale=w[:, k:k + 1])
                    ins.then_inc((S.out0, S.out1)[odd], 1)

            @block.scalar
            def _(act):
                for j in range(4):
                    self.leave(act, j)
                    if j >= 2:
                        act.wait_ge(S.z_used, j - 1)
                    for e in range(2):
                        nc.scalar.activation(Z[:, j % 2, e, :], self.bank(j, e), ACT.Silu).then_inc(self.freed(S, j), 1)
                    nc.scalar.drain().then_inc(S.z, 1)
                for j in (4, 5):
                    self.leave(act, j)
                    for e in range(2):
                        t = 4 * (j - 4) + 2 * e
                        nc.scalar.mul(QT[:, t:t + 2, :].rearrange("p t n -> p (t n)"), self.bank(j, e),
                                      1.0 / math.sqrt(P)).then_inc(self.freed(S, j), 1)
                turned(act, nc.scalar, 0)

            @block.vector
            def _(ve):
                for j in range(4):
                    ve.wait_ge(S.z, j + 1)
                    c = slice(j * BANK, (j + 1) * BANK)
                    nc.vector.tensor_tensor(XS[:, :, c], XS[:, :, c], Z[:, j % 2], ALU.mult).then_inc(S.z_used, 1)
                nc.vector.drain()
                for i in range(NB * SSM_G):
                    nc.vector.tensor_tensor_reduce(self.xn[:].rearrange("p b (g n) -> p (b g) n", n=256)[:, i % 8, :] if i < 8 else
                                                   YT[:, i - 8, :], groups[:, i, :], groups[:, i, :], 1.0 / 256,
                                                   LN_EPS, ALU.mult, ALU.add, gms[:, i:i + 1])
                nc.vector.drain().then_inc(S.g_ms, 1)
                ve.wait_ge(S.g_rstd, 1)
                nc.vector.tensor_tensor(groups, groups, grs[:].unsqueeze(2).to_broadcast([P, NB * SSM_G, 256]), ALU.mult).then_inc(S.g_y, 1)
                turned(ve, nc.vector, 1)

            @block.gpsimd
            def _(pool):
                pool.wait_ge(S.g_ms, 1)
                nc.gpsimd.tensor_tensor(grs[:], gms[:], self.neghalf[:, 0:NB * SSM_G], ALU.pow).then_inc(S.g_rstd, 1)

        with self.stage("p_free0 p_free1", "ssm_out") as (block, S):
            @block.tensor
            def _(pe):
                self.project(pe, S, [("T", 512)] * 2, YT, 16)

            @block.scalar
            def _(act):
                for j in range(2):
                    self.leave(act, j, per=4)
                    for e in range(2):
                        nc.scalar.copy(YS[:, e, j * BANK:(j + 1) * BANK], self.bank(j, e)).then_inc(self.freed(S, j), 1)

    def moba(self, ctx, YS, QT):
        nc, a = self.nc, self.a
        AH = 8
        KT_ = self.sb("moba_kT", [P, KT, SEQ], ctx=ctx)
        V = self.sb("moba_v", [P, NB, D], ctx=ctx)
        YT = self.sb("moba_yT", [P, KT, SEQ], ctx=ctx)
        YA = self.sb("moba_branch", [P, NB, D], ctx=ctx)
        bg = self.sb("b_gate", [P, 2 * D], ctx=ctx)
        lnp = self.sb("ln2_params", [P, 2, D], ctx=ctx)
        side = nc.alloc_semaphore("moba_side")

        with self.stage("p_free0 p_free1", "att_in") as (block, S):
            @block.tensor
            def _(pe):
                self.project(pe, S, [("F", 512)] * 2 + [("T", 512)] * 2, self.hT, KT)

            @block.scalar
            def _(act):
                act.dma_start(bg[:], a["b_gate_3"].partition_broadcast(P)).then_inc(side, 16)
                act.dma_start(lnp[:, 0, :], a["ln2_g_3"].partition_broadcast(P)).then_inc(side, 16)
                act.dma_start(lnp[:, 1, :], a["ln2_b_3"].partition_broadcast(P)).then_inc(side, 16)
                for j in (1, 3):
                    self.leave(act, j)
                    for e in range(2):
                        dst = V[:, e, BANK:] if j == 3 else KT_[:, 4 + 2 * e:6 + 2 * e, :].rearrange("p t n -> p (t n)")
                        nc.scalar.copy(dst, self.bank(j, e)).then_inc(self.freed(S, j), 1)

            @block.vector
            def _(ve):
                for j in (0, 2):
                    self.leave(ve, j)
                    for e in range(2):
                        dst = V[:, e, 0:BANK] if j == 2 else KT_[:, 2 * e:2 * e + 2, :].rearrange("p t n -> p (t n)")
                        nc.vector.tensor_copy(dst, self.bank(j, e)).then_inc(self.freed(S, j), 1)

        with self.stage(self.ATT) as (block, S):
            self.attention(block, S, ctx, AH, P, QT, KT_, V, self.causal3_add, None, YT)

        with self.stage("p_free0 p_free1 pre sig mixed", "att_out") as (block, S):
            pre = self.sb("gate_pre", [P, 2, NB, BANK], ctx=ctx)

            @block.tensor
            def _(pe):
                self.project(pe, S, [("T", 512)] * 2, YT, KT)
                self.project(pe, S, [("T", 512)] * 4, self.hT, KT, first=2)

            @block.scalar
            def _(act):
                for j in range(2):
                    self.leave(act, j)
                    for e in range(2):
                        nc.scalar.copy(YA[:, e, j * BANK:(j + 1) * BANK], self.bank(j, e)).then_inc(self.freed(S, j), 1)
                nc.scalar.drain()
                for i in range(4):
                    act.wait_ge(S.pre, i + 1)
                    nc.scalar.activation(pre[:, i % 2], pre[:, i % 2], ACT.Sigmoid).then_inc(S.sig, 1)

            @block.vector
            def _(ve):
                ve.wait_ge(side, 48)
                for i in range(4):
                    j = i + 2
                    self.leave(ve, j)
                    for e in range(2):
                        nc.vector.tensor_tensor(pre[:, i % 2, e, :], self.bank(j, e), bg[:, i * BANK:(i + 1) * BANK],
                                                ALU.add).then_inc(self.freed(S, j), 1)
                    nc.vector.drain().then_inc(S.pre, 1)
                    ve.wait_ge(S.sig, i + 1)
                    branch = (YS if i < 2 else YA)[:, :, (i % 2) * BANK:(i % 2 + 1) * BANK]
                    nc.vector.tensor_tensor(branch, branch, pre[:, i % 2], ALU.mult)
                    nc.vector.drain()
                nc.vector.tensor_tensor(YA[:], YA[:], YS[:], ALU.add)

        with self.stage("n_tr n_hT p_free0 p_free1 l_ms l_rstd", "mix3_out") as (block, S):
            @block.tensor
            def _(pe):
                self.turn_plain(pe, S, YA)
                pe.wait_ge(S.n_hT, self.N_HT)
                self.project(pe, S, [("T", 512)] * 2, self.hT, KT)

            @block.scalar
            def _(act):
                self.copy_tiles(act, nc.scalar.copy, S, 0)

            @block.vector
            def _(ve):
                for b in range(NB):
                    nc.vector.tensor_scalar(self.X[:, b, :], self.X[:, b, :], ALPHA, None, ALU.mult)
                self.copy_tiles(ve, nc.vector.tensor_copy, S, 1)
                nc.vector.drain()
                self.plain_residual(ve, S)
                nc.vector.drain()
                self.layer_norm_vector(ve, S, lnp)

            @block.gpsimd
            def _(pool):
                self.layer_norm_gpsimd(pool, S)

    def build(self, out):
        a = self.a
        with self.ctx:
            self.place()
            self.plan()
            self.plan_side()
            group = KT * SIDE_GROUP
            for l in range(2):
                with ExitStack() as ada:
                    self.place_side(ada, (4 - 2 * l) * group)
                    if l == 0:
                        self.load_constants()
                        self.ada_start()
                    self.mixer(l)
                self.peer(l)
            self.final_norm(a["final_norm"])
            for l in range(2):
                cols = slice(KT * l, KT * (l + 1))
                self.ffn(f"ffn1_{l}", self.col("ffn1_norm_2")[:, cols])
                if l == 0:
                    self.pool_conv()
                else:
                    self.sparse_attention()
                self.ffn(f"ffn2_{l}", self.col("ffn2_norm_2")[:, cols])
            self.final_norm(a["final_norm_2"])
            self.ffn("ffn1_3", layer_norm=(a["ln1_g_3"], a["ln1_b_3"]))
            self.hybrid()
            self.ffn("ffn2_3", layer_norm=(a["ln3_g_3"], a["ln3_b_3"]))
            self.store(out)


def kernel(**inputs):
    import concourse.bacc as bacc
    from concourse.bass_utils import run_bass_kernel_spmd

    nc = bacc.Bacc("TRN2", target_bir_lowering=False, num_devices=1)
    arrays, args = {}, {}
    inputs = {**inputs, "shape_consts": shape_constants()[0]}
    for name, value in inputs.items():
        value = np.ascontiguousarray(value)
        arrays[f"in_{name}_dram"] = value
        args[name] = nc.dram_tensor(f"in_{name}_dram", value.shape, mybir.dt.from_np(value.dtype), kind="ExternalInput").ap()
    out = nc.dram_tensor("out_dram", (1, SEQ, D), F32, kind="ExternalOutput").ap()
    Program(nc, args).build(out)
    return run_bass_kernel_spmd(nc, [arrays], core_ids=[0]).results[0]["out_dram"]
```
